# Optimizing a Trainium2 kernel written in Bass

```python
import jax, jax.numpy as jnp
from jax import lax
import numpy as np
import math

D_MODEL = 1024
BATCH = 1
SEQ = 256
DEPTH = 2

D_FF = 2816
CHUNK = 128
A_GROUPS = 8
A_GROUP_DIM = 128
A_WIDTH = A_GROUPS * A_GROUP_DIM
B_HEAD_DIM = 64
B_WIDTH = D_MODEL
B_HEADS = B_WIDTH // B_HEAD_DIM
DECAY_LORA = 64
AAA_LORA = 64
MV_LORA = 32
GATE_WIDTH = 2 * D_MODEL
SHIFT_WIDTH_FIRST = 3 * B_WIDTH + DECAY_LORA + AAA_LORA
SHIFT_WIDTH_REST = SHIFT_WIDTH_FIRST + MV_LORA
IN_WIDTH_FIRST = GATE_WIDTH + 2 * A_WIDTH + SHIFT_WIDTH_FIRST
IN_WIDTH_REST = GATE_WIDTH + 2 * A_WIDTH + SHIFT_WIDTH_REST

NORM_EPS = 1e-6
LN_EPS = 1e-5
GN_EPS = 64e-5


def rms_norm(x, g):
    xf = x.astype(jnp.float32)
    xf = xf * lax.rsqrt(jnp.mean(xf * xf, axis=-1, keepdims=True) + NORM_EPS)
    return (xf * g).astype(x.dtype)

def layer_norm(x, g, b):
    xf = x.astype(jnp.float32)
    mu = jnp.mean(xf, axis=-1, keepdims=True)
    var = jnp.mean(jnp.square(xf - mu), axis=-1, keepdims=True)
    return ((xf - mu) * lax.rsqrt(var + LN_EPS) * g + b).astype(x.dtype)

def swiglu_ffn(h, w_gu, w_down):
    gate, up = jnp.split(h @ w_gu, 2, axis=-1)
    return (jax.nn.silu(gate) * up) @ w_down

def token_shift_mix(p, mu):
    prev = jnp.pad(p, ((0, 0), (1, 0), (0, 0)))[:, :-1]
    return p + mu * (prev - p)

def chunked_sgu(u, v, ln_g, ln_b, w_s, b_s):
    u = jax.nn.gelu(u)
    v = layer_norm(jax.nn.gelu(v), ln_g, ln_b)
    bsz, t, _ = v.shape
    vc = v.reshape(bsz, t // CHUNK, CHUNK, A_GROUPS, A_GROUP_DIM)
    causal = jnp.tril(jnp.ones((CHUNK, CHUNK), dtype=bool))
    ws = jnp.where(causal, w_s, 0)
    s = jnp.einsum('gts,bcsgd->bctgd', ws, vc) + b_s.T[:, :, None]
    return u * s.reshape(bsz, t, A_WIDTH)

def rwkv7_time_mix(p, v_first, w0, w2, a0, a2, k_k, k_a, r_k, gn_g, gn_b, v0, v2):
    out_dtype = p.dtype
    p = p.astype(jnp.float32)
    bsz, t, _ = p.shape
    r = p[..., :B_WIDTH]
    k = p[..., B_WIDTH:2 * B_WIDTH]
    v = p[..., 2 * B_WIDTH:3 * B_WIDTH]
    off = 3 * B_WIDTH
    w_down = p[..., off:off + DECAY_LORA]
    off += DECAY_LORA
    a_down = p[..., off:off + AAA_LORA]
    off += AAA_LORA
    log_w = -jax.nn.softplus(-(w0 + jnp.tanh(w_down) @ w2)) - 0.5
    decay = jnp.exp(-jnp.exp(log_w))
    a = jax.nn.sigmoid(a0 + a_down @ a2)
    if v_first is None:
        v_first = v
    else:
        v_res_down = p[..., off:off + MV_LORA]
        v = v + (v_first - v) * jax.nn.sigmoid(v0 + v_res_down @ v2)

    def heads(z):
        return z.reshape(bsz, t, B_HEADS, B_HEAD_DIM)

    kk = heads(k * k_k)
    kk = kk / jnp.maximum(jnp.sqrt(jnp.sum(kk * kk, axis=-1, keepdims=True)), 1e-12)
    k = k * (1 + (a - 1) * k_a)
    r, k, v, decay, a = heads(r), heads(k), heads(v), heads(decay), heads(a)

    def time_major(z):
        return jnp.swapaxes(z, 0, 1)

    def step(state, inp):
        r_t, w_t, k_t, v_t, kk_t, a_t = inp
        sa = jnp.einsum('bhvk,bhk->bhv', state, kk_t)
        state = (state * w_t[:, :, None, :]
                 - sa[..., None] * (kk_t * a_t)[:, :, None, :]
                 + v_t[..., None] * k_t[:, :, None, :])
        return state, jnp.einsum('bhvk,bhk->bhv', state, r_t)

    state0 = jnp.zeros((bsz, B_HEADS, B_HEAD_DIM, B_HEAD_DIM), jnp.float32)
    _, y = lax.scan(step, state0, (time_major(r), time_major(decay), time_major(k),
                                   time_major(v), time_major(kk), time_major(a)))
    y = jnp.swapaxes(y, 0, 1)
    mu = jnp.mean(y, axis=-1, keepdims=True)
    var = jnp.mean(jnp.square(y - mu), axis=-1, keepdims=True)
    y = (y - mu) * lax.rsqrt(var + GN_EPS)
    y = y.reshape(bsz, t, B_WIDTH) * gn_g + gn_b
    bonus = jnp.sum(r * k * r_k, axis=-1, keepdims=True) * v
    y = y + bonus.reshape(bsz, t, B_WIDTH)
    return y.astype(out_dtype), v_first

def first_inputs(seed: int = 0) -> dict:
    key = jax.random.key(seed)
    ks = iter(jax.random.split(key, 40))
    nrm = lambda shape, s: jax.random.normal(next(ks), shape, jnp.float32) * s
    gain = lambda shape: 1.0 + nrm(shape, 0.02)
    nr = max(DEPTH - 1, 0)
    return {
        "x": nrm((BATCH, SEQ, D_MODEL), 1.0),
        "w_in_first": nrm((D_MODEL, IN_WIDTH_FIRST), D_MODEL ** -0.5),
        "mu_first": jax.random.uniform(next(ks), (SHIFT_WIDTH_FIRST,), jnp.float32),
        "w_in_rest": nrm((nr, D_MODEL, IN_WIDTH_REST), D_MODEL ** -0.5),
        "mu_rest": jax.random.uniform(next(ks), (nr, SHIFT_WIDTH_REST), jnp.float32),
        "rwkv_v0": 1.0 + nrm((nr, B_WIDTH), 0.1),
        "rwkv_v2": nrm((nr, MV_LORA, B_WIDTH), 0.5 * MV_LORA ** -0.5),
        "ffn1_norm": gain((DEPTH, D_MODEL)),
        "ffn1_w_gu": nrm((DEPTH, D_MODEL, 2 * D_FF), D_MODEL ** -0.5),
        "ffn1_w_down": nrm((DEPTH, D_FF, D_MODEL), D_FF ** -0.5),
        "mix_norm": gain((DEPTH, D_MODEL)),
        "sgu_ln_g": gain((DEPTH, A_WIDTH)),
        "sgu_ln_b": nrm((DEPTH, A_WIDTH), 0.02),
        "sgu_w_s": nrm((DEPTH, A_GROUPS, CHUNK, CHUNK), CHUNK ** -0.5),
        "sgu_b_s": 1.0 + nrm((DEPTH, A_GROUPS, CHUNK), 0.02),
        "rwkv_w0": jax.random.uniform(next(ks), (DEPTH, B_WIDTH), jnp.float32, -5.0, 0.0),
        "rwkv_w2": nrm((DEPTH, DECAY_LORA, B_WIDTH), 0.5 * DECAY_LORA ** -0.5),
        "rwkv_a0": nrm((DEPTH, B_WIDTH), 0.1),
        "rwkv_a2": nrm((DEPTH, AAA_LORA, B_WIDTH), 0.5 * AAA_LORA ** -0.5),
        "rwkv_k_k": 0.85 + nrm((DEPTH, B_WIDTH), 0.02),
        "rwkv_k_a": gain((DEPTH, B_WIDTH)),
        "rwkv_r_k": nrm((DEPTH, B_HEADS, B_HEAD_DIM), 0.1),
        "rwkv_gn_g": gain((DEPTH, B_WIDTH)),
        "rwkv_gn_b": nrm((DEPTH, B_WIDTH), 0.02),
        "w_proj_a": nrm((DEPTH, A_WIDTH, D_MODEL), A_WIDTH ** -0.5),
        "w_proj_b": nrm((DEPTH, B_WIDTH, D_MODEL), B_WIDTH ** -0.5),
        "w_out": nrm((DEPTH, D_MODEL, D_MODEL), D_MODEL ** -0.5),
        "ffn2_norm": gain((DEPTH, D_MODEL)),
        "ffn2_w_gu": nrm((DEPTH, D_MODEL, 2 * D_FF), D_MODEL ** -0.5),
        "ffn2_w_down": nrm((DEPTH, D_FF, D_MODEL), D_FF ** -0.5),
        "final_norm": gain((D_MODEL,)),
    }

def first_block(x, w_in_first, mu_first, w_in_rest, mu_rest, rwkv_v0, rwkv_v2,
              ffn1_norm, ffn1_w_gu, ffn1_w_down, mix_norm,
              sgu_ln_g, sgu_ln_b, sgu_w_s, sgu_b_s,
              rwkv_w0, rwkv_w2, rwkv_a0, rwkv_a2, rwkv_k_k, rwkv_k_a, rwkv_r_k,
              rwkv_gn_g, rwkv_gn_b, w_proj_a, w_proj_b, w_out,
              ffn2_norm, ffn2_w_gu, ffn2_w_down, final_norm):
    v_first = None
    for layer in range(DEPTH):
        h = rms_norm(x, ffn1_norm[layer])
        x = x + 0.5 * swiglu_ffn(h, ffn1_w_gu[layer], ffn1_w_down[layer])

        h = rms_norm(x, mix_norm[layer])
        if layer == 0:
            p = h @ w_in_first
            mu = mu_first
            v0, v2 = None, None
        else:
            p = h @ w_in_rest[layer - 1]
            mu = mu_rest[layer - 1]
            v0, v2 = rwkv_v0[layer - 1], rwkv_v2[layer - 1]
        gate_a = p[..., :D_MODEL]
        gate_b = p[..., D_MODEL:GATE_WIDTH]
        u_a = p[..., GATE_WIDTH:GATE_WIDTH + A_WIDTH]
        v_a = p[..., GATE_WIDTH + A_WIDTH:GATE_WIDTH + 2 * A_WIDTH]
        p_b = token_shift_mix(p[..., GATE_WIDTH + 2 * A_WIDTH:], mu)

        y_a = chunked_sgu(u_a, v_a, sgu_ln_g[layer], sgu_ln_b[layer],
                          sgu_w_s[layer], sgu_b_s[layer])
        y_b, v_first = rwkv7_time_mix(p_b, v_first, rwkv_w0[layer], rwkv_w2[layer],
                                      rwkv_a0[layer], rwkv_a2[layer], rwkv_k_k[layer],
                                      rwkv_k_a[layer], rwkv_r_k[layer],
                                      rwkv_gn_g[layer], rwkv_gn_b[layer], v0, v2)

        merged = (jax.nn.sigmoid(gate_a) * (y_a @ w_proj_a[layer])
                  + jax.nn.sigmoid(gate_b) * (y_b @ w_proj_b[layer]))
        x = x + merged @ w_out[layer]

        h = rms_norm(x, ffn2_norm[layer])
        x = x + 0.5 * swiglu_ffn(h, ffn2_w_gu[layer], ffn2_w_down[layer])
    return rms_norm(x, final_norm)


_first_inputs = first_inputs


def first_inputs(seed=0):
    import zlib

    import numpy as np

    out = dict(_first_inputs(seed))
    spreads = {}
    factors = {'rwkv_v0': 4.014,
     'ffn1_norm': 3.79,
     'sgu_ln_g': 8.0,
     'sgu_ln_b': 8.0,
     'sgu_b_s': 6.744,
     'rwkv_w2': 2.703,
     'rwkv_k_k': 6.91,
     'rwkv_k_a': 4.169,
     'rwkv_gn_g': 4.428,
     'rwkv_gn_b': 4.558,
     'ffn2_norm': 5.868,
     'final_norm': 2.77}
    for name, (base, spread) in spreads.items():
        noise = np.random.default_rng([zlib.crc32(name.encode()), seed]).standard_normal(out[name].shape)
        drawn = base * np.exp(spread * noise) if base else spread * noise
        out[name] = __import__('jax').numpy.asarray(drawn.astype(out[name].dtype))
    for name, factor in factors.items():
        out[name] = (out[name] * factor).astype(out[name].dtype)
    return out


_narrow_inputs = first_inputs


def first_inputs(seed=0):

    out = dict(_narrow_inputs(seed))
    wider = {'rwkv_v0': 12.0,
     'rwkv_v2': 12.0,
     'sgu_ln_g': 5.88,
     'sgu_ln_b': 5.92,
     'sgu_b_s': 4.65,
     'rwkv_k_k': 7.89,
     'rwkv_gn_g': 4.7,
     'rwkv_gn_b': 4.82,
     'final_norm': 3.11}
    for name, times in wider.items():
        mean = out[name].mean()
        out[name] = (mean + times * (out[name] - mean)).astype(out[name].dtype)
    return out


GRID_W = 64
CTX_LEN = 256
N_MIXERS = 3
HEAD_DIM = 64
ROPE_BASE = 10000.0
ROPE_PAIRS_PER_AXIS = HEAD_DIM // 4
Q_BLOCK = 128
NEG_INF = -1e30
DIFF_HEADS = D_MODEL // (2 * HEAD_DIM)
NA_HEADS = D_MODEL // HEAD_DIM
NA_KH_MAX = 8
NA_KW = 16
SWA_HEADS = D_MODEL // HEAD_DIM
SWA_KV_HEADS = SWA_HEADS // 4
SWA_WINDOW = 128
CONV_W = 3
N_LAYERS_A = (DEPTH + N_MIXERS - 1) // N_MIXERS
N_LAYERS_B = (DEPTH + N_MIXERS - 2) // N_MIXERS
N_LAYERS_C = (DEPTH + N_MIXERS - 3) // N_MIXERS


def rmsnorm(t, g):
    tf = t.astype(jnp.float32)
    tf = tf * lax.rsqrt(jnp.mean(tf * tf, axis=-1, keepdims=True) + NORM_EPS)
    return tf.astype(t.dtype) * g

def rope_tables(n_tokens, dtype):
    t = jnp.arange(n_tokens, dtype=jnp.int32)
    row = (t // GRID_W).astype(jnp.float32)
    col = (t % GRID_W).astype(jnp.float32)
    inv = ROPE_BASE ** (-jnp.arange(ROPE_PAIRS_PER_AXIS, dtype=jnp.float32) / ROPE_PAIRS_PER_AXIS)
    ar = row[:, None] * inv[None, :]
    ac = col[:, None] * inv[None, :]
    return tuple(a.astype(dtype) for a in (jnp.cos(ar), jnp.sin(ar), jnp.cos(ac), jnp.sin(ac)))

def _rotate(t, cos, sin):
    t1, t2 = jnp.split(t, 2, axis=-1)
    return jnp.concatenate([t1 * cos - t2 * sin, t2 * cos + t1 * sin], axis=-1)

def rope_2d(t, tables):
    cr, sr, cc, sc = (a[None, :, None, :] for a in tables)
    half = HEAD_DIM // 2
    return jnp.concatenate([_rotate(t[..., :half], cr, sr), _rotate(t[..., half:], cc, sc)], axis=-1)

def _to_blocks(t, blk):
    b, s = t.shape[:2]
    return jnp.moveaxis(t.reshape(b, s // blk, blk, *t.shape[2:]), 1, 0)

def _from_blocks(t):
    t = jnp.moveaxis(t, 0, 1)
    return t.reshape(t.shape[0], t.shape[1] * t.shape[2], *t.shape[3:])

def _diff_attend(q, k, v, lam, subln, lam_init):
    s = jnp.einsum('bqhjd,bkhjd->bhjqk', q, k).astype(jnp.float32) * (HEAD_DIM ** -0.5)
    p = jax.nn.softmax(s, axis=-1)
    a = (p[:, :, 0] - lam * p[:, :, 1]).astype(v.dtype)
    o = jnp.einsum('bhqk,bkhe->bqhe', a, v)
    o = rmsnorm(o, subln) * (1.0 - lam_init)
    return o.reshape(o.shape[0], o.shape[1], -1)

def diff_attention(h, hc, wqkv, wo, lam_vecs, subln, layer_idx, tables, need_ctx):
    B, S, _ = h.shape
    H, dh = DIFF_HEADS, HEAD_DIM
    lam_init = 0.8 - 0.6 * math.exp(-0.3 * layer_idx)
    lv = lam_vecs.astype(jnp.float32)
    lam = jnp.exp(jnp.sum(lv[0] * lv[1])) - jnp.exp(jnp.sum(lv[2] * lv[3])) + lam_init

    def proj(t):
        n = t.shape[1]
        q, k, v = jnp.split(t @ wqkv, 3, axis=-1)
        return q.reshape(B, n, 2 * H, dh), k.reshape(B, n, 2 * H, dh), v.reshape(B, n, H, 2 * dh)

    q, k, v = proj(h)
    q, k = rope_2d(q, tables), rope_2d(k, tables)
    qc, kc, vc = proj(hc)
    q = q.reshape(B, S, H, 2, dh)
    k = k.reshape(B, S, H, 2, dh)
    n_ctx = hc.shape[1]
    qc = qc.reshape(B, n_ctx, H, 2, dh)
    kc = kc.reshape(B, n_ctx, H, 2, dh)
    k_all = jnp.concatenate([k, kc], axis=1)
    v_all = jnp.concatenate([v, vc], axis=1)
    y = _from_blocks(lax.map(lambda qb: _diff_attend(qb, k_all, v_all, lam, subln, lam_init),
                             _to_blocks(q, Q_BLOCK))) @ wo
    yc = (_diff_attend(qc, kc, vc, lam, subln, lam_init) @ wo) if need_ctx else None
    return y, yc

def _mha(q, k, v, mask=None, bias=None):
    s = jnp.einsum('bqhd,bkhd->bhqk', q, k).astype(jnp.float32) * (q.shape[-1] ** -0.5)
    if bias is not None:
        s = s + bias
    if mask is not None:
        s = jnp.where(mask, s, NEG_INF)
    p = jax.nn.softmax(s, axis=-1).astype(v.dtype)
    return jnp.einsum('bhqk,bkhd->bqhd', p, v)

def neighbourhood_attention(h, hc, wqkv, wo, rpb, need_ctx):
    B, S, _ = h.shape
    H, dh = NA_HEADS, HEAD_DIM
    rows = S // GRID_W
    kh = min(NA_KH_MAX, rows)
    kw = NA_KW

    def proj(t):
        n = t.shape[1]
        q, k, v = jnp.split(t @ wqkv, 3, axis=-1)
        return q.reshape(B, n, H, dh), k.reshape(B, n, H, dh), v.reshape(B, n, H, dh)

    q, k, v = proj(h)
    qc, kc, vc = proj(hc)
    n_ctx = hc.shape[1]
    kg = k.reshape(B, rows, GRID_W, H, dh)
    vg = v.reshape(B, rows, GRID_W, H, dh)
    col = jnp.arange(GRID_W, dtype=jnp.int32)
    col_start = jnp.clip(col - kw // 2, 0, GRID_W - kw)
    col_ok = (col[None, :] >= col_start[:, None]) & (col[None, :] < col_start[:, None] + kw)
    dx_idx = jnp.clip(col[None, :] - col[:, None], -(kw - 1), kw - 1) + (kw - 1)
    mask = jnp.concatenate(
        [jnp.broadcast_to(col_ok[:, None, :], (GRID_W, kh, GRID_W)).reshape(GRID_W, kh * GRID_W),
         jnp.ones((GRID_W, n_ctx), dtype=bool)], axis=-1)
    rpb32 = rpb.astype(jnp.float32)
    ctx_bias = jnp.zeros((H, GRID_W, n_ctx), jnp.float32)

    def row_block(args):
        r, q_row = args
        rs = jnp.clip(r - kh // 2, 0, rows - kh)
        k_win = lax.dynamic_slice_in_dim(kg, rs, kh, axis=1).reshape(B, kh * GRID_W, H, dh)
        v_win = lax.dynamic_slice_in_dim(vg, rs, kh, axis=1).reshape(B, kh * GRID_W, H, dh)
        dy_idx = rs + jnp.arange(kh, dtype=jnp.int32) - r + (NA_KH_MAX - 1)
        bias = rpb32[:, dy_idx[None, :, None], dx_idx[:, None, :]].reshape(H, GRID_W, kh * GRID_W)
        bias = jnp.concatenate([bias, ctx_bias], axis=-1)
        o = _mha(q_row, jnp.concatenate([k_win, kc], axis=1), jnp.concatenate([v_win, vc], axis=1),
                 mask, bias)
        return o.reshape(B, GRID_W, H * dh)

    q_rows = jnp.moveaxis(q.reshape(B, rows, GRID_W, H, dh), 1, 0)
    y = _from_blocks(lax.map(row_block, (jnp.arange(rows, dtype=jnp.int32), q_rows))) @ wo
    yc = (_mha(qc, kc, vc).reshape(B, n_ctx, H * dh) @ wo) if need_ctx else None
    return y, yc

def _gqa_sink(q, k, v, sink, mask=None):
    s = jnp.einsum('bqkgd,bmkd->bkgqm', q, k).astype(jnp.float32) * (HEAD_DIM ** -0.5)
    if mask is not None:
        s = jnp.where(mask, s, NEG_INF)
    b, kv, g, n, _ = s.shape
    s = jnp.concatenate([s, jnp.broadcast_to(sink[None, :, :, None, None], (b, kv, g, n, 1))], axis=-1)
    p = jax.nn.softmax(s, axis=-1)[..., :-1].astype(v.dtype)
    o = jnp.einsum('bkgqm,bmkd->bqkgd', p, v)
    return o.reshape(b, n, -1)

def window_gqa_sink(h, hc, wqkv, wo, sinks, tables, need_ctx):
    B, S, _ = h.shape
    H, KV, dh = SWA_HEADS, SWA_KV_HEADS, HEAD_DIM
    G = H // KV
    n_ctx = hc.shape[1]

    def proj(t):
        n = t.shape[1]
        q, k, v = jnp.split(t @ wqkv, [H * dh, (H + KV) * dh], axis=-1)
        return q.reshape(B, n, H, dh), k.reshape(B, n, KV, dh), v.reshape(B, n, KV, dh)

    q, k, v = proj(h)
    q, k = rope_2d(q, tables), rope_2d(k, tables)
    q = q.reshape(B, S, KV, G, dh)
    qc, kc, vc = proj(hc)
    qc = qc.reshape(B, n_ctx, KV, G, dh)
    sink = sinks.astype(jnp.float32).reshape(KV, G)

    pad = SWA_WINDOW
    kp = jnp.pad(k, ((0, 0), (pad, pad), (0, 0), (0, 0)))
    vp = jnp.pad(v, ((0, 0), (pad, pad), (0, 0), (0, 0)))
    span = Q_BLOCK + 2 * pad
    qi = jnp.arange(Q_BLOCK, dtype=jnp.int32)
    kj = jnp.arange(span, dtype=jnp.int32)
    band = (kj[None, :] >= qi[:, None]) & (kj[None, :] <= qi[:, None] + 2 * SWA_WINDOW)
    ctx_ok = jnp.ones((Q_BLOCK, n_ctx), dtype=bool)

    def block(args):
        n, q_blk = args
        start = n * Q_BLOCK
        k_loc = lax.dynamic_slice_in_dim(kp, start, span, axis=1)
        v_loc = lax.dynamic_slice_in_dim(vp, start, span, axis=1)
        kpos = start - pad + kj
        valid = band & ((kpos >= 0) & (kpos < S))[None, :]
        mask = jnp.concatenate([valid, ctx_ok], axis=-1)
        return _gqa_sink(q_blk, jnp.concatenate([k_loc, kc], axis=1),
                         jnp.concatenate([v_loc, vc], axis=1), sink, mask)

    nb = S // Q_BLOCK
    y = _from_blocks(lax.map(block, (jnp.arange(nb, dtype=jnp.int32), _to_blocks(q, Q_BLOCK)))) @ wo
    yc = (_gqa_sink(qc, kc, vc, sink) @ wo) if need_ctx else None
    return y, yc

def conv_ffn(t, w_up, w_conv, b_conv, w_down):
    n = t.shape[1]
    u = t @ w_up
    half = CONV_W // 2
    up = jnp.pad(u, ((0, 0), (half, half), (0, 0)))
    acc = b_conv
    for tap in range(CONV_W):
        acc = acc + up[:, tap:tap + n] * w_conv[tap]
    a, g = jnp.split(acc, 2, axis=-1)
    return (jax.nn.silu(g) * a) @ w_down

def second_inputs(seed: int = 0) -> dict:
    key = jax.random.key(seed)
    ks = iter(jax.random.split(key, 32))

    def nrm(shape, scale):
        return jax.random.normal(next(ks), shape, jnp.float32) * scale

    D = D_MODEL
    s = D ** -0.5
    return {
        "x": nrm((BATCH, SEQ, D), 1.0),
        "c": nrm((BATCH, D), 1.0),
        "ctx": nrm((BATCH, CTX_LEN, D), 1.0),
        "c_ctx": nrm((D,), 1.0),
        "ada_w": nrm((DEPTH, D, 6 * D), s),
        "ada_b": nrm((DEPTH, 6 * D), 0.02),
        "norm_mix": 1.0 + nrm((DEPTH, D), 0.05),
        "norm_ffn": 1.0 + nrm((DEPTH, D), 0.05),
        "norm_out": 1.0 + nrm((D,), 0.05),
        "ffn_up": nrm((DEPTH, D, 2 * D_FF), s),
        "ffn_conv": nrm((DEPTH, CONV_W, 2 * D_FF), CONV_W ** -0.5),
        "ffn_conv_b": nrm((DEPTH, 2 * D_FF), 0.02),
        "ffn_down": nrm((DEPTH, D_FF, D), D_FF ** -0.5),
        "a_wqkv": nrm((N_LAYERS_A, D, 3 * D), s),
        "a_wo": nrm((N_LAYERS_A, D, D), s),
        "a_lambda": nrm((N_LAYERS_A, 4, HEAD_DIM), 0.1),
        "a_subln": 1.0 + nrm((N_LAYERS_A, 2 * HEAD_DIM), 0.05),
        "b_wqkv": nrm((N_LAYERS_B, D, 3 * D), s),
        "b_wo": nrm((N_LAYERS_B, D, D), s),
        "b_rpb": nrm((N_LAYERS_B, NA_HEADS, 2 * NA_KH_MAX - 1, 2 * NA_KW - 1), 0.5),
        "c_wqkv": nrm((N_LAYERS_C, D, (SWA_HEADS + 2 * SWA_KV_HEADS) * HEAD_DIM), s),
        "c_wo": nrm((N_LAYERS_C, D, D), s),
        "c_sinks": nrm((N_LAYERS_C, SWA_HEADS), 0.5),
    }

def second_block(x, c, ctx, c_ctx, ada_w, ada_b, norm_mix, norm_ffn, norm_out,
              ffn_up, ffn_conv, ffn_conv_b, ffn_down,
              a_wqkv, a_wo, a_lambda, a_subln,
              b_wqkv, b_wo, b_rpb,
              c_wqkv, c_wo, c_sinks):
    S = x.shape[1]
    tables = rope_tables(S, x.dtype)
    xc = ctx
    silu_c = jax.nn.silu(c)
    silu_cc = jax.nn.silu(c_ctx)
    for i in range(DEPTH):
        need_ctx = i < DEPTH - 1
        kind, j = i % N_MIXERS, i // N_MIXERS
        sh1, sc1, g1, sh2, sc2, g2 = jnp.split((silu_c @ ada_w[i] + ada_b[i])[:, None, :], 6, axis=-1)
        csh1, csc1, cg1, csh2, csc2, cg2 = jnp.split(silu_cc @ ada_w[i] + ada_b[i], 6, axis=-1)
        h = rmsnorm(x, norm_mix[i]) * (1.0 + sc1) + sh1
        hc = rmsnorm(xc, norm_mix[i]) * (1.0 + csc1) + csh1
        if kind == 0:
            y, yc = diff_attention(h, hc, a_wqkv[j], a_wo[j], a_lambda[j], a_subln[j], i, tables, need_ctx)
        elif kind == 1:
            y, yc = neighbourhood_attention(h, hc, b_wqkv[j], b_wo[j], b_rpb[j], need_ctx)
        else:
            y, yc = window_gqa_sink(h, hc, c_wqkv[j], c_wo[j], c_sinks[j], tables, need_ctx)
        x = x + g1 * y
        h2 = rmsnorm(x, norm_ffn[i]) * (1.0 + sc2) + sh2
        x = x + g2 * conv_ffn(h2, ffn_up[i], ffn_conv[i], ffn_conv_b[i], ffn_down[i])
        if need_ctx:
            xc = xc + cg1 * yc
            hc2 = rmsnorm(xc, norm_ffn[i]) * (1.0 + csc2) + csh2
            xc = xc + cg2 * conv_ffn(hc2, ffn_up[i], ffn_conv[i], ffn_conv_b[i], ffn_down[i])
    return rmsnorm(x, norm_out)


def setup_inputs(seed=0):
    out = dict(first_inputs(seed))
    for name, value in second_inputs(seed + 1).items():
        if name != "x":
            out[name + "_2"] = value
    return out


def reference(
    x, w_in_first, mu_first, w_in_rest, mu_rest, rwkv_v0, rwkv_v2, ffn1_norm, ffn1_w_gu,
    ffn1_w_down, mix_norm, sgu_ln_g, sgu_ln_b, sgu_w_s, sgu_b_s, rwkv_w0, rwkv_w2, rwkv_a0,
    rwkv_a2, rwkv_k_k, rwkv_k_a, rwkv_r_k, rwkv_gn_g, rwkv_gn_b, w_proj_a, w_proj_b, w_out,
    ffn2_norm, ffn2_w_gu, ffn2_w_down, final_norm, c_2, ctx_2, c_ctx_2, ada_w_2, ada_b_2,
    norm_mix_2, norm_ffn_2, norm_out_2, ffn_up_2, ffn_conv_2, ffn_conv_b_2, ffn_down_2,
    a_wqkv_2, a_wo_2, a_lambda_2, a_subln_2, b_wqkv_2, b_wo_2, b_rpb_2, c_wqkv_2, c_wo_2,
    c_sinks_2,
):
    x = first_block(
        x, w_in_first, mu_first, w_in_rest, mu_rest, rwkv_v0, rwkv_v2, ffn1_norm, ffn1_w_gu,
        ffn1_w_down, mix_norm, sgu_ln_g, sgu_ln_b, sgu_w_s, sgu_b_s, rwkv_w0, rwkv_w2, rwkv_a0,
        rwkv_a2, rwkv_k_k, rwkv_k_a, rwkv_r_k, rwkv_gn_g, rwkv_gn_b, w_proj_a, w_proj_b, w_out,
        ffn2_norm, ffn2_w_gu, ffn2_w_down, final_norm,
    )
    return second_block(
        x, c_2, ctx_2, c_ctx_2, ada_w_2, ada_b_2, norm_mix_2, norm_ffn_2, norm_out_2, ffn_up_2,
        ffn_conv_2, ffn_conv_b_2, ffn_down_2, a_wqkv_2, a_wo_2, a_lambda_2, a_subln_2, b_wqkv_2,
        b_wo_2, b_rpb_2, c_wqkv_2, c_wo_2, c_sinks_2,
    )


_drawn_inputs = setup_inputs


def setup_inputs(seed=0):
    import zlib

    import numpy as np

    out = dict(_drawn_inputs(seed))
    spreads = {}
    factors = {'ada_b_2': 2.918,
     'norm_mix_2': 5.543,
     'ffn_conv_b_2': 7.887,
     'a_subln_2': 5.155,
     'b_rpb_2': 4.207}
    for name, (base, spread) in spreads.items():
        noise = np.random.default_rng([zlib.crc32(name.encode()), seed]).standard_normal(out[name].shape)
        drawn = base * np.exp(spread * noise) if base else spread * noise
        out[name] = __import__('jax').numpy.asarray(drawn.astype(out[name].dtype))
    for name, factor in factors.items():
        out[name] = (out[name] * factor).astype(out[name].dtype)
    return out
```

```python
from contextlib import ExitStack, contextmanager

import numpy as np
import concourse.bass as bass
from concourse import mybir

F32 = mybir.dt.float32
F32R = mybir.dt.float32r
ACT = mybir.ActivationFunctionType
ALU = mybir.AluOpType
AX = mybir.AxisListType

P = 128
D = 1024
T = 256
NT = T // P
KT = D // P
F = 2816
FT = F // P
LORA = 64
MV = 32
CHUNK = 64
HEADS = 16
HD = 64
SHIFT = (3 * D + 2 * LORA, 3 * D + 2 * LORA + MV)
UNIT = 2048
RAW, SPLIT = 2, 4
NORM_EPS, LN_EPS, GN_EPS = 1e-6, 1e-5, 64e-5
DECAY = float(np.exp(np.float32(-0.5)))
LAM_INIT = 0.2
SCALE = 0.125

C_ID, C_LEVEL, C_LEVEL0T = 0, 128, 128 * 7
C_GRAM, C_TRI, C_TRIX, C_BD, C_TRIU = 128 * 8, 128 * 10, 128 * 11, 128 * 12, 128 * 13
C_CHUNK = 128 * 14
NCONST = C_CHUNK + 2


def constants():
    a = np.arange(P)
    row, col = a[:, None], a[None, :]
    same = row // CHUNK == col // CHUNK
    out = np.zeros((P, NCONST), np.float32)
    out[:, C_ID:C_ID + P] = row == col
    for j in range(6):
        m = (row >> (j + 1) == col >> (j + 1)) & (row >> j & 1 == 1) & (col >> j & 1 == 0)
        out[:, C_LEVEL + P * j:C_LEVEL + P * (j + 1)] = m
        if j == 0:
            out[:, C_LEVEL0T:C_LEVEL0T + P] = m.T
    out[:, C_GRAM:C_GRAM + P] = (row < col) & same
    out[:, C_GRAM + P:C_GRAM + 2 * P] = (row <= col) & same
    out[:, C_TRI:C_TRI + P] = ((row <= col) & same) * np.float32(-DECAY)
    out[:, C_TRIX:C_TRIX + P] = ((row < col) & same) * np.float32(-DECAY)
    out[:, C_BD:C_BD + P] = row // HD == col // HD
    out[:, C_TRIU:C_TRIU + P] = row <= col
    for c in range(2):
        out[:, C_CHUNK + c] = (a // CHUNK == c) * np.float32(-DECAY)
    return out


def rope_constants():
    t = np.arange(T)
    inv = (np.float32(10000.0) ** (-np.arange(16, dtype=np.float32) / np.float32(16))).astype(np.float32)
    ar = (t // 64).astype(np.float32)[:, None] * inv
    ac = (t % 64).astype(np.float32)[:, None] * inv
    cos = np.concatenate([np.cos(ar), np.cos(ar), np.cos(ac), np.cos(ac)], 1)
    sin = np.concatenate([-np.sin(ar), np.sin(ar), -np.sin(ac), np.sin(ac)], 1)
    return np.stack([cos, sin]).reshape(2, NT, P, 64).transpose(2, 0, 1, 3).astype(np.float32)


def window_constants():
    q, k = np.arange(P)[:, None] % 64, np.arange(T)[None, :] % 64
    start = np.clip(q - 8, 0, 48)
    return np.where((k >= start) & (k < start + 16), 0.0, -1e30).astype(np.float32)


V_W0, V_A0, V_KK, V_KA, V_RK, V_GNG, V_GNB, V_LNG, V_LNB, V_V0 = range(10)
V_FINAL, V_OUT, V_ADA = 20, 21, 22
NVEC = V_ADA + 12
G_FFN1, G_MIX, G_FFN2, G_NMIX, G_NFFN = 0, 16, 32, 48, 64
G_BS = 80
NCOL = G_BS + 16


def stream_plan():
    plan, at = {}, 0

    def add(name, units):
        nonlocal at
        plan[name] = (at, units)
        at += units

    for l in range(2):
        add(f"gu1{l}", 22), add(f"down1{l}", 11)
        add(f"pb{l}", 14), add(f"sgu{l}", 8), add(f"ga{l}", 4), add(f"pa{l}", 4), add(f"gb{l}", 4)
        add(f"pr{l}", 4), add(f"out{l}", 4)
        add(f"gu2{l}", 22), add(f"down2{l}", 11)
    add("ada0", 24), add("ada1", 24)
    add("qkv0", 12), add("qkvc0", 12), add("wo0", 4), add("woc0", 4)
    add("up0", 22), add("cdown0", 11), add("upc0", 22), add("cdownc0", 11)
    add("qkv1", 12), add("kvc1", 8), add("wo1", 4), add("up1", 22), add("cdown1", 11)
    return plan, at


PLAN, NUNITS = stream_plan()


class Counts:

    def __init__(self, eng, sems):
        self.eng, self.sems = eng, sems
        self.base, self.local, self.i, self.per = {}, {}, None, {}

    def next(self, view, k=1):
        if self.i is None:
            self.base[view] = self.base.get(view, 0) + k
            return self.base[view]
        self.local[view] = self.local.get(view, 0) + k
        return self.i * self.per[view] + (self.base.get(view, 0) + self.local[view])

    @contextmanager
    def loop(self, n, per):
        with self.eng.Fori(0, n) as i:
            self.i, self.per, self.local = i, per, {}
            yield i
            assert self.local == per, (self.local, per)
            self.i = None
        for view, k in per.items():
            self.base[view] = self.base.get(view, 0) + n * k


def build(nc, wstream, vecs, cols, consts, x_in, ctx_in, mus, lora_wa, lora_v, wst, convw, cc, lam, subln,
          toe, rope, window, out, mod_scr, vfirst_scr):
    ctx = ExitStack()
    with ctx:
        top = nc.sbuf_base
        base = (top + 63) // 64 * 64
        place = {"at": base}

        def sb(name, shape, dt=F32, at=None):
            size = 4 * int(np.prod(shape[1:]))
            if at is None:
                at = place["at"]
                place["at"] += (size + 31) // 32 * 32
            assert at + size <= nc.sbuf_usable_end, (name, at + size)
            return nc.alloc_sbuf_tensor_at(name, list(shape), dt, offset=at)

        raw = sb("raw", [P, RAW, UNIT])
        w_hi = sb("w_hi", [P, SPLIT, UNIT], F32R)
        w_lo = sb("w_lo", [P, SPLIT, UNIT], F32R)
        X = sb("X", [P, NT, D])
        HA_hi, HA_lo = sb("HA_hi", [P, KT, T], F32R), sb("HA_lo", [P, KT, T], F32R)
        K_ = sb("K_", [P, NCONST])
        COL = sb("COL", [P, NCOL])
        SS = sb("SS", [P, 32])
        RS = sb("RS", [P, 32])
        ST = sb("ST", [P, 64])
        BN = sb("BN", [P, NT, HEADS])
        GAM = sb("GAM", [P, 32])
        MODC = sb("MODC", [P, 2, 4, KT, 2])
        MODS = sb("MODS", [P, 2, 2, KT, 2])
        arena = place["at"]
        KB = 1024

        def ar(name, kib, shape, dt=F32):
            return sb(name, shape, dt, at=arena + int(kib * KB))

        FT_hi, FT_lo = ar("FT_hi", 8, [P, FT, T], F32R), ar("FT_lo", 30, [P, FT, T], F32R)
        HID = ar("HID", 52, [P, 2, NT, 256])
        XN = ar("XN", 56, [P, NT, D])
        BC = ar("BC", 64, [P, 2, D])
        TF = ar("TF", 72, [P, 2, 512])
        HB_hi, HB_lo = ar("HB_hi", 78, [P, KT, T], F32R), ar("HB_lo", 86, [P, KT, T], F32R)
        R, K, V = ar("R", 0, [P, NT, D]), ar("K", 8, [P, NT, D]), ar("V", 16, [P, NT, D])
        KK, AA = ar("KK", 24, [P, NT, D]), ar("AA", 32, [P, NT, D])
        T1, T2 = ar("T1", 40, [P, NT, D]), ar("T2", 48, [P, NT, D])
        LOR = ar("LOR", 48, [P, NT, 160])
        LORT = ar("LORT", 50, [P, 512])
        W2A2, V2 = ar("W2A2", 56, [P, D]), ar("V2", 60, [MV, D])
        MU = ar("MU", 72, [P, SHIFT[1]])
        PREV = ar("PREV", 85, [P, 2, NT, 512])
        DIF = ar("DIF", 40, [P, NT, 512])
        VF = ar("VF", 72, [P, NT, D])
        ARBK = ar("ARBK", 56, [P, 4, 4, P])
        LG = ar("LG", 72, [P, 8, 512])
        S, SU = ar("S", 88, [P, 4, P]), ar("SU", 90, [P, 4, P])
        XX = ar("XX", 40, [P, 4, 2, 2, P])
        MVY = ar("MVY", 48, [P, 4, 256])
        TM = ar("TM", 52, [P, 4, 256])
        PM = ar("PM", 52, [P, 4, P])
        U = ar("U", 54, [P, 4, P])
        VA, UA = ar("VA", 8, [P, NT, D]), ar("UA", 16, [P, NT, D])
        MERG, GATE = ar("MERG", 24, [P, NT, D]), ar("GATE", 40, [P, NT, D])
        WST = ar("WST", 48, [P, 8, P])
        SQ = ar("SQ", 56, [P, NT, D])
        XC = ar("XC", 0, [P, NT, D])
        QTX, QTC = ar("QTX", 8, [P, KT, T]), ar("QTC", 16, [P, KT, T])
        KTT = ar("KTT", 24, [P, KT, 2 * T])
        VV = ar("VV", 40, [P, 4, D])
        PR = ar("PR", 76, [P, 2, 2, 512])
        AT = ar("AT", 84, [P, 2, 512])
        SC = ar("SC", 88, [P, 2, 512])
        BIAS = ar("BIAS", 16, [P, 2, 2, T])
        WIN = ar("WIN", 20, [P, T])
        ROPE = ar("ROPE", 76, [P, 2, NT, 64])
        LAMB = ar("LAMB", 92, [P, 4, HD])
        SUBL = ar("SUBL", 93, [P, P])
        QK = ar("QK", 64, [P, 512])
        US = ar("US", 52, [P, 2, NT, 512])
        CV = ar("CV", 76, [P, 2, 4, T])
        HV = ar("HV", 84, [P, 2, 2, T])
        CW = ar("CW", 88, [P, 4, 2 * FT])

        ACC = [ctx.enter_context(nc.psum_tensor(f"ACC{i}", [P, NT, 512], F32)) for i in range(2)]
        TP = [ctx.enter_context(nc.psum_tensor(f"TP{i}", [P, 512], F32)) for i in range(2)]
        M = [ctx.enter_context(nc.psum_tensor(f"M{i}", [P, 512], F32)) for i in range(2)]
        A4 = [ACC[0][:, 0, :], ACC[0][:, 1, :], ACC[1][:, 0, :], ACC[1][:, 1, :]]
        B4 = [TP[0][:, :], TP[1][:, :], M[0][:, :], M[1][:, :]]

        names = ["land0", "land1", "bc0", "bc1", "hi_ready", "lo_ready", "unit_done", "acc_ready", "acc_free0",
                 "acc_free1", "tp_ready", "tp_free0", "tp_free1", "tf_ready", "hi_feat", "feat_ready",
                 "xn_ready", "ss_ready", "rs_ready", "sil_ready", "hid_ready", "bc_free", "phase_done",
                 "p_ready", "mix_done", "shift0", "shift1", "zero_ready", "mu_land", "lora_tanh", "lora_tr",
                 "pre_ready", "sig_ready", "vsig_ready", "asig_ready", "gn_done", "merge_done", "res_ready",
                 "rs_pre", "v_final", "cc_hi", "modg_ready", "cw_land", "rope_land", "exp_ready", "exp_used",
                 "param_land", "v_stored", "vf_land", "gam_ready", "arbk_ready", "gram_ready", "lg_ready",
                 "x_ready", "t_ready", "t_masked", "u_ready", "mv_ready", "mv_copied", "pp_ready", "pm_ready",
                 "uu_ready", "u_copied", "sy_ready", "s_done", "y_done", "s_zero", "wst_land", "va_ready",
                 "gelu_ready", "gate_ready", "const_land", "x_land", "ctx_land", "cc_land", "cc_ready",
                 "mod_ready", "mod_stored", "lam_ready", "lam_exp", "lam_land", "q_ready", "sc_ready",
                 "max_ready", "prob_ready", "mix_ready", "at_ready", "o_ready", "o_copied", "o_free",
                 "sc_free", "bias0", "bias1", "bias_ready", "bias_free", "win_land", "u_copy", "cv_ready",
                 "cv_conv", "sg_ready", "hv_ready", "out_ready", "out_land"]
        sem = {n: ctx.enter_context(nc.semaphore(n)) for n in names}
        block = ctx.enter_context(nc.Block())

        def row(v):
            return vecs[v:v + 1, :].broadcast_to([P, D])

        def whole(t):
            return t[:, :, :].rearrange("p t n -> p (t n)")

        def heads(t):
            return t[:, :, :].rearrange("p t (h d) -> p (t h) d", d=HD)

        def ident(n=P):
            return K_[0:n, C_ID:C_ID + n]

        @block.sync
        def _(eng):
            for u in range(RAW):
                eng.dma_start(raw[:, u, :], wstream[u]).then_inc(sem[f"land{u}"], 16)
            with eng.Fori(1, NUNITS // RAW) as i:
                for s in range(RAW):
                    eng.wait_ge(sem["lo_ready"], i * RAW + (s + 1 - RAW))
                    eng.dma_start(raw[:, s, :], wstream[bass.ds(i * RAW + s, 1), :, :]
                                  .rearrange("a p n -> p (a n)")).then_inc(sem[f"land{s}"], 16)
            for u in range(NUNITS // RAW * RAW, NUNITS):
                eng.wait_ge(sem["lo_ready"], u + 1 - RAW)
                eng.dma_start(raw[:, u % RAW, :], wstream[u]).then_inc(sem[f"land{u % RAW}"], 16)
            eng.wait_ge(sem["out_ready"], 1)
            eng.dma_start(out.rearrange("a (t p) d -> p (a t) d", p=P), XN[:, :, :]).then_inc(sem["out_land"], 16)
            eng.wait_ge(sem["out_land"], 16)

        @block.tensor
        def _(pe):
            c = Counts(pe, sem)

            def phase():
                pe.drain().then_inc(sem["phase_done"], 1)
                pe.wait_ge(sem["phase_done"], c.next("phase_done", 4))

            st = {"u": 0, "b": 0, "tp": 0, "at": 0}
            Z = {"wkv": 0}

            def mm(*a, **k):
                return pe.matmul(*a, skip_group_check=True, **k)

            def unit_wide(h_hi, h_lo, part, width=512, tiles=NT):
                pe.wait_ge(sem["lo_ready"], c.next("lo_ready"))
                s, acc = st["u"] % SPLIT, ACC[st["b"] % 2]
                for k in range(4):
                    cols_ = slice(512 * k, 512 * k + width)
                    for t in range(tiles):
                        a = h_hi[:, 4 * part + k, P * t:P * t + P]
                        al = h_lo[:, 4 * part + k, P * t:P * t + P]
                        mm(acc[:, t, 0:width], a, w_hi[:, s, cols_], start=part == 0 and k == 0, stop=False)
                        mm(acc[:, t, 0:width], a, w_lo[:, s, cols_], start=False, stop=False)
                        last = mm(acc[:, t, 0:width], al, w_hi[:, s, cols_], start=False, stop=part == 1 and k == 3)
                last.then_inc(sem["unit_done"], 1)
                st["u"] += 1

            def block_wide(h_hi, h_lo, **k):
                pe.wait_ge(sem[f"acc_free{st['b'] % 2}"], c.next(f"acc_free{st['b'] % 2}"))
                unit_wide(h_hi, h_lo, 0, **k)
                unit_wide(h_hi, h_lo, 1, **k)
                st["b"] += 1

            def down():
                for n in range(2):
                    pe.wait_ge(sem[f"acc_free{(st['b'] + n) % 2}"], c.next(f"acc_free{(st['b'] + n) % 2}"))
                for j in range(FT // 2):
                    pe.wait_ge(sem["feat_ready"], c.next("feat_ready"))
                    pe.wait_ge(sem["lo_ready"], c.next("lo_ready"))
                    s = st["u"] % SPLIT
                    for k in range(2):
                        for n in range(2):
                            acc = ACC[(st["b"] + n) % 2]
                            cols_ = slice(1024 * k + 512 * n, 1024 * k + 512 * n + 512)
                            for t in range(NT):
                                a, al = (z[:, 2 * j + k, P * t:P * t + P] for z in (FT_hi, FT_lo))
                                first, end = j == 0 and k == 0, j == FT // 2 - 1 and k == 1
                                mm(acc[:, t, :], a, w_hi[:, s, cols_], start=first, stop=False)
                                mm(acc[:, t, :], a, w_lo[:, s, cols_], start=False, stop=False)
                                last = mm(acc[:, t, :], al, w_hi[:, s, cols_], start=False, stop=end)
                    last.then_inc(sem["unit_done"], 1)
                    st["u"] += 1
                    if j == 0:
                        yield
                st["b"] += 2

            def turn(src, n, dst=None, k0=0):
                pe.wait_ge(sem[f"tp_free{st['tp'] % 2}"], c.next(f"tp_free{st['tp'] % 2}"))
                bank = TP[st["tp"] % 2]
                for k in range(n):
                    for t in range(NT):
                        last = pe.transpose(bank[:, (NT * k + t) * P:(NT * k + t + 1) * P],
                                            src[:, t, (k0 + k) * P:(k0 + k + 1) * P], ident())
                last.then_inc(sem["tp_ready"], 1)
                st["tp"] += 1

            def features(src, wait):
                pe.wait_ge(sem[wait], c.next(wait))
                for g in range(KT // 2):
                    turn(src, 2, k0=2 * g)

            def need_features(n=KT // 2):
                pe.wait_ge(sem["feat_ready"], c.next("feat_ready", n))

            def swiglu():
                features(XN, "xn_ready")
                need_features()

                def hidden(b):
                    pe.wait_ge(sem["hid_ready"], c.next("hid_ready"))
                    turn(HID[:, b % 2, :, :], 2)

                block_wide(HA_hi, HA_lo)
                with c.loop(5, {"lo_ready": 4, "acc_free0": 1, "acc_free1": 1, "hid_ready": 2, "tp_free0": 1, "tp_free1": 1}):
                    for b in (1, 2):
                        block_wide(HA_hi, HA_lo)
                        hidden(b - 1)
                d = down()
                next(d)
                hidden(10)
                for _ in d:
                    pass

            def mixer(l):
                features(XN, "xn_ready")
                need_features()
                for j in range(6):
                    block_wide(HA_hi, HA_lo)
                block_wide(HA_hi, HA_lo, width=SHIFT[l] - 3 * D)
                pe.wait_ge(sem["lora_tanh"], c.next("lora_tanh"))
                pe.wait_ge(sem[f"tp_free{st['tp'] % 2}"], c.next(f"tp_free{st['tp'] % 2}"))
                bank = TP[st["tp"] % 2]
                for t in range(NT):
                    last = pe.transpose(bank[:, P * t:P * t + P], LOR[:, t, 0:P], ident())
                if l:
                    for t in range(NT):
                        last = pe.transpose(bank[0:MV, T + P * t:T + P * t + P], LOR[:, t, P:P + MV], ident())
                last.then_inc(sem["tp_ready"], 1)
                st["tp"] += 1
                pe.wait_ge(sem["lora_tr"], c.next("lora_tr"))
                pe.wait_ge(sem["param_land"], c.next("param_land", 16 * (1 + l)))

                def up(rows, w, col0):
                    for t in range(NT):
                        pe.wait_ge(sem[f"acc_free{st['b'] % 2}"], c.next(f"acc_free{st['b'] % 2}"))
                        for n in range(2):
                            last = mm(ACC[st["b"] % 2][:, n, :], LORT[rows, col0 + P * t:col0 + P * t + P],
                                      w[rows, 512 * n:512 * n + 512], start=True, stop=True)
                        last.then_inc(sem["acc_ready"], 1)
                        st["b"] += 1

                if l:
                    up(slice(0, MV), V2, T)
                up(slice(0, LORA), W2A2, 0)
                up(slice(LORA, 2 * LORA), W2A2, 0)
                for t in range(NT):
                    pe.wait_ge(sem["sig_ready"], c.next("sig_ready"))
                    for tri in (C_TRIX, C_TRI):
                        pe.wait_ge(sem[f"acc_free{st['b'] % 2}"], c.next(f"acc_free{st['b'] % 2}"))
                        for n in range(2):
                            last = mm(ACC[st["b"] % 2][:, n, :], K_[:, tri:tri + P], T1[:, t, 512 * n:512 * n + 512],
                                      start=True, stop=True)
                        last.then_inc(sem["acc_ready"], 1)
                        st["b"] += 1
                    for q in range(KT):
                        last = mm(M[0][:, 4 * q + 2 * t:4 * q + 2 * t + 2], T1[:, t, P * q:P * q + P],
                                  K_[:, C_CHUNK:C_CHUNK + 2], start=True, stop=True)
                last.then_inc(sem["gam_ready"], 1)
                phase()
                for g in range(2):
                    for t in range(NT):
                        wkv_parallel(g, t)
                        wkv_chain(g, t)
                phase()

                for j in range(4):
                    block_wide(HA_hi, HA_lo)
                pe.wait_ge(sem["va_ready"], c.next("va_ready"))
                for t in range(NT):
                    pe.wait_ge(sem[f"acc_free{st['b'] % 2}"], c.next(f"acc_free{st['b'] % 2}"))
                    for g in range(8):
                        last = mm(ACC[st["b"] % 2][:, g // 4, P * (g % 4):P * (g % 4) + P], WST[:, g, :],
                                  VA[:, t, P * g:P * g + P], start=True, stop=True)
                    last.then_inc(sem["acc_ready"], 1)
                    st["b"] += 1
                for j in range(2):
                    block_wide(HA_hi, HA_lo)
                features(VA, "xn_ready")
                need_features()
                for j in range(2):
                    block_wide(HB_hi, HB_lo)
                for j in range(2):
                    block_wide(HA_hi, HA_lo)
                features(R, "xn_ready")
                need_features()
                for j in range(2):
                    block_wide(HB_hi, HB_lo)
                features(MERG, "xn_ready")
                need_features()
                for j in range(2):
                    block_wide(HA_hi, HA_lo)

            def wkv_parallel(g, t):
                for p in range(4):
                    q = 4 * g + p
                    pe.wait_ge(sem[f"tp_free{st['tp'] % 2}"], c.next(f"tp_free{st['tp'] % 2}"))
                    bank = TP[st["tp"] % 2]
                    for n, src in enumerate((KK, R, AA, K)):
                        last = pe.transpose(bank[:, P * n:P * n + P], src[:, t, P * q:P * q + P], ident())
                    last.then_inc(sem["tp_ready"], 1)
                    st["tp"] += 1
                    pe.wait_ge(sem["arbk_ready"], c.next("arbk_ready"))
                    for hb in range(2):
                        rows = slice(HD * hb, HD * hb + HD)
                        n = 8 * (2 * g + t) + 2 * p + hb
                        if n >= 2:
                            pe.wait_ge(sem["lg_ready"], Z["wkv"] + n - 1)
                        ar_ = ARBK[rows, p, 0:2, :].rearrange("p a n -> p (a n)")
                        mm(M[hb][:, 0:256], ARBK[rows, p, 2, :], ar_, start=True, stop=True)
                        mm(M[hb][:, 256:512], ARBK[rows, p, 3, :], ar_, start=True, stop=True) \
                            .then_inc(sem["gram_ready"], 1)
                pe.wait_ge(sem["lg_ready"], Z["wkv"] + 8 * (2 * g + t + 1))
                for p in range(4):
                    for hb in range(2):
                        last = mm(A4[p][:, P * hb:P * hb + P], LG[:, 2 * p + hb, 0:P], ident(), start=True, stop=True)
                    last.then_inc(sem["t_ready"], 1)
                for j in range(1, 6):
                    for p in range(4):
                        pe.wait_ge(sem["x_ready"], c.next("x_ready"))
                        for hb in range(2):
                            last = mm(A4[p][:, P * hb:P * hb + P], LG[:, 2 * p + hb, 0:P], XX[:, p, hb, 0, :],
                                      start=True, stop=True)
                        last.then_inc(sem["t_ready"], 1)
                    for p in range(4):
                        pe.wait_ge(sem["t_masked"], c.next("t_masked"))
                        for hb in range(2):
                            tm = TM[:, p, P * hb:P * hb + P]
                            if j < 5:
                                mm(B4[p][:, 256 * hb:256 * hb + P], XX[:, p, hb, 1, :], tm, start=True, stop=True)
                            last = mm(B4[p][:, 256 * hb + P:256 * hb + 256], tm, XX[:, p, hb, 1, :],
                                      start=True, stop=True)
                        last.then_inc(sem["u_ready"], 1)
                for p in range(4):
                    q = 4 * g + p
                    for n, (col0, lg0) in enumerate(((0, 256), (P, 384))):
                        for hb in range(2):
                            last = mm(A4[p][:, col0 + HD * hb:col0 + HD * hb + HD], LG[:, 2 * p + hb, lg0:lg0 + P],
                                      V[:, t, P * q + HD * hb:P * q + HD * hb + HD], start=True, stop=True)
                    last.then_inc(sem["mv_ready"], 1)
                pe.wait_ge(sem["x_ready"], c.next("x_ready", 4))

            def wkv_chain(g, t):
                call = 2 * g + t
                if t == 0:
                    pe.wait_ge(sem["s_zero"], c.next("s_zero"))
                for ch in range(2):
                    rows = slice(CHUNK * ch, CHUNK * ch + CHUNK)
                    for p in range(4):
                        if ch == 0:
                            pe.wait_ge(sem["mv_copied"], c.next("mv_copied"))
                        else:
                            pe.wait_ge(sem["y_done"], Z["wkv"] + 8 * call + p + 1)
                            pe.wait_ge(sem["s_done"], Z["wkv"] + 8 * call + p + 1)
                        mm(A4[p][rows, 0:P], ARBK[:, p, 0, rows], S[:, p, :], start=True, stop=True) \
                            .then_inc(sem["pp_ready"], 1)
                    for p in range(4):
                        pe.wait_ge(sem["pm_ready"], c.next("pm_ready"))
                        for hb in range(2):
                            last = mm(B4[p][rows, HD * hb:HD * hb + HD], XX[rows, p, hb, 1, rows],
                                      PM[rows, p, HD * hb:HD * hb + HD], start=True, stop=True)
                        last.then_inc(sem["uu_ready"], 1)
                    for p in range(4):
                        q = 4 * g + p
                        pe.wait_ge(sem["u_copied"], c.next("u_copied"))
                        mm(A4[p][rows, P:2 * P], ARBK[:, p, 1, rows], S[:, p, :], start=True, stop=False)
                        for hb in range(2):
                            mm(A4[p][rows, P + HD * hb:P + HD * hb + HD],
                               LG[rows, 2 * p + hb, P + CHUNK * ch:P + CHUNK * ch + CHUNK],
                               U[rows, p, HD * hb:HD * hb + HD], start=False, stop=hb == 1)
                        cols_ = slice(P * q, P * q + P)
                        mm(B4[p][:, P:2 * P], AA[rows, t, cols_], U[rows, p, :], start=True, stop=False)
                        mm(B4[p][:, P:2 * P], K[rows, t, cols_], V[rows, t, cols_], start=False, stop=True) \
                            .then_inc(sem["sy_ready"], 1)
                pe.wait_ge(sem["y_done"], Z["wkv"] + 8 * (call + 1))
                pe.wait_ge(sem["s_done"], Z["wkv"] + 8 * (call + 1))

            def modulation():
                pe.wait_ge(sem["cc_ready"], c.next("cc_ready"))
                for l in range(2):
                    for j in range(12):
                        block_wide(HA_hi, HA_lo, tiles=1)
                        if j in (1, 3, 7, 9):
                            pe.wait_ge(sem["mod_ready"], c.next("mod_ready", 2))
                            for h in range(2):
                                pe.wait_ge(sem[f"tp_free{st['tp'] % 2}"], c.next(f"tp_free{st['tp'] % 2}"))
                                for k in range(4):
                                    m = 4 * h + k
                                    last = pe.transpose(TP[st["tp"] % 2][:, P * k:P * k + P],
                                                        XN[:, j // 2 % 2, P * m:P * m + P], ident())
                                last.then_inc(sem["tp_ready"], 1)
                                st["tp"] += 1

            def project(first, hf_hi, hf_lo):
                for n in range(first, 3):
                    for j in range(2):
                        block_wide(hf_hi, hf_lo)
                    if n < 2:
                        features(XN, "q_ready")

            def attend(l, s):
                nk = 4 if s == 0 else 2
                keys = slice(0, 512) if s == 0 else slice(T, 2 * T)
                qt_ = QTX if s == 0 else QTC
                turns = [(q, hp) for q in range(NT) for hp in range(8)]

                def scores(n):
                    q, hp = turns[n]
                    for hb in range(2):
                        rows = slice(HD * hb, HD * hb + HD)
                        pe.wait_ge(sem["sc_free"], c.next("sc_free"))
                        mm(A4[2 * (n % 2) + hb][:, 0:nk * P], qt_[rows, hp, P * q:P * q + P], KTT[rows, hp, keys],
                           start=True, stop=True).then_inc(sem["sc_ready"], 1)

                def values(n):
                    q, hp = turns[n]
                    for hb in range(1 if l == 0 else 2):
                        if l == 0 or hb == 0:
                            pe.wait_ge(sem["mix_ready"], c.next("mix_ready"))
                        pe.wait_ge(sem[f"tp_free{st['tp'] % 2}"], c.next(f"tp_free{st['tp'] % 2}"))
                        for k in range(nk):
                            last = pe.transpose(TP[st["tp"] % 2][:, P * k:P * k + P],
                                                PR[:, n % 2, hb, P * k:P * k + P], ident())
                        last.then_inc(sem["tp_ready"], 1)
                        st["tp"] += 1
                    for hb in range(1 if l == 0 else 2):
                        pe.wait_ge(sem["at_ready"], c.next("at_ready"))
                        if hb == 0:
                            pe.wait_ge(sem["o_free"], c.next("o_free"))
                        w = P if l == 0 else HD
                        for k in range(nk):
                            kt = k if s == 0 else 2 + k
                            last = mm(M[n % 2][:, w * hb:w * hb + w],
                                      AT[:, st["at"] % 2, P * k:P * k + P],
                                      VV[:, kt, P * hp + w * hb:P * hp + w * hb + w], start=k == 0, stop=k == nk - 1)
                        st["at"] += 1
                    last.then_inc(sem["o_ready"], 1)

                scores(0)
                for n in range(16):
                    if n < 15:
                        scores(n + 1)
                    values(n)

            def conv_ffn():
                features(XN, "xn_ready")
                need_features()

                def turn_up(b):
                    pe.wait_ge(sem["u_copy"], c.next("u_copy"))
                    for h in range(2):
                        turn(US[:, b % 2, :, :], 2, k0=2 * h)

                block_wide(HA_hi, HA_lo)
                with c.loop(5, {"lo_ready": 4, "acc_free0": 1, "acc_free1": 1, "u_copy": 2, "tp_free0": 2, "tp_free1": 2}):
                    for b in (1, 2):
                        block_wide(HA_hi, HA_lo)
                        turn_up(b - 1)
                d = down()
                turn_up(10)
                for _ in d:
                    pass

            pe.wait_ge(sem["const_land"], c.next("const_land", 32))
            for l in range(2):
                Z["wkv"] = 32 * l
                swiglu()
                mixer(l)
                swiglu()
            phase()
            modulation()
            phase()
            for l in range(2):
                for s in range(2):
                    features(XN, "xn_ready")
                    need_features()
                    project(l * s, *((HB_hi, HB_lo) if s else (HA_hi, HA_lo)))
                phase()
                for s in range(2 - l):
                    attend(l, s)
                    features(XN, "xn_ready")
                    need_features()
                    for j in range(2):
                        block_wide(HA_hi, HA_lo)
                    phase()
                for s in range(2 - l):
                    conv_ffn()
                    phase()

        class Side:

            def __init__(self, eng):
                self.c = Counts(eng, sem)
                self.pos, self.u, self.b, self.tp = 0, 0, 0, 0

            def turn(self):
                return 0 if self.c.i is None else self.c.i * SPLIT

            def skip(self, units, blocks):
                self.pos += units
                self.b += blocks

            def skip_turns(self, n):
                self.tp += n
                self.c.next("tp_ready", n)

            def reached(self, units=2):
                self.pos += units
                return self.turn() + self.pos

            def pair(self):
                self.b += 1
                return ACC[(self.b - 1) % 2]

            def bank(self):
                self.tp += 1
                return TP[(self.tp - 1) % 2]

            def acc_free(self):
                return sem[f"acc_free{(self.b - 1) % 2}"]

            def tp_free(self):
                return sem[f"tp_free{(self.tp - 1) % 2}"]

            @contextmanager
            def loop(self, n, per):
                pos, u, b, tp = self.pos, self.u, self.b, self.tp
                with self.c.loop(n, per) as i:
                    yield i
                    assert self.u - u == SPLIT and self.pos - pos == SPLIT and (self.b - b) % 2 == 0 and (self.tp - tp) % 2 == 0
                self.pos, self.u = self.pos + SPLIT * (n - 1), self.u + SPLIT * (n - 1)

        def tile(b, h, k, dyn):
            at = FT * h + 2 * b + k
            return slice(at, at + 1) if dyn is None else bass.ds(dyn * 4 + at, 1)

        @block.scalar
        def _(act):
            e = Side(act)
            c = e.c

            def phase():
                act.drain().then_inc(sem["phase_done"], 1)
                act.wait_ge(sem["phase_done"], c.next("phase_done", 4))

            def split(n):
                for _ in range(min(n, NUNITS - e.u)):
                    slot, s = e.u % RAW, e.u % SPLIT
                    act.wait_ge(sem[f"land{slot}"], c.next(f"land{slot}", 16))
                    if e.u >= SPLIT:
                        act.wait_ge(sem["unit_done"], e.turn() + (e.u + 1 - SPLIT))
                    act.activation(w_hi[:, s, :], raw[:, slot, :], ACT.Copy).then_inc(sem["hi_ready"], 1)
                    e.u += 1


            def squares(src, junk):
                act.wait_ge(sem["res_ready"], c.next("res_ready"))
                for t in range(NT):
                    last = act.activation(junk[:, t, :], src[:, t, :], ACT.Square, accum_out=SS[:, t:t + 1])
                last.then_inc(sem["ss_ready"], 1)
                root(2)

            def root(n):
                act.wait_ge(sem["rs_pre"], c.next("rs_pre"))
                act.activation(RS[:, 0:n], RS[:, 0:n], ACT.Sqrt).then_inc(sem["rs_ready"], 1)

            def features_scaled(hi):
                for g in range(KT // 2):
                    act.wait_ge(sem["tf_ready"], c.next("tf_ready"))
                    act.activation(hi[:, 2 * g:2 * g + 2, :].rearrange("p k n -> p (k n)"), TF[:, g % 2, :],
                                   ACT.Copy).then_inc(sem["hi_feat"], 1)

            def feature_hi(dst):
                act.wait_ge(sem["tp_ready"], c.next("tp_ready"))
                bank = e.bank()
                act.activation(dst, bank[:, :].rearrange("p (k n) -> p k n", n=T), ACT.Copy).then_inc(sem["hi_feat"], 1)

            def features_plain(hi):
                for g in range(KT // 2):
                    feature_hi(hi[:, 2 * g:2 * g + 2, :])

            def swiglu():
                squares(X, XN)
                features_scaled(HA_hi)

                def gate(b):
                    act.wait_ge(sem["unit_done"], e.reached())
                    acc = e.pair()
                    act.activation(HID[:, b % 2, :, :], acc[:, :, 0:256], ACT.Silu).then_inc(sem["sil_ready"], 1)

                e.skip_turns(4)
                gate(0)
                split(2)
                with e.loop(5, {"land0": 32, "land1": 32, "tp_ready": 2}) as i:
                    for b in (1, 2):
                        gate(b)
                        feature_hi(FT_hi[:, bass.ds(i * 4 + 2 * (b - 1), 2), :])
                        split(2)
                feature_hi(FT_hi[:, 20:22, :])
                split(11)
                e.skip(11, 2)

            def evacuate(dst, name, func=ACT.Copy, width=512):
                act.wait_ge(sem["unit_done"], e.reached())
                acc = e.pair()
                act.activation(dst, acc[:, :, 0:width], func).then_inc(sem[name], 1)
                act.drain().then_inc(e.acc_free(), 1)
                split(2)

            def cols(t, j):
                return t[:, :, 512 * j:512 * j + 512]

            def mixer(l):
                squares(X, XN)
                features_scaled(HA_hi)
                e.skip_turns(4)
                for n, dst in enumerate((R, K, V)):
                    for j in range(2):
                        evacuate(cols(dst, j), "p_ready")
                w = SHIFT[l] - 3 * D
                evacuate(LOR[:, :, 0:w], "p_ready", width=w)
                act.wait_ge(sem["mix_done"], c.next("mix_done", 7))
                act.activation(LOR[:, :, 0:LORA], LOR[:, :, 0:LORA], ACT.Tanh).then_inc(sem["lora_tanh"], 1)
                act.wait_ge(sem["tp_ready"], c.next("tp_ready"))
                bank = e.bank()
                last = act.activation(LORT[:, 0:T], bank[:, 0:T], ACT.Copy)
                if l:
                    last = act.activation(LORT[0:MV, T:2 * T], bank[0:MV, T:2 * T], ACT.Copy)
                last.then_inc(sem["lora_tr"], 1)
                act.drain().then_inc(e.tp_free(), 1)
                for src, name in ([(KK, "vsig_ready")] if l else []) + [(T1, "sig_ready"), (AA, "asig_ready")]:
                    for t in range(NT):
                        act.wait_ge(sem["pre_ready"], c.next("pre_ready"))
                        act.activation(src[:, t, :], src[:, t, :], ACT.Sigmoid).then_inc(sem[name], 1)
                        c.next("acc_ready")
                        e.b += 1
                root(32)
                n = 0
                for t in range(NT):
                    for signs in ((1.0,), (1.0, -1.0)):
                        act.wait_ge(sem["acc_ready"], c.next("acc_ready"))
                        acc = e.pair()
                        for sign in signs:
                            act.wait_ge(sem["exp_used"], c.next("exp_used"))
                            act.activation(T2[:, n % 2, :], acc[:, :, :].rearrange("p t n -> p (t n)"), ACT.Exp,
                                           scale=sign).then_inc(sem["exp_ready"], 1)
                            n += 1
                        act.drain().then_inc(e.acc_free(), 1)
                act.wait_ge(sem["gam_ready"], c.next("gam_ready"))
                act.activation(GAM[:, :], M[0][:, 0:32], ACT.Exp)
                phase()
                for g in range(2):
                    for t in range(NT):
                        for p in range(4):
                            act.wait_ge(sem["tp_ready"], c.next("tp_ready"))
                            bank = e.bank()
                            act.activation(ARBK[:, p, :, :].rearrange("p a n -> p (a n)"), bank[:, :],
                                           ACT.Copy).then_inc(sem["arbk_ready"], 1)
                            act.drain().then_inc(e.tp_free(), 1)
                        for p in range(4):
                            act.wait_ge(sem["mv_ready"], c.next("mv_ready"))
                            act.activation(MVY[:, p, :], A4[p][:, 0:256], ACT.Copy).then_inc(sem["mv_copied"], 1)
                        for ch in range(2):
                            rows = slice(CHUNK * ch, CHUNK * ch + CHUNK)
                            for p in range(4):
                                act.wait_ge(sem["uu_ready"], c.next("uu_ready"))
                                act.activation(U[rows, p, :], B4[p][rows, 0:P], ACT.Copy).then_inc(sem["u_copied"], 1)
                phase()
                root(32)
                act.wait_ge(sem["gn_done"], c.next("gn_done"))
                for j in range(2):
                    evacuate(cols(VA, j), "gelu_ready", ACT.Gelu_apprx_tanh)
                squares(VA, SQ)
                for j in range(2):
                    evacuate(cols(UA, j), "gelu_ready", ACT.Gelu_apprx_tanh)
                e.b += 2
                c.next("acc_ready", 2)
                for j in range(2):
                    evacuate(cols(GATE, j), "gate_ready", ACT.Sigmoid)
                features_plain(HB_hi)
                for j in range(2):
                    e.skip(2, 1)
                    split(2)
                for j in range(2):
                    act.wait_ge(sem["merge_done"], c.next("merge_done"))
                    evacuate(cols(GATE, j), "gate_ready", ACT.Sigmoid)
                features_plain(HB_hi)
                for j in range(2):
                    e.skip(2, 1)
                    split(2)
                features_plain(HA_hi)
                for j in range(2):
                    e.skip(2, 1)
                    split(2)

            def modulation():
                act.wait_ge(sem["cc_land"], c.next("cc_land", 16))
                act.activation(ST[:, 0:16], ST[:, 16:32], ACT.Silu)
                act.drain()
                act.activation(HA_hi[:, :, 0:P].rearrange("p k (s n) -> p k s n", s=2),
                               ST[:, 0:16].rearrange("p (k s) -> p k s", s=2).unsqueeze(3).broadcast_to([P, KT, 2, 64]),
                               ACT.Copy).then_inc(sem["cc_hi"], 1)
                for l in range(2):
                    for j in range(12):
                        e.skip(2, 1)
                        split(2)
                e.skip_turns(16)

            def project(l, s):
                for n in range(l * s, 3):
                    for j in range(2):
                        if n == 2:
                            act.wait_ge(sem["unit_done"], e.reached())
                            acc = e.pair()
                            act.activation(VV[:, 2 * s:2 * s + 2, 512 * j:512 * j + 512], acc[:, :, :], ACT.Copy)
                            act.drain().then_inc(e.acc_free(), 1)
                            split(2)
                        elif s:
                            act.wait_ge(sem["unit_done"], e.reached())
                            acc = e.pair()
                            act.activation(cols(XN, j), acc[:, :, :], ACT.Copy)
                            act.drain().then_inc(e.acc_free(), 1)
                            if j:
                                act.drain().then_inc(sem["q_ready"], 1)
                            split(2)
                        else:
                            e.skip(2, 1)
                            split(2)
                    for g in range(KT // 2 if n < 2 else 0):
                        act.wait_ge(sem["tp_ready"], c.next("tp_ready"))
                        bank = e.bank()
                        dst = (QTC if s else QTX)[:, 2 * g:2 * g + 2, :] if n == 0 else \
                            KTT[:, 2 * g:2 * g + 2, T * s:T * s + T]
                        act.activation(dst, bank[:, :].rearrange("p (k n) -> p k n", n=T), ACT.Copy)
                        act.drain().then_inc(e.tp_free(), 1)

            def attend(l, s):
                nk = 4 if s == 0 else 2
                at = 0
                for n in range(17):
                    if n < 16:
                        st0 = 8 * (n % 2)
                        for hb in range(2):
                            act.wait_ge(sem["max_ready"], c.next("max_ready"))
                            src = A4[2 * (n % 2) + hb][:, 0:nk * P] if l == 0 else SC[:, hb, :]
                            act.activation(PR[:, n % 2, hb, 0:nk * P], src, ACT.Exp,
                                           bias=ST[:, st0 + 2 + hb:st0 + 3 + hb], scale=SCALE if l == 0 else 1.0,
                                           accum_out=ST[:, st0 + 4 + hb:st0 + 5 + hb]).then_inc(sem["prob_ready"], 1)
                            if l == 0:
                                act.drain().then_inc(sem["sc_free"], 1)
                    if n:
                        m = n - 1
                        q, hp = m // 8, m % 8
                        heads_ = 1 if l == 0 else 2
                        for hb in range(heads_):
                            act.wait_ge(sem["tp_ready"], c.next("tp_ready"))
                            bank = e.bank()
                            act.activation(AT[:, at % 2, 0:nk * P], bank[:, 0:nk * P], ACT.Copy).then_inc(sem["at_ready"], 1)
                            act.drain().then_inc(e.tp_free(), 1)
                            at += 1
                        w = P // heads_
                        act.wait_ge(sem["o_ready"], c.next("o_ready"))
                        for hb in range(heads_):
                            dst = XN[:, q, P * hp + w * hb:P * hp + w * hb + w]
                            src = M[m % 2][:, w * hb:w * hb + w]
                            if l == 0:
                                act.activation(dst, src, ACT.Copy).then_inc(sem["o_copied"], 1)
                            else:
                                k = 8 * (m % 2) + 6 + hb
                                act.activation(dst, src, ACT.Identity, scale=ST[:, k:k + 1]).then_inc(sem["o_copied"], 1)
                        act.drain().then_inc(sem["o_free"], 1)
                if l == 0:
                    root(16)
                features_plain(HA_hi)
                for j in range(2):
                    e.skip(2, 1)
                    split(2)

            def conv_ffn(src):
                squares(src, XN)
                features_scaled(HA_hi)
                e.skip_turns(4)
                if src is X:
                    act.wait_ge(sem["cw_land"], c.next("cw_land", 16))

                def up(b):
                    act.wait_ge(sem["unit_done"], e.reached())
                    acc = e.pair()
                    act.activation(US[:, b % 2, :, :], acc[:, :, :], ACT.Copy).then_inc(sem["u_copy"], 1)
                    act.drain().then_inc(e.acc_free(), 1)

                def conv(b, dyn=None):
                    for h in range(2):
                        act.wait_ge(sem["tp_ready"], c.next("tp_ready"))
                        bank = e.bank()
                        for k in range(2):
                            col = tile(b, h, k, dyn)
                            last = act.activation(CV[:, b % 2, 2 * h + k, :], bank[:, T * k:T * k + T], ACT.Identity,
                                                  scale=CW[:, 1, col], bias=CW[:, 3, col])
                        last.then_inc(sem["cv_ready"], 1)

                def gate(b, dst):
                    act.wait_ge(sem["cv_conv"], c.next("cv_conv"))
                    g = CV[:, b % 2, 2:4, :]
                    act.activation(g, g, ACT.Silu).then_inc(sem["sg_ready"], 1)
                    act.wait_ge(sem["hv_ready"], c.next("hv_ready"))
                    act.activation(dst, HV[:, b % 2, :, :], ACT.Copy).then_inc(sem["hi_feat"], 1)

                up(0)
                split(2)
                with e.loop(5, {"land0": 32, "land1": 32, "tp_ready": 4, "cv_conv": 2, "hv_ready": 2}) as i:
                    for b in (1, 2):
                        up(b)
                        conv(b - 1, i)
                        split(2)
                        gate(b - 1, FT_hi[:, bass.ds(i * 4 + 2 * (b - 1), 2), :])
                conv(10)
                gate(10, FT_hi[:, 20:22, :])
                split(11)
                e.skip(11, 2)

            act.wait_ge(sem["const_land"], c.next("const_land", 32))
            split(SPLIT)
            for l in range(2):
                swiglu()
                mixer(l)
                swiglu()
            squares(X, XN)
            phase()
            modulation()
            phase()
            for l in range(2):
                for s in range(2):
                    squares(XC if s else X, XN)
                    features_scaled((HB_hi, HA_hi)[1 - s])
                    e.skip_turns(4)
                    project(l, s)
                phase()
                if l == 0:
                    act.wait_ge(sem["lam_ready"], c.next("lam_ready"))
                    act.activation(ST[:, 20:22], ST[:, 18:20], ACT.Exp).then_inc(sem["lam_exp"], 1)
                for s in range(2 - l):
                    attend(l, s)
                    phase()
                for s in range(2 - l):
                    conv_ffn(XC if s else X)
                    phase()
            squares(X, XN)

        @block.vector
        def _(dve):
            e = Side(dve)
            c = e.c

            def phase():
                dve.drain().then_inc(sem["phase_done"], 1)
                dve.wait_ge(sem["phase_done"], c.next("phase_done", 4))

            def split(n):
                for _ in range(min(n, NUNITS - e.u)):
                    slot, s = e.u % RAW, e.u % SPLIT
                    dve.wait_ge(sem["hi_ready"], c.next("hi_ready"))
                    dve.tensor_tensor(w_lo[:, s, :], raw[:, slot, :], w_hi[:, s, :].bitcast(F32),
                                      ALU.subtract).then_inc(sem["lo_ready"], 1)
                    e.u += 1

            tt, ts, stt = dve.tensor_tensor, dve.tensor_scalar, dve.scalar_tensor_tensor
            vec = {"n": 0}

            def vector():
                s = vec["n"] % 2
                vec["n"] += 1
                dve.wait_ge(sem[f"bc{s}"], c.next(f"bc{s}", 16))
                return BC[:, s, :]

            def cols(t, j):
                return t[:, :, 512 * j:512 * j + 512]

            def both(v):
                return v.unsqueeze(1).broadcast_to([P, NT, D])

            def per_head(v, n, d):
                return v.unsqueeze(2).broadcast_to([P, n, d])

            def rates(n, width=1.0, eps=0.0, floor=None):
                if floor is None:
                    ts(RS[:, 0:n], SS[:, 0:n], 1.0 / width, eps, ALU.mult, ALU.add)
                else:
                    ts(RS[:, 0:n], SS[:, 0:n], floor, None, ALU.max)
                dve.drain()
                dve.reciprocal(RS[:, 0:n], RS[:, 0:n]).then_inc(sem["rs_pre"], 1)

            def factors(src, dst):
                dve.wait_ge(sem["ss_ready"], c.next("ss_ready"))
                rates(2, D, NORM_EPS)
                dve.wait_ge(sem["rs_ready"], c.next("rs_ready"))
                for t in range(NT):
                    last = ts(dst[:, t, :], src[:, t, :], RS[:, t:t + 1], None, ALU.mult)
                last.then_inc(sem["xn_ready"], 1)

            def feature_lo(dst, dst_hi):
                c.next("tp_ready")
                dve.wait_ge(sem["hi_feat"], c.next("hi_feat"))
                bank = e.bank()
                tt(dst, bank[:, :].rearrange("p (k n) -> p k n", n=T), dst_hi.bitcast(F32), ALU.subtract) \
                    .then_inc(sem["feat_ready"], 1)
                dve.drain().then_inc(e.tp_free(), 1)

            def features_plain(hi, lo):
                for g in range(KT // 2):
                    feature_lo(lo[:, 2 * g:2 * g + 2, :], hi[:, 2 * g:2 * g + 2, :])

            def features_scaled(hi, lo, scale, shift=None):
                def low(g):
                    dve.wait_ge(sem["hi_feat"], c.next("hi_feat"))
                    tt(lo[:, 2 * g:2 * g + 2, :].rearrange("p k n -> p (k n)"), TF[:, g % 2, :],
                       hi[:, 2 * g:2 * g + 2, :].rearrange("p k n -> p (k n)").bitcast(F32), ALU.subtract) \
                        .then_inc(sem["feat_ready"], 1)

                for g in range(KT // 2):
                    dve.wait_ge(sem["tp_ready"], c.next("tp_ready"))
                    bank = e.bank()
                    for k in range(2):
                        f = 2 * g + k
                        last = ts(TF[:, g % 2, T * k:T * k + T], bank[:, T * k:T * k + T], scale(f),
                                  None if shift is None else shift(f), ALU.mult,
                                  ALU.bypass if shift is None else ALU.add)
                    last.then_inc(sem["tf_ready"], 1)
                    dve.drain().then_inc(e.tp_free(), 1)
                    if g:
                        low(g - 1)
                        dve.drain()
                low(KT // 2 - 1)

            def norm_features(src, gain):
                dve.drain().then_inc(sem["res_ready"], 1)
                factors(src, XN)
                features_scaled(HA_hi, HA_lo, lambda f: COL[:, gain + f:gain + f + 1])

            def swiglu(gain):
                norm_features(X, gain)

                def hidden(b):
                    dve.wait_ge(sem["unit_done"], e.reached())
                    acc = e.pair()
                    dve.wait_ge(sem["sil_ready"], c.next("sil_ready"))
                    h = HID[:, b % 2, :, :]
                    tt(h, acc[:, :, 256:512], h, ALU.mult).then_inc(sem["hid_ready"], 1)
                    dve.drain().then_inc(e.acc_free(), 1)

                hidden(0)
                split(2)
                with e.loop(5, {"hi_ready": 4, "sil_ready": 2, "hi_feat": 2, "tp_ready": 2}) as i:
                    for b in (1, 2):
                        hidden(b)
                        f = bass.ds(i * 4 + 2 * (b - 1), 2)
                        feature_lo(FT_lo[:, f, :], FT_hi[:, f, :])
                        split(2)
                feature_lo(FT_lo[:, 20:22, :], FT_hi[:, 20:22, :])
                split(11)
                e.pos += 11
                for n in range(2):
                    x = cols(X, n)
                    dve.wait_ge(sem["unit_done"], e.reached(0))
                    acc = e.pair()
                    stt(x, acc[:, :, :], 0.5, x, ALU.mult, ALU.add).then_inc(e.acc_free(), 1)

            def to_feat(v):
                return v.rearrange("p t n -> p (t n)")

            def prepare(l):
                for dst, name in ([(KK, 0)] if l else []) + [(T1, 1), (AA, 2)]:
                    v = vector()
                    for t in range(NT):
                        dve.wait_ge(sem["acc_ready"], c.next("acc_ready"))
                        acc = e.pair()
                        tt(dst[:, t, :], to_feat(acc[:, :, :]), v, ALU.add).then_inc(sem["pre_ready"], 1)
                        dve.drain().then_inc(e.acc_free(), 1)
                    dve.drain().then_inc(sem["bc_free"], 1)
                if l:
                    dve.wait_ge(sem["vf_land"], c.next("vf_land", 16))
                    dve.wait_ge(sem["vsig_ready"], c.next("vsig_ready", 2))
                    tt(whole(VF), whole(VF), whole(V), ALU.subtract)
                    dve.drain()
                    tt(whole(VF), whole(VF), whole(KK), ALU.mult)
                    dve.drain()
                    tt(whole(V), whole(V), whole(VF), ALU.add)
                    dve.drain()
                else:
                    dve.drain().then_inc(sem["v_final"], 1)
                v = vector()
                tt(KK[:, :, :], K[:, :, :], both(v), ALU.mult)
                dve.drain().then_inc(sem["bc_free"], 1)
                tt(whole(T2), whole(KK), whole(KK), ALU.mult)
                dve.drain()
                dve.tensor_reduce(SS[:, :], heads(T2), AX.X, ALU.add)
                dve.drain()
                rates(32, floor=1e-24)
                v = vector()
                dve.wait_ge(sem["asig_ready"], c.next("asig_ready", 2))
                stt(T2[:, :, :], AA[:, :, :], -1.0, both(v), ALU.add, ALU.mult)
                dve.drain().then_inc(sem["bc_free"], 1)
                stt(whole(K), whole(T2), 1.0, whole(K), ALU.add, ALU.mult)
                dve.wait_ge(sem["rs_ready"], c.next("rs_ready"))
                tt(heads(KK), heads(KK), per_head(RS[:, :], 32, HD), ALU.mult)
                v = vector()
                dve.drain()
                tt(T2[:, :, :], R[:, :, :], both(v), ALU.mult)
                dve.drain().then_inc(sem["bc_free"], 1)
                tt(whole(AA), whole(AA), whole(KK), ALU.mult)
                tt(whole(T2), whole(T2), whole(K), ALU.mult)
                dve.drain()
                dve.tensor_reduce(BN[:, :, :].rearrange("p t h -> p (t h)"), heads(T2), AX.X, ALU.add)
                dve.drain().then_inc(sem["exp_used"], 2)
                n = 0

                def factor():
                    nonlocal n
                    dve.wait_ge(sem["exp_ready"], c.next("exp_ready"))
                    n += 1
                    return T2[:, (n - 1) % 2, :]

                for t in range(NT):
                    w = factor()
                    stt(KK[:, t, :], KK[:, t, :], -1.0, w, ALU.mult, ALU.mult).then_inc(sem["exp_used"], 1)
                    w = factor()
                    last = tt(R[:, t, :], R[:, t, :], w, ALU.mult)
                    if t == 0:
                        last.then_inc(sem["exp_used"], 1)
                    w = factor()
                    tt(AA[:, t, :], AA[:, t, :], w, ALU.mult)
                    last = tt(K[:, t, :], K[:, t, :], w, ALU.mult)
                    if t == 0:
                        last.then_inc(sem["exp_used"], 1)

            def mask(col, n):
                return K_[:, col:col + P].unsqueeze(1).broadcast_to([P, n, P])

            def wkv(g, t):
                if t == 0:
                    dve.drain()
                    dve.memset(S[:, :, :], 0.0)
                    dve.drain().then_inc(sem["s_zero"], 1)
                for n in range(8):
                    dve.wait_ge(sem["gram_ready"], c.next("gram_ready"))
                    tt(LG[:, n, :].rearrange("p (a n) -> p a n", a=2), M[n % 2][:, :].rearrange("p (a n) -> p a n", a=2),
                       K_[:, C_GRAM:C_GRAM + 256].unsqueeze(1).broadcast_to([P, 2, 256]), ALU.mult) \
                        .then_inc(sem["lg_ready"], 1)
                e.tp += 4
                c.next("tp_ready", 4)
                dve.drain()
                for p in range(4):
                    dve.wait_ge(sem["t_ready"], c.next("t_ready"))
                    tt(XX[:, p, :, 0, :], A4[p][:, 0:256].rearrange("p (h n) -> p h n", h=2), mask(C_LEVEL, 2), ALU.mult)
                    tt(XX[:, p, :, 1, :], LG[:, 2 * p:2 * p + 2, 0:P], mask(C_LEVEL0T, 2), ALU.mult)
                    dve.drain()
                    x = XX[:, p, :, :, :].rearrange("p h a n -> p (h a) n")
                    tt(x, x, mask(C_ID, 4), ALU.add).then_inc(sem["x_ready"], 1)
                for j in range(1, 6):
                    for p in range(4):
                        dve.wait_ge(sem["t_ready"], c.next("t_ready"))
                        tt(TM[:, p, :].rearrange("p (h n) -> p h n", h=2),
                           A4[p][:, 0:256].rearrange("p (h n) -> p h n", h=2), mask(C_LEVEL + P * j, 2), ALU.mult) \
                            .then_inc(sem["t_masked"], 1)
                    for p in range(4):
                        dve.wait_ge(sem["u_ready"], c.next("u_ready"))
                        if j < 5:
                            x = XX[:, p, :, :, :].rearrange("p h a n -> p (h a n)")
                            tt(x, x, B4[p], ALU.add).then_inc(sem["x_ready"], 1)
                        else:
                            x = XX[:, p, :, 1, :]
                            tt(x, x, B4[p].rearrange("p (h a n) -> p h a n", h=2, a=2)[:, :, 1, :], ALU.add) \
                                .then_inc(sem["x_ready"], 1)
                for ch in range(2):
                    rows = slice(CHUNK * ch, CHUNK * ch + CHUNK)
                    for p in range(4):
                        dve.wait_ge(sem["pp_ready"], c.next("pp_ready"))
                        tt(PM[rows, p, :], A4[p][rows, 0:P], MVY[rows, p, 0:P], ALU.add).then_inc(sem["pm_ready"], 1)
                    for p in range(4):
                        q = 4 * g + p
                        dve.wait_ge(sem["sy_ready"], c.next("sy_ready"))
                        gam = GAM[:, 4 * q + 2 * t + ch:4 * q + 2 * t + ch + 1]
                        stt(SU[:, p, :], B4[p][:, P:2 * P], gam, K_[:, C_BD:C_BD + P], ALU.mult, ALU.mult)
                        tt(R[rows, t, P * q:P * q + P], A4[p][rows, P:2 * P], MVY[rows, p, P:2 * P], ALU.add) \
                            .then_inc(sem["y_done"], 1)
                        dve.drain()
                        stt(S[:, p, :], S[:, p, :], gam, SU[:, p, :], ALU.mult, ALU.add).then_inc(sem["s_done"], 1)

            def group_norm():
                dve.tensor_reduce(SS[:, :], heads(R), AX.X, ALU.add)
                dve.drain()
                ts(RS[:, :], SS[:, :], -1.0 / HD, None, ALU.mult)
                dve.drain()
                tt(heads(R), heads(R), per_head(RS[:, :], 32, HD), ALU.add)
                dve.drain()
                tt(whole(T1), whole(R), whole(R), ALU.mult)
                dve.drain()
                dve.tensor_reduce(SS[:, :], heads(T1), AX.X, ALU.add)
                dve.drain()
                rates(32, HD, GN_EPS)
                tt(heads(T1), heads(V), per_head(BN[:, :, :].rearrange("p t h -> p (t h)"), 32, HD), ALU.mult)
                dve.wait_ge(sem["rs_ready"], c.next("rs_ready"))
                tt(heads(R), heads(R), per_head(RS[:, :], 32, HD), ALU.mult)
                v = vector()
                dve.drain()
                tt(R[:, :, :], R[:, :, :], both(v), ALU.mult)
                dve.drain().then_inc(sem["bc_free"], 1)
                v = vector()
                tt(R[:, :, :], R[:, :, :], both(v), ALU.add)
                dve.drain().then_inc(sem["bc_free"], 1)
                tt(whole(R), whole(R), whole(T1), ALU.add)
                dve.drain().then_inc(sem["gn_done"], 1)

            def mixer(l):
                norm_features(X, G_MIX + 8 * l)
                dve.wait_ge(sem["mu_land"], c.next("mu_land", 16))
                for n in range(7):
                    e.skip(2, 1)
                    split(2)
                    w = 512 if n < 6 else SHIFT[l] - 3 * D
                    p_ = cols((R, K, V)[n // 2], n % 2) if n < 6 else LOR[:, :, 0:w]
                    prev, dif = PREV[:, n % 2, :, 0:w], DIF[:, :, 0:w]
                    dve.wait_ge(sem[f"shift{n % 2}"], c.next(f"shift{n % 2}", 48))
                    tt(dif, prev, p_, ALU.subtract)
                    dve.drain()
                    tt(dif, dif, MU[:, 512 * n:512 * n + w].unsqueeze(1).broadcast_to([P, NT, w]), ALU.mult)
                    dve.drain()
                    tt(p_, p_, dif, ALU.add)
                    dve.drain().then_inc(sem["mix_done"], 1)
                e.skip_turns(1)
                prepare(l)
                e.b += 4
                c.next("acc_ready", 4)
                phase()
                for g in range(2):
                    for t in range(NT):
                        wkv(g, t)
                phase()
                group_norm()
                dve.wait_ge(sem["wst_land"], c.next("wst_land", 16))
                tt(WST[:, :, :], WST[:, :, :], mask(C_TRIU, 8), ALU.mult)
                for j in range(2):
                    e.skip(2, 1)
                    split(2)
                dve.wait_ge(sem["gelu_ready"], c.next("gelu_ready", 2))
                dve.tensor_reduce(ST[:, 0:2], VA[:, :, :], AX.X, ALU.add)
                dve.drain()
                ts(ST[:, 2:4], ST[:, 0:2], -1.0 / D, None, ALU.mult)
                dve.drain()
                for t in range(NT):
                    ts(VA[:, t, :], VA[:, t, :], ST[:, 2 + t:3 + t], None, ALU.add)
                dve.drain().then_inc(sem["res_ready"], 1)
                v = vector()
                dve.wait_ge(sem["ss_ready"], c.next("ss_ready"))
                rates(2, D, LN_EPS)
                dve.wait_ge(sem["rs_ready"], c.next("rs_ready"))
                for t in range(NT):
                    stt(VA[:, t, :], VA[:, t, :], RS[:, t:t + 1], v, ALU.mult, ALU.mult)
                dve.drain().then_inc(sem["bc_free"], 1)
                v = vector()
                tt(VA[:, :, :], VA[:, :, :], both(v), ALU.add)
                dve.drain().then_inc(sem["bc_free"], 1)
                dve.drain().then_inc(sem["va_ready"], 1)
                for j in range(2):
                    e.skip(2, 1)
                    split(2)
                dve.wait_ge(sem["gelu_ready"], c.next("gelu_ready", 2))
                bs = COL[:, G_BS + 8 * l:G_BS + 8 * l + 8]
                for t in range(NT):
                    dve.wait_ge(sem["acc_ready"], c.next("acc_ready"))
                    acc = e.pair()
                    tt(SQ[:, t, :].rearrange("p (g d) -> p g d", g=8),
                       to_feat(acc[:, :, :]).rearrange("p (g d) -> p g d", g=8), per_head(bs, 8, P), ALU.add)
                    dve.drain().then_inc(e.acc_free(), 1)
                    tt(VA[:, t, :], SQ[:, t, :], UA[:, t, :], ALU.mult)
                dve.drain().then_inc(sem["xn_ready"], 1)
                for j in range(2):
                    e.skip(2, 1)
                    split(2)
                features_plain(HB_hi, HB_lo)
                dve.wait_ge(sem["gate_ready"], c.next("gate_ready", 2))
                for j in range(2):
                    dve.wait_ge(sem["unit_done"], e.reached())
                    acc = e.pair()
                    tt(cols(MERG, j), acc[:, :, :], cols(GATE, j), ALU.mult).then_inc(e.acc_free(), 1)
                    dve.drain().then_inc(sem["merge_done"], 1)
                    split(2)
                for j in range(2):
                    e.skip(2, 1)
                    split(2)
                dve.drain().then_inc(sem["xn_ready"], 1)
                features_plain(HB_hi, HB_lo)
                dve.wait_ge(sem["gate_ready"], c.next("gate_ready", 2))
                for j in range(2):
                    dve.wait_ge(sem["unit_done"], e.reached())
                    acc = e.pair()
                    tt(cols(SQ, j), acc[:, :, :], cols(GATE, j), ALU.mult).then_inc(e.acc_free(), 1)
                    dve.drain()
                    tt(cols(MERG, j), cols(MERG, j), cols(SQ, j), ALU.add)
                    if j:
                        dve.drain().then_inc(sem["xn_ready"], 1)
                    split(2)
                features_plain(HA_hi, HA_lo)
                for j in range(2):
                    dve.wait_ge(sem["unit_done"], e.reached())
                    acc = e.pair()
                    x = cols(X, j)
                    tt(x, acc[:, :, :], x, ALU.add).then_inc(e.acc_free(), 1)
                    split(2)

            def scaled_rows(v, name):
                dve.drain().then_inc(sem["res_ready"], 1)
                dve.wait_ge(sem["ss_ready"], c.next("ss_ready"))
                rates(2, D, NORM_EPS)
                dve.wait_ge(sem["rs_ready"], c.next("rs_ready"))
                for t in range(NT):
                    stt((X if name is None else XN)[:, t, :], X[:, t, :], RS[:, t:t + 1], v, ALU.mult, ALU.mult)

            def modulation():
                dve.wait_ge(sem["cc_hi"], c.next("cc_hi"))
                tt(HA_lo[:, :, 0:P].rearrange("p k (s n) -> p k s n", s=2),
                   ST[:, 0:16].rearrange("p (k s) -> p k s", s=2).unsqueeze(3).broadcast_to([P, KT, 2, 64]),
                   HA_hi[:, :, 0:P].rearrange("p k (s n) -> p k s n", s=2).bitcast(F32), ALU.subtract) \
                    .then_inc(sem["cc_ready"], 1)
                for l in range(2):
                    for m in range(6):
                        if (l, m) in ((0, 4), (1, 1), (1, 4)):
                            dve.wait_ge(sem["mod_stored"], c.next("mod_stored", 32))
                        bias = vector()
                        for j in range(2):
                            dve.wait_ge(sem["unit_done"], e.reached())
                            acc = e.pair()
                            tt(XN[:, m % 2, 512 * j:512 * j + 512], acc[:, 0, :], bias[:, 512 * j:512 * j + 512], ALU.add) \
                                .then_inc(sem["modg_ready" if m in (2, 5) else "mod_ready"], 1)
                            dve.drain().then_inc(e.acc_free(), 1)
                            split(2)
                        dve.drain().then_inc(sem["bc_free"], 1)
                        if m in (2, 5):
                            continue
                        for h in range(2):
                            dve.wait_ge(sem["tp_ready"], c.next("tp_ready"))
                            bank = e.bank()
                            dve.tensor_copy(MODC[:, l, (0, 1, None, 2, 3)[m], 4 * h:4 * h + 4, :],
                                            bank[:, :].rearrange("p (k s n) -> p k s n", k=4, s=2)[:, :, :, 0])
                            dve.drain().then_inc(e.tp_free(), 1)
                for l in range(2):
                    for w, gain in enumerate((G_NMIX, G_NFFN)):
                        g = COL[:, gain + 8 * l:gain + 8 * l + 8]
                        stt(MODS[:, l, w, :, :], MODC[:, l, 2 * w + 1, :, :], 1.0, per_head(g, KT, 2), ALU.add, ALU.mult)
                dve.drain()

            def modulated(src, l, w, s):
                dve.drain().then_inc(sem["res_ready"], 1)
                factors(src, XN)
                hi, lo = (HB_hi, HB_lo) if s and w == 0 else (HA_hi, HA_lo)
                features_scaled(hi, lo, lambda f: MODS[:, l, w, f, s:s + 1], lambda f: MODC[:, l, 2 * w, f, s:s + 1])

            def rotate(acc, j):
                for t in range(NT):
                    src = acc[:, t, :]
                    x = XN[:, t, 512 * j:512 * j + 512]
                    h3 = "p (h x) -> p h x"
                    tt(x.rearrange(h3, x=HD), src.rearrange(h3, x=HD),
                       ROPE[:, 0, t, :].unsqueeze(1).broadcast_to([P, 8, HD]), ALU.mult)
                    for b in range(2):
                        v5 = "p (h a b i) -> p h a b i"
                        tt(QK[:, :].rearrange(v5, a=2, b=2, i=16)[:, :, :, b, :],
                           src.rearrange(v5, a=2, b=2, i=16)[:, :, :, 1 - b, :],
                           ROPE[:, 1, t, :].rearrange("p (a b i) -> p a b i", a=2, b=2)[:, :, b, :].unsqueeze(1)
                           .broadcast_to([P, 8, 2, 16]), ALU.mult)
                    dve.drain()
                    tt(x, x, QK[:, :], ALU.add)
                    dve.drain()

            def project(l, s):
                for n in range(l * s, 3):
                    for j in range(2):
                        if n == 2 or s:
                            e.skip(2, 1)
                        elif l == 1:
                            dve.wait_ge(sem["unit_done"], e.reached())
                            acc = e.pair()
                            dve.tensor_copy(cols(XN, j), acc[:, :, :])
                            dve.drain().then_inc(e.acc_free(), 1)
                            if j:
                                dve.drain().then_inc(sem["q_ready"], 1)
                        else:
                            dve.wait_ge(sem["unit_done"], e.reached())
                            acc = e.pair()
                            rotate(acc, j)
                            dve.drain().then_inc(e.acc_free(), 1)
                            if j:
                                dve.drain().then_inc(sem["q_ready"], 1)
                        split(2)
                    if n < 2:
                        e.skip_turns(4)

            def attend(l, s):
                nk = 4 if s == 0 else 2
                w = nk * P

                def peak(n):
                    st0 = 8 * (n % 2)
                    for hb in range(2):
                        dve.wait_ge(sem["sc_ready"], c.next("sc_ready"))
                        src = A4[2 * (n % 2) + hb][:, 0:w]
                        if l:
                            if hb == 0:
                                dve.wait_ge(sem["bias_ready"], c.next("bias_ready"))
                            stt(SC[:, hb, 0:T], src[:, 0:T], SCALE, BIAS[:, n % 2, hb, :], ALU.mult, ALU.add)
                            ts(SC[:, hb, T:2 * T], src[:, T:2 * T], SCALE, None, ALU.mult)
                            dve.drain().then_inc(sem["sc_free"], 1)
                            if hb:
                                dve.drain().then_inc(sem["bias_free"], 1)
                            src = SC[:, hb, :]
                        dve.tensor_reduce(ST[:, st0 + hb:st0 + hb + 1], src, AX.X, ALU.max)
                        dve.drain()
                        ts(ST[:, st0 + 2 + hb:st0 + 3 + hb], ST[:, st0 + hb:st0 + hb + 1], -1.0 if l else -SCALE, None,
                           ALU.mult).then_inc(sem["max_ready"], 1)

                def mix(n):
                    st0 = 8 * (n % 2)
                    dve.wait_ge(sem["prob_ready"], c.next("prob_ready", 2))
                    dve.reciprocal(ST[:, st0 + 6:st0 + 8], ST[:, st0 + 4:st0 + 6])
                    if l == 0:
                        dve.drain()
                        ts(ST[:, st0 + 7:st0 + 8], ST[:, st0 + 7:st0 + 8], ST[:, 16:17], None, ALU.mult)
                        dve.drain()
                        p0, p1 = PR[:, n % 2, 0, 0:w], PR[:, n % 2, 1, 0:w]
                        ts(p1, p1, ST[:, st0 + 7:st0 + 8], None, ALU.mult)
                        dve.drain()
                        stt(p0, p0, ST[:, st0 + 6:st0 + 7], p1, ALU.mult, ALU.subtract)
                    dve.drain().then_inc(sem["mix_ready"], 1)

                peak(0)
                for n in range(16):
                    if l:
                        mix(n)
                        if n < 15:
                            peak(n + 1)
                    else:
                        if n < 15:
                            peak(n + 1)
                        mix(n)
                e.skip_turns(16 if l == 0 else 32)
                dve.wait_ge(sem["o_copied"], c.next("o_copied", 16 if l == 0 else 32))
                if l == 0:
                    tmp = (QTC if s else QTX)[:, :, :].rearrange("p k n -> p (k n)")
                    tt(tmp, whole(XN), whole(XN), ALU.mult)
                    dve.drain()
                    dve.tensor_reduce(SS[:, 0:16], tmp.rearrange("p (h n) -> p h n", n=P), AX.X, ALU.add)
                    dve.drain()
                    rates(16, P, NORM_EPS)
                    dve.wait_ge(sem["rs_ready"], c.next("rs_ready"))
                    y = whole(XN).rearrange("p (h n) -> p h n", n=P)
                    stt(y, y, 1.0 - LAM_INIT, per_head(RS[:, 0:16], 16, P), ALU.mult, ALU.mult)
                    dve.drain()
                    tt(y, y, SUBL[:, :].unsqueeze(1).broadcast_to([P, 16, P]), ALU.mult)
                dve.drain().then_inc(sem["xn_ready"], 1)
                features_plain(HA_hi, HA_lo)
                g = vector()
                dst = XC if s else X
                for j in range(2):
                    dve.wait_ge(sem["unit_done"], e.reached())
                    acc = e.pair()
                    gated(acc, g, j, dst)
                    split(2)
                dve.drain().then_inc(sem["bc_free"], 1)

            def gated(acc, g, j, dst):
                tt(cols(XN, j), acc[:, :, :], g[:, 512 * j:512 * j + 512].unsqueeze(1).broadcast_to([P, NT, 512]),
                   ALU.mult).then_inc(e.acc_free(), 1)
                dve.drain()
                tt(cols(dst, j), cols(dst, j), cols(XN, j), ALU.add)

            def lam_factor():
                dve.wait_ge(sem["lam_land"], c.next("lam_land", 32))
                tt(LAMB[:, 0:2, :], LAMB[:, 0:4:2, :], LAMB[:, 1:4:2, :], ALU.mult)
                dve.drain()
                dve.tensor_reduce(ST[:, 18:20], LAMB[:, 0:2, :], AX.X, ALU.add).then_inc(sem["lam_ready"], 1)
                dve.wait_ge(sem["lam_exp"], c.next("lam_exp"))
                stt(ST[:, 16:17], ST[:, 20:21], LAM_INIT, ST[:, 21:22], ALU.add, ALU.subtract)
                dve.drain()

            def conv_ffn(l, s, src):
                modulated(src, l, 1, s)

                def conv(b, dyn=None):
                    for h in range(2):
                        c.next("tp_ready")
                        dve.wait_ge(sem["cv_ready"], c.next("cv_ready"))
                        bank = e.bank()
                        for k in range(2):
                            col = tile(b, h, k, dyn)
                            y, u = CV[:, b % 2, 2 * h + k, :], bank[:, T * k:T * k + T]
                            stt(y[:, 1:T], u[:, 0:T - 1], CW[:, 0, col], y[:, 1:T], ALU.mult, ALU.add)
                        dve.drain()
                        for k in range(2):
                            col = tile(b, h, k, dyn)
                            y, u = CV[:, b % 2, 2 * h + k, :], bank[:, T * k:T * k + T]
                            stt(y[:, 0:T - 1], u[:, 1:T], CW[:, 2, col], y[:, 0:T - 1], ALU.mult, ALU.add)
                        dve.drain().then_inc(e.tp_free(), 1)
                    dve.drain().then_inc(sem["cv_conv"], 1)

                def gate(b, dst_hi, dst_lo):
                    dve.wait_ge(sem["sg_ready"], c.next("sg_ready"))
                    tt(HV[:, b % 2, :, :], CV[:, b % 2, 0:2, :], CV[:, b % 2, 2:4, :], ALU.mult).then_inc(sem["hv_ready"], 1)
                    dve.wait_ge(sem["hi_feat"], c.next("hi_feat"))
                    tt(dst_lo, HV[:, b % 2, :, :], dst_hi.bitcast(F32), ALU.subtract).then_inc(sem["feat_ready"], 1)

                e.skip(2, 1)
                split(2)
                with e.loop(5, {"hi_ready": 4, "tp_ready": 4, "cv_ready": 4, "sg_ready": 2, "hi_feat": 2}) as i:
                    for b in (1, 2):
                        e.skip(2, 1)
                        conv(b - 1, i)
                        split(2)
                        f = bass.ds(i * 4 + 2 * (b - 1), 2)
                        gate(b - 1, FT_hi[:, f, :], FT_lo[:, f, :])
                conv(10)
                gate(10, FT_hi[:, 20:22, :], FT_lo[:, 20:22, :])
                split(11)
                e.pos += 11
                g = vector()
                for n in range(2):
                    dve.wait_ge(sem["unit_done"], e.reached(0))
                    gated(e.pair(), g, n, src)
                dve.drain().then_inc(sem["bc_free"], 1)

            dve.wait_ge(sem["const_land"], c.next("const_land", 32))
            dve.wait_ge(sem["x_land"], c.next("x_land", 16))
            split(SPLIT)
            for l in range(2):
                swiglu(G_FFN1 + 8 * l)
                mixer(l)
                swiglu(G_FFN2 + 8 * l)
            v = vector()
            scaled_rows(v, None)
            dve.drain().then_inc(sem["bc_free"], 1)
            phase()
            modulation()
            phase()
            dve.wait_ge(sem["ctx_land"], c.next("ctx_land", 16))
            dve.wait_ge(sem["rope_land"], c.next("rope_land", 16))
            for l in range(2):
                for s in range(2):
                    modulated(XC if s else X, l, 0, s)
                    project(l, s)
                phase()
                if l == 0:
                    lam_factor()
                for s in range(2 - l):
                    attend(l, s)
                    phase()
                for s in range(2 - l):
                    if s == 0:
                        dve.wait_ge(sem["cw_land"], c.next("cw_land", 16))
                    conv_ffn(l, s, XC if s else X)
                    phase()
            v = vector()
            scaled_rows(v, "out")
            dve.drain().then_inc(sem["out_ready"], 1)

        @block.gpsimd
        def _(pool):
            c = Counts(pool, sem)

            def phase():
                pool.drain().then_inc(sem["phase_done"], 1)
                pool.wait_ge(sem["phase_done"], c.next("phase_done", 4))

            n_vec = {"n": 0}

            def vector(src):
                s = n_vec["n"] % 2
                n_vec["n"] += 1
                if n_vec["n"] > 2:
                    pool.wait_ge(sem["bc_free"], c.next("bc_free"))
                pool.dma_start(BC[:, s, :], src).then_inc(sem[f"bc{s}"], 16)

            def shifts(l):
                for n in range(7):
                    w = 512 if n < 6 else SHIFT[l] - 3 * D
                    src = (R, K, V)[n // 2][:, :, 512 * (n % 2):512 * (n % 2) + 512] if n < 6 else LOR[:, :, 0:w]
                    dst = PREV[:, n % 2, :, 0:w]
                    pool.wait_ge(sem["p_ready"], c.next("p_ready"))
                    if n >= 2:
                        pool.wait_ge(sem["mix_done"], 7 * l + n - 1)
                    pool.dma_start(dst[1:113], src[0:112]).then_inc(sem[f"shift{n % 2}"], 16)
                    pool.dma_start(dst[113:128], src[112:127]).then_inc(sem[f"shift{n % 2}"], 16)
                    pool.dma_start(dst[0:1, 1, :], src[127:128, 0, :]).then_inc(sem[f"shift{n % 2}"], 16)

            def mixer(l):
                pool.wait_ge(sem["feat_ready"], 46 * l + 15 + 4)
                pool.memset(PREV[0:1, :, 0, :], 0.0).then_inc(sem["zero_ready"], 1)
                pool.wait_ge(sem["zero_ready"], c.next("zero_ready"))
                pool.dma_start(MU[:, 0:SHIFT[l]], mus[l:l + 1, 0:SHIFT[l]].broadcast_to([P, SHIFT[l]])) \
                    .then_inc(sem["mu_land"], 16)
                pool.dma_start(W2A2[:, :], lora_wa[l]).then_inc(sem["param_land"], 16)
                if l:
                    pool.dma_start(V2[:, :], lora_v).then_inc(sem["param_land"], 16)
                order = ([V_V0] if l else []) + [V_W0, V_A0, V_KK, V_KA, V_RK]
                rows = [row(v if v == V_V0 else 10 * l + v) for v in order]
                for r in rows[:2]:
                    vector(r)
                shifts(l)
                pool.wait_ge(sem["mix_done"], c.next("mix_done", 7))
                if l:
                    pool.dma_start(VF[:, :, :], vfirst_scr).then_inc(sem["vf_land"], 16)
                else:
                    pool.wait_ge(sem["v_final"], c.next("v_final"))
                    pool.dma_start(vfirst_scr, V[:, :, :]).then_inc(sem["v_stored"], 16)
                for r in rows[2:]:
                    vector(r)
                if not l:
                    pool.wait_ge(sem["v_stored"], c.next("v_stored", 16))
                phase()
                phase()
                pool.dma_start(WST[:, :, :], wst[l]).then_inc(sem["wst_land"], 16)
                vector(row(10 * l + V_GNG))
                vector(row(10 * l + V_GNB))
                vector(row(10 * l + V_LNG))
                vector(row(10 * l + V_LNB))

            def modulation():
                for l in range(2):
                    for m in range(6):
                        vector(row(V_ADA + 6 * l + m))
                        if m in (2, 5):
                            store(l, m)

            def store(l, m):
                pool.wait_ge(sem["modg_ready"], c.next("modg_ready", 2))
                for s in range(2):
                    pool.dma_start(mod_scr[l, m // 3, s:s + 1, :], XN[64 * s:64 * s + 1, m % 2, :]) \
                        .then_inc(sem["mod_stored"], 16)

            def gate_row(l, w, s):
                return mod_scr[l, w, s:s + 1, :].broadcast_to([P, D])

            def attend(l, s):
                if l:
                    for n in range(16):
                        q, hp = n // 8, n % 8
                        if n >= 2:
                            pool.wait_ge(sem["bias_free"], c.next("bias_free"))
                        for r in range(2):
                            dy = 3 - (2 * q + r)
                            for hb in range(2):
                                pool.dma_start(BIAS[64 * r:64 * r + 64, n % 2, hb, :].rearrange("p (k c) -> p k c", k=4),
                                               toe[2 * hp + hb, dy:dy + 4].rearrange("k q c -> q k c")) \
                                    .then_inc(sem[f"bias{n % 2}"], 16)
                        pool.wait_ge(sem[f"bias{n % 2}"], c.next(f"bias{n % 2}", 64))
                        b = BIAS[:, n % 2, :, :]
                        pool.tensor_tensor(b, b, WIN[:, :].unsqueeze(1).broadcast_to([P, 2, T]), ALU.add) \
                            .then_inc(sem["bias_ready"], 1)
                vector(gate_row(l, 0, s))

            for name, k in (("acc_free0", 1), ("acc_free1", 1), ("tp_free0", 1), ("tp_free1", 1), ("sc_free", 4), ("o_free", 2)):
                pool.sem_inc(sem[name], k)
            pool.dma_start(K_[:, :], consts).then_inc(sem["const_land"], 16)
            pool.dma_start(COL[:, :], cols).then_inc(sem["const_land"], 16)
            pool.dma_start(X[:, :, :], x_in.rearrange("a (t p) d -> p (a t) d", p=P)).then_inc(sem["x_land"], 16)
            for l in range(2):
                mixer(l)
            vector(row(V_FINAL))
            phase()
            pool.dma_start(ST[:, 16:32], cc).then_inc(sem["cc_land"], 16)
            pool.dma_start(XC[:, :, :], ctx_in.rearrange("a (t p) d -> p (a t) d", p=P)).then_inc(sem["ctx_land"], 16)
            pool.dma_start(ROPE[:, :, :, :], rope).then_inc(sem["rope_land"], 16)
            modulation()
            pool.wait_ge(sem["mod_stored"], c.next("mod_stored", 64 + 64))
            phase()
            for l in range(2):
                phase()
                if l == 0:
                    pool.dma_start(LAMB[:, :, :], lam).then_inc(sem["lam_land"], 16)
                    pool.dma_start(SUBL[:, :], subln).then_inc(sem["lam_land"], 16)
                else:
                    pool.dma_start(WIN[:, :], window).then_inc(sem["win_land"], 16)
                    pool.wait_ge(sem["win_land"], c.next("win_land", 16))
                for s in range(2 - l):
                    attend(l, s)
                    phase()
                pool.dma_start(CW[:, :, :], convw[l]).then_inc(sem["cw_land"], 16)
                for s in range(2 - l):
                    vector(gate_row(l, 1, s))
                    phase()
            vector(row(V_OUT))


def _units(w):
    m = w.shape[1] // 512
    return w.reshape(2, 4, P, m, 512).transpose(3, 0, 2, 1, 4).reshape(2 * m, P, UNIT)


def _units_down(w):
    return w.reshape(FT // 2, 2, P, D).transpose(0, 2, 1, 3).reshape(FT // 2, P, UNIT)


def _paired(w):
    return w.reshape(D, 2, FT // 2, 256).transpose(0, 2, 1, 3).reshape(D, 2 * F)


def _by_feature(v):
    return v.reshape(-1, P).T


def _stream(i):
    parts = []
    for l in range(2):
        w = i["w_in_first"] if l == 0 else i["w_in_rest"][0]
        pb = np.zeros((D, 7 * 512), np.float32)
        pb[:, :SHIFT[l]] = w[:, 4 * D:]
        parts += [_units(_paired(i["ffn1_w_gu"][l])), _units_down(i["ffn1_w_down"][l]), _units(pb),
                  _units(w[:, 3 * D:4 * D]), _units(w[:, 2 * D:3 * D]), _units(w[:, 0:D]), _units(i["w_proj_a"][l]),
                  _units(w[:, D:2 * D]), _units(i["w_proj_b"][l]), _units(i["w_out"][l]),
                  _units(_paired(i["ffn2_w_gu"][l])), _units_down(i["ffn2_w_down"][l])]
    parts += [_units(i["ada_w_2"][0]), _units(i["ada_w_2"][1])]
    qkv, up, down = i["a_wqkv_2"][0], _units(_paired(i["ffn_up_2"][0])), _units_down(i["ffn_down_2"][0])
    parts += [_units(qkv), _units(qkv), _units(i["a_wo_2"][0]), _units(i["a_wo_2"][0]), up, down, up, down]
    qkv = i["b_wqkv_2"][0]
    parts += [_units(qkv), _units(qkv[:, D:]), _units(i["b_wo_2"][0]),
              _units(_paired(i["ffn_up_2"][1])), _units_down(i["ffn_down_2"][1])]
    out = np.concatenate(parts)
    assert out.shape == (NUNITS, P, UNIT)
    return out


def kernel(**inputs):
    import concourse.bacc as bacc
    from concourse.bass_utils import run_bass_kernel_spmd

    i = {k: np.asarray(v) for k, v in inputs.items()}
    vecs = np.zeros((NVEC, D), np.float32)
    cols = np.zeros((P, NCOL), np.float32)
    for l in range(2):
        for n, name in enumerate(("rwkv_w0", "rwkv_a0", "rwkv_k_k", "rwkv_k_a", "rwkv_r_k", "rwkv_gn_g", "rwkv_gn_b",
                                  "sgu_ln_g", "sgu_ln_b")):
            vecs[10 * l + n] = i[name][l].reshape(-1)
        for at, name in ((G_FFN1, "ffn1_norm"), (G_MIX, "mix_norm"), (G_FFN2, "ffn2_norm"), (G_NMIX, "norm_mix_2"),
                         (G_NFFN, "norm_ffn_2")):
            cols[:, at + 8 * l:at + 8 * l + 8] = _by_feature(i[name][l])
        cols[:, G_BS + 8 * l:G_BS + 8 * l + 8] = i["sgu_b_s"][l].T
    vecs[V_V0] = i["rwkv_v0"][0]
    vecs[V_FINAL], vecs[V_OUT] = i["final_norm"], i["norm_out_2"]
    vecs[V_ADA:] = i["ada_b_2"].reshape(12, D)
    mus = np.zeros((2, SHIFT[1]), np.float32)
    mus[0, :SHIFT[0]], mus[1] = i["mu_first"], i["mu_rest"][0]
    col = np.arange(64)
    near = np.clip(col[None, :] - col[:, None], -15, 15) + 15
    arrays = {
        "wstream": _stream(i), "vecs": vecs, "cols": cols, "consts": constants(),
        "x_in": i["x"], "ctx_in": i["ctx_2"], "mus": mus,
        "lora_wa": np.concatenate([i["rwkv_w2"], i["rwkv_a2"]], axis=1), "lora_v": i["rwkv_v2"][0],
        "wst": i["sgu_w_s"].transpose(0, 3, 1, 2),
        "convw": np.stack([np.stack([_by_feature(i["ffn_conv_2"][l, t]) for t in range(3)]
                                    + [_by_feature(i["ffn_conv_b_2"][l])], axis=1) for l in range(2)]),
        "cc": np.stack([i["c_2"][0], i["c_ctx_2"]]).reshape(2, KT, P).transpose(2, 1, 0).reshape(P, 2 * KT),
        "lam": i["a_lambda_2"], "subln": i["a_subln_2"],
        "toe": i["b_rpb_2"][0][:, 4:11][:, :, near], "rope": rope_constants(),
        "window": window_constants(),
    }
    nc = bacc.Bacc("TRN2", target_bir_lowering=False, num_devices=1)
    args = {}
    for name, a in arrays.items():
        arrays[name] = a = np.ascontiguousarray(a)
        args[name] = nc.dram_tensor(name, a.shape, mybir.dt.from_np(a.dtype), kind="ExternalInput").ap()
    args["lam"] = args["lam"].broadcast_to([P, 4, HD])
    args["subln"] = args["subln"].broadcast_to([P, P])
    args["out"] = nc.dram_tensor("out", (1, T, D), F32, kind="ExternalOutput").ap()
    args["mod_scr"] = nc.dram_tensor("mod_scr", (2, 2, 2, D), F32, kind="Internal").ap()
    args["vfirst_scr"] = nc.dram_tensor("vfirst_scr", (P, NT, D), F32, kind="Internal").ap()
    build(nc, **args)
    got = run_bass_kernel_spmd(nc, [arrays], core_ids=[0])
    return got.results[0]["out"]
```

```python
from contextlib import ExitStack, contextmanager

import numpy as np
import concourse.bass as bass
from concourse import mybir

F32 = mybir.dt.float32
F32R = mybir.dt.float32r
ACT = mybir.ActivationFunctionType
ALU = mybir.AluOpType
AX = mybir.AxisListType

P = 128
D = 1024
T = 256
NT = T // P
KT = D // P
F = 2816
FT = F // P
LORA = 64
MV = 32
CHUNK = 64
HEADS = 16
HD = 64
SHIFT = (3 * D + 2 * LORA, 3 * D + 2 * LORA + MV)
UNIT = 2048
RAW, SPLIT = 2, 4
WIDE = 4
NORM_EPS, LN_EPS, GN_EPS = 1e-6, 1e-5, 64e-5
DECAY = float(np.exp(np.float32(-0.5)))
LAM_INIT = 0.2
SCALE = 0.125

C_ID, C_LEVEL, C_LEVEL0T = 0, 128, 128 * 7
C_GRAM, C_TRI, C_TRIX, C_BD, C_TRIU = 128 * 8, 128 * 10, 128 * 11, 128 * 12, 128 * 13
C_ONE = 128 * 14
C_CHUNK = 128 * 15
NCONST = C_CHUNK + 2


def constants():
    a = np.arange(P)
    row, col = a[:, None], a[None, :]
    same = row // CHUNK == col // CHUNK
    out = np.zeros((P, NCONST), np.float32)
    out[:, C_ID:C_ID + P] = row == col
    for j in range(6):
        m = (row >> (j + 1) == col >> (j + 1)) & (row >> j & 1 == 1) & (col >> j & 1 == 0)
        out[:, C_LEVEL + P * j:C_LEVEL + P * (j + 1)] = m
        if j == 0:
            out[:, C_LEVEL:C_LEVEL + P] += row == col
            out[:, C_LEVEL0T:C_LEVEL0T + P] = m.T
    out[:, C_GRAM:C_GRAM + P] = (row < col) & same
    out[:, C_GRAM + P:C_GRAM + 2 * P] = (row <= col) & same
    out[:, C_TRI:C_TRI + P] = ((row <= col) & same) * np.float32(-DECAY)
    out[:, C_TRIX:C_TRIX + P] = ((row < col) & same) * np.float32(-DECAY)
    out[:, C_BD:C_BD + P] = row // HD == col // HD
    out[:, C_TRIU:C_TRIU + P] = row <= col
    out[:, C_ONE:C_ONE + P] = 1.0
    for c in range(2):
        out[:, C_CHUNK + c] = (a // CHUNK == c) * np.float32(-DECAY)
    return out


def rope_constants():
    t = np.arange(T)
    inv = (np.float32(10000.0) ** (-np.arange(16, dtype=np.float32) / np.float32(16))).astype(np.float32)
    ar = (t // 64).astype(np.float32)[:, None] * inv
    ac = (t % 64).astype(np.float32)[:, None] * inv
    cos = np.concatenate([np.cos(ar), np.cos(ar), np.cos(ac), np.cos(ac)], 1)
    sin = np.concatenate([-np.sin(ar), np.sin(ar), -np.sin(ac), np.sin(ac)], 1)
    return np.stack([cos, sin]).reshape(2, NT, P, 64).transpose(2, 0, 1, 3).astype(np.float32)


def window_constants():
    q, k = np.arange(P)[:, None] % 64, np.arange(T)[None, :] % 64
    start = np.clip(q - 8, 0, 48)
    return np.where((k >= start) & (k < start + 16), 0.0, -1e30).astype(np.float32)


V_W0, V_A0, V_KK, V_KA, V_RK, V_GNG, V_GNB, V_LNG, V_LNB, V_V0 = range(10)
V_FINAL, V_OUT, V_ADA = 20, 21, 22
NVEC = V_ADA + 12
G_FFN1, G_MIX, G_FFN2, G_NMIX, G_NFFN = 0, 16, 32, 48, 64
G_BS = 80
NCOL = G_BS + 16


def stream_plan():
    plan, at = {}, 0

    def add(name, units):
        nonlocal at
        plan[name] = (at, units)
        at += units

    for l in range(2):
        add(f"gu1{l}", 22), add(f"down1{l}", 11)
        add(f"pb{l}", 14), add(f"gate_a{l}", 4), add(f"sgu_v{l}", 4), add(f"gate_b{l}", 4), add(f"sgu_u{l}", 4)
        add(f"proj_b{l}", 4), add(f"proj_a{l}", 4), add(f"out{l}", 4)
        add(f"gu2{l}", 22), add(f"down2{l}", 11)
    add("ada0", 24), add("ada1", 24)
    add("qkv0", 12), add("qkvc0", 12), add("wo0", 4), add("woc0", 4)
    add("up0", 22), add("cdown0", 11), add("upc0", 22), add("cdownc0", 11)
    add("qkv1", 12), add("kvc1", 8), add("wo1", 4), add("up1", 22), add("cdown1", 11)
    return plan, at


PLAN, NUNITS = stream_plan()
WIDE_FROM, WIDE_TO = PLAN["ada0"][0] + SPLIT, PLAN["ada1"][0] + PLAN["ada1"][1]


Q_PART, K_PART, V_PART = range(3)


def projections(l):
    out = []
    for s, parts in ((0, (Q_PART, V_PART, K_PART)), (1, (V_PART, K_PART) if l else (V_PART, Q_PART, K_PART))):
        for part in parts:
            for half in range(2):
                behind = {(0, V_PART, 0): (0, Q_PART), (1, V_PART, 0): (0, K_PART), (1, K_PART, 1): (1, K_PART)}
                if not l:
                    behind[1, K_PART, 0] = (1, Q_PART)
                out.append((s, part, half, behind.get((s, part, half))))
    return out


class Counts:

    def __init__(self, eng, sems):
        self.eng, self.sems = eng, sems
        self.base, self.local, self.i, self.per = {}, {}, None, {}

    def next(self, view, k=1):
        if self.i is None:
            self.base[view] = self.base.get(view, 0) + k
            return self.base[view]
        self.local[view] = self.local.get(view, 0) + k
        return self.i * self.per[view] + (self.base.get(view, 0) + self.local[view])

    @contextmanager
    def loop(self, n, per):
        with self.eng.Fori(0, n) as i:
            self.i, self.per, self.local = i, per, {}
            yield i
            assert self.local == per, (self.local, per)
            self.i = None
        for view, k in per.items():
            self.base[view] = self.base.get(view, 0) + n * k


def build(nc, wstream, vecs, cols, consts, x_in, ctx_in, mus, lora_wa, lora_v, wst, convw, cc, lam, subln,
          toe, rope, window, out, mod_scr, vfirst_scr):
    ctx = ExitStack()
    with ctx:
        top = nc.sbuf_base
        base = (top + 63) // 64 * 64
        place = {"at": base}

        def sb(name, shape, dt=F32, at=None):
            size = 4 * int(np.prod(shape[1:]))
            if at is None:
                at = place["at"]
                place["at"] += (size + 31) // 32 * 32
            assert at + size <= nc.sbuf_usable_end, (name, at + size)
            return nc.alloc_sbuf_tensor_at(name, list(shape), dt, offset=at)

        raw = sb("raw", [P, RAW, UNIT])
        w_hi = sb("w_hi", [P, SPLIT, UNIT], F32R)
        w_lo = sb("w_lo", [P, SPLIT, UNIT], F32R)
        X = sb("X", [P, NT, D])
        HA_hi, HA_lo = sb("HA_hi", [P, KT, T], F32R), sb("HA_lo", [P, KT, T], F32R)
        K_ = sb("K_", [P, NCONST])
        COL = sb("COL", [P, NCOL])
        SS = sb("SS", [P, 32])
        RS = sb("RS", [P, 32])
        ST = sb("ST", [P, 64])
        RN = ST[:, 60:62]
        CC_IN, CC = sb("CC_IN", [P, 2 * KT]), sb("CC", [P, 2 * KT])
        BN = sb("BN", [P, NT, HEADS])
        GAM = sb("GAM", [P, 32])
        MODC = sb("MODC", [P, 2, 4, KT, 2])
        MODS = sb("MODS", [P, 2, 2, KT, 2])
        arena = place["at"]
        KB = 1024

        def ar(name, kib, shape, dt=F32):
            return sb(name, shape, dt, at=arena + int(kib * KB))

        FT_hi, FT_lo = ar("FT_hi", 8, [P, FT, T], F32R), ar("FT_lo", 30, [P, FT, T], F32R)
        HID = ar("HID", 52, [P, 2, NT, 256])
        XN = ar("XN", 56, [P, NT, D])
        BC = ar("BC", 64, [P, 2, D])
        TF = ar("TF", 72, [P, 2, 512])
        HB_hi, HB_lo = ar("HB_hi", 78, [P, KT, T], F32R), ar("HB_lo", 86, [P, KT, T], F32R)
        R, K, V = ar("R", 0, [P, NT, D]), ar("K", 8, [P, NT, D]), ar("V", 16, [P, NT, D])
        KK, AA = ar("KK", 24, [P, NT, D]), ar("AA", 32, [P, NT, D])
        T1, T2 = ar("T1", 40, [P, NT, D]), ar("T2", 48, [P, NT, D])
        LOR = ar("LOR", 48, [P, NT, 160])
        LORT = ar("LORT", 50, [P, 3, T])
        W2A2, V2 = ar("W2A2", 56, [P, D]), ar("V2", 60, [P, D])
        MU = ar("MU", 72, [P, SHIFT[1]])
        PREV = ar("PREV", 85, [P, 2, NT, 512])
        DIF = ar("DIF", 40, [P, NT, 512])
        VF = ar("VF", 72, [P, NT, D])
        AR = ar("AR", 56, [P, 4, 2, P])
        BK = ar("BK", 60, [P, 2, 2, 2, P])
        VZ, U = ar("VZ", 64, [P, 4, 2, P]), ar("U", 68, [P, 4, 2, P])
        LG = ar("LG", 72, [P, 8, 512])
        S, SU = ar("S", 88, [P, 4, P]), ar("SU", 90, [P, 4, P])
        XX = ar("XX", 40, [P, 4, 2, 2, P])
        MVY = ar("MVY", 48, [P, 4, 256])
        TM = ar("TM", 52, [P, 4, 256])
        PM = ar("PM", 52, [P, 4, P])
        VA, UA = ar("VA", 8, [P, NT, D]), ar("UA", 16, [P, NT, D])
        MERG, GATE_A, GATE_B = (ar(n, at, [P, NT, D]) for n, at in (("MERG", 24), ("GATE_A", 32), ("GATE_B", 40)))
        WST = ar("WST", 48, [P, 8, P])
        SQ = ar("SQ", 56, [P, NT, D])
        RAWX = ar("RAWX", 8, [P, WIDE, UNIT])
        XC = ar("XC", 0, [P, NT, D])
        QTX, QTC = ar("QTX", 8, [P, KT, T]), ar("QTC", 16, [P, KT, T])
        KTT = ar("KTT", 24, [P, KT, 2 * T])
        VV = ar("VV", 40, [P, 4, D])
        PR = ar("PR", 76, [P, 2, 2, 512])
        AT = ar("AT", 84, [P, 2, 512])
        SC = ar("SC", 0, [P, 2, 2, 512])
        BIAS = ar("BIAS", 16, [P, 3, 2, T])
        WIN = ar("WIN", 22, [P, T])
        ROPE = ar("ROPE", 76, [P, 2, NT, 64])
        LAMB = ar("LAMB", 92, [P, 4, HD])
        SUBL = ar("SUBL", 93, [P, P])
        QK = ar("QK", 64, [P, 512])
        OUTJ = ar("OUTJ", 74, [P, P])
        RB = ar("RB", 62, [P, 2, T])
        JUNK = ar("JUNK", 52, [P, D])
        DIAG = ar("DIAG", 77, [P, NT, P])
        QZ = ar("QZ", 72, [P, 2, 2, P])
        US = ar("US", 52, [P, 2, NT, 512])
        CV = ar("CV", 76, [P, 2, 4, T])
        HV = ar("HV", 84, [P, 2, 2, T])
        CW = ar("CW", 88, [P, 4, 2 * FT])

        ACC = [ctx.enter_context(nc.psum_tensor(f"ACC{i}", [P, NT, 512], F32)) for i in range(2)]
        TP = [ctx.enter_context(nc.psum_tensor(f"TP{i}", [P, 512], F32)) for i in range(2)]
        M = [ctx.enter_context(nc.psum_tensor(f"M{i}", [P, 512], F32)) for i in range(2)]
        A4 = [ACC[0][:, 0, :], ACC[0][:, 1, :], ACC[1][:, 0, :], ACC[1][:, 1, :]]
        B4 = [TP[0][:, :], TP[1][:, :], M[0][:, :], M[1][:, :]]

        names = ["land0", "land1", "wide0", "wide1", "wide2", "wide3", "bc0", "bc1", "hi_ready", "lo_ready",
                 "unit_done", "acc_ready", "acc_free0", "acc_free1", "tp_ready", "tp_free0", "tp_free1",
                 "tf_ready", "hi_feat", "feat_ready", "xn_ready", "ss_ready", "rs_ready", "sil_ready",
                 "hid_ready", "bc_free", "phase_done", "p_ready", "mix_done", "shift0", "shift1", "zero_ready",
                 "mu_land", "lora_tanh", "lora_tr", "pre_ready", "sig_ready", "vsig_ready", "asig_ready",
                 "gn_done", "r_done", "bonus_ready", "merge_done", "res_ready", "x_half", "diag_ready",
                 "rb_ready", "rs_pre", "v_final", "cc_hi", "modg_ready", "cw_land", "rope_land", "exp_ready",
                 "exp_used", "param_land", "v_stored", "vf_land", "gam_ready", "arbk_ready", "gram_ready",
                 "lg_ready", "x_ready", "t_ready", "t_masked", "u_ready", "mv_ready", "mv_copied", "pp_ready",
                 "pm_ready", "uu_ready", "vz_ready", "qz_ready", "u_copied", "sy_ready", "s_done", "y_done",
                 "s_zero", "wst_land", "va_ready", "gelu_ready", "gate_ready", "const_land", "x_land",
                 "ctx_land", "cc_land", "cc_ready", "mod_ready", "mod_stored", "lam_ready", "lam_exp",
                 "lam_land", "q_ready", "sc_ready", "max_ready", "prob_ready", "mix_ready", "at_ready",
                 "o_ready", "o_copied", "o_free", "sc_free", "bias0", "bias1", "bias2", "bias_ready",
                 "bias_free", "win_land", "u_copy", "cv_ready", "cv_conv", "sg_ready", "hv_ready", "out_ready",
                 "out_land"]
        sem = {n: ctx.enter_context(nc.semaphore(n)) for n in names}
        block = ctx.enter_context(nc.Block())

        def row(v):
            return vecs[v:v + 1, :].broadcast_to([P, D])

        def whole(t):
            return t[:, :, :].rearrange("p t n -> p (t n)")

        def heads(t):
            return t[:, :, :].rearrange("p t (h d) -> p (t h) d", d=HD)

        def shifted(l, n):
            if n == 0:
                return LOR[:, :, 0:SHIFT[l] - 3 * D], SHIFT[l] - 3 * D, 3 * D
            half = (n - 1) % 2
            return (R, K, V)[(n - 1) // 2][:, :, 512 * half:512 * half + 512], 512, 512 * (n - 1)

        def arrival(u):
            if WIDE_FROM <= u < WIDE_TO:
                return RAWX[:, (u - WIDE_FROM) % WIDE, :], f"wide{(u - WIDE_FROM) % WIDE}"
            return raw[:, u % RAW, :], f"land{u % RAW}"

        def ident(n=P):
            return K_[0:n, C_ID:C_ID + n]

        @block.sync
        def _(eng):
            for u in range(RAW):
                eng.dma_start(raw[:, u, :], wstream[u]).then_inc(sem[f"land{u}"], 16)
            with eng.Fori(1, WIDE_FROM // RAW) as i:
                for s in range(RAW):
                    eng.wait_ge(sem["lo_ready"], i * RAW + (s + 1 - RAW))
                    eng.dma_start(raw[:, s, :], wstream[bass.ds(i * RAW + s, 1), :, :]
                                  .rearrange("a p n -> p (a n)")).then_inc(sem[f"land{s}"], 16)
            eng.wait_ge(sem["unit_done"], PLAN["ada0"][0])
            for s in range(WIDE):
                eng.dma_start(RAWX[:, s, :], wstream[WIDE_FROM + s]).then_inc(sem[f"wide{s}"], 16)
            with eng.Fori(1, (WIDE_TO - WIDE_FROM) // WIDE) as i:
                for s in range(WIDE):
                    eng.wait_ge(sem["lo_ready"], i * WIDE + (WIDE_FROM + s + 1 - WIDE))
                    eng.dma_start(RAWX[:, s, :], wstream[bass.ds(i * WIDE + (WIDE_FROM + s), 1), :, :]
                                  .rearrange("a p n -> p (a n)")).then_inc(sem[f"wide{s}"], 16)
            for u in range(WIDE_TO, WIDE_TO + RAW):
                eng.wait_ge(sem["lo_ready"], WIDE_FROM - RAW + u % RAW + 1)
                eng.dma_start(raw[:, u % RAW, :], wstream[u]).then_inc(sem[f"land{u % RAW}"], 16)
            with eng.Fori(WIDE_TO // RAW + 1, NUNITS // RAW) as i:
                for s in range(RAW):
                    eng.wait_ge(sem["lo_ready"], i * RAW + (s + 1 - RAW))
                    eng.dma_start(raw[:, s, :], wstream[bass.ds(i * RAW + s, 1), :, :]
                                  .rearrange("a p n -> p (a n)")).then_inc(sem[f"land{s}"], 16)
            for u in range(NUNITS // RAW * RAW, NUNITS):
                eng.wait_ge(sem["lo_ready"], u + 1 - RAW)
                eng.dma_start(raw[:, u % RAW, :], wstream[u]).then_inc(sem[f"land{u % RAW}"], 16)
            eng.wait_ge(sem["out_ready"], 1)
            eng.dma_start(out.rearrange("a (t p) d -> p (a t) d", p=P), XN[:, :, :]).then_inc(sem["out_land"], 16)
            eng.wait_ge(sem["out_land"], 16)

        @block.tensor
        def _(pe):
            c = Counts(pe, sem)

            def phase():
                pe.drain().then_inc(sem["phase_done"], 1)
                pe.wait_ge(sem["phase_done"], c.next("phase_done", 4))

            st = {"u": 0, "b": 0, "tp": 0, "at": 0}
            Z = {"wkv": 0}

            def mm(*a, **k):
                return pe.matmul(*a, skip_group_check=True, **k)

            def unit_wide(h_hi, h_lo, part, width=512, tiles=NT):
                pe.wait_ge(sem["lo_ready"], c.next("lo_ready"))
                s, acc = st["u"] % SPLIT, ACC[st["b"] % 2]
                for k in range(4):
                    cols_ = slice(512 * k, 512 * k + width)
                    for t in range(tiles):
                        a = h_hi[:, 4 * part + k, P * t:P * t + P]
                        al = h_lo[:, 4 * part + k, P * t:P * t + P]
                        mm(acc[:, t, 0:width], a, w_hi[:, s, cols_], start=part == 0 and k == 0, stop=False)
                        mm(acc[:, t, 0:width], a, w_lo[:, s, cols_], start=False, stop=False)
                        last = mm(acc[:, t, 0:width], al, w_hi[:, s, cols_], start=False, stop=part == 1 and k == 3)
                last.then_inc(sem["unit_done"], 1)
                st["u"] += 1

            def block_wide(h_hi, h_lo, fresh=False, **k):
                pe.wait_ge(sem[f"acc_free{st['b'] % 2}"], c.next(f"acc_free{st['b'] % 2}"))
                for part in range(2):
                    if fresh:
                        need_features(2)
                    unit_wide(h_hi, h_lo, part, **k)
                st["b"] += 1

            def down():
                for n in range(2):
                    pe.wait_ge(sem[f"acc_free{(st['b'] + n) % 2}"], c.next(f"acc_free{(st['b'] + n) % 2}"))
                for j in range(FT // 2):
                    pe.wait_ge(sem["feat_ready"], c.next("feat_ready"))
                    pe.wait_ge(sem["lo_ready"], c.next("lo_ready"))
                    s = st["u"] % SPLIT
                    for k in range(2):
                        for n in range(2):
                            acc = ACC[(st["b"] + n) % 2]
                            cols_ = slice(1024 * k + 512 * n, 1024 * k + 512 * n + 512)
                            for t in range(NT):
                                a, al = (z[:, 2 * j + k, P * t:P * t + P] for z in (FT_hi, FT_lo))
                                first, end = j == 0 and k == 0, j == FT // 2 - 1 and k == 1
                                mm(acc[:, t, :], a, w_hi[:, s, cols_], start=first, stop=False)
                                mm(acc[:, t, :], a, w_lo[:, s, cols_], start=False, stop=False)
                                last = mm(acc[:, t, :], al, w_hi[:, s, cols_], start=False, stop=end)
                    last.then_inc(sem["unit_done"], 1)
                    st["u"] += 1
                    yield
                st["b"] += 2

            def turn(src, n, dst=None, k0=0):
                pe.wait_ge(sem[f"tp_free{st['tp'] % 2}"], c.next(f"tp_free{st['tp'] % 2}"))
                bank = TP[st["tp"] % 2]
                for k in range(n):
                    for t in range(NT):
                        last = pe.transpose(bank[:, (NT * k + t) * P:(NT * k + t + 1) * P],
                                            src[:, t, (k0 + k) * P:(k0 + k + 1) * P], ident())
                last.then_inc(sem["tp_ready"], 1)
                st["tp"] += 1

            def features(src, wait):
                pe.wait_ge(sem[wait], c.next(wait))
                for g in range(KT // 2):
                    turn(src, 2, k0=2 * g)

            def raw_features():
                for g in range(KT // 2):
                    if g % 2 == 0:
                        pe.wait_ge(sem["x_half"], c.next("x_half"))
                    turn(X, 2, k0=2 * g)

            def normed_features(src, s):
                pe.wait_ge(sem["res_ready"], c.next("res_ready"))
                for g in range(KT // 2):
                    if g == 2:
                        pe.wait_ge(sem["diag_ready"], c.next("diag_ready"))
                        for t in range(NT):
                            last = mm(M[s][:, P * t:P * t + P], K_[:, C_ONE:C_ONE + P], DIAG[:, t, :],
                                      start=True, stop=True)
                        last.then_inc(sem["rb_ready"], 1)
                    turn(src, 2, k0=2 * g)

            def need_features(n=KT // 2):
                pe.wait_ge(sem["feat_ready"], c.next("feat_ready", n))

            def swiglu():
                raw_features()

                def hidden(b):
                    pe.wait_ge(sem["hid_ready"], c.next("hid_ready"))
                    turn(HID[:, b % 2, :, :], 2)

                block_wide(HA_hi, HA_lo, fresh=True)
                with c.loop(5, {"lo_ready": 4, "acc_free0": 1, "acc_free1": 1, "hid_ready": 2, "tp_free0": 1, "tp_free1": 1}):
                    for b in (1, 2):
                        block_wide(HA_hi, HA_lo)
                        hidden(b - 1)
                d = down()
                next(d)
                hidden(10)
                for _ in d:
                    pass

            def mixer(l):
                raw_features()
                block_wide(HA_hi, HA_lo, fresh=True, width=SHIFT[l] - 3 * D)
                for j in range(3):
                    block_wide(HA_hi, HA_lo)
                pe.wait_ge(sem["lora_tanh"], c.next("lora_tanh"))
                pe.wait_ge(sem[f"tp_free{st['tp'] % 2}"], c.next(f"tp_free{st['tp'] % 2}"))
                bank = TP[st["tp"] % 2]
                for t in range(NT):
                    last = pe.transpose(bank[:, P * t:P * t + P], LOR[:, t, 0:P], ident())
                if l:
                    for t in range(NT):
                        last = pe.transpose(bank[0:MV, T + P * t:T + P * t + P], LOR[:, t, P:P + MV], ident())
                last.then_inc(sem["tp_ready"], 1)
                st["tp"] += 1
                for j in range(3):
                    block_wide(HA_hi, HA_lo)
                pe.wait_ge(sem["lora_tr"], c.next("lora_tr"))
                pe.wait_ge(sem["param_land"], c.next("param_land", 16 * (1 + l)))

                def up(w, part):
                    for t in range(NT):
                        pe.wait_ge(sem[f"acc_free{st['b'] % 2}"], c.next(f"acc_free{st['b'] % 2}"))
                        for n in range(2):
                            last = mm(ACC[st["b"] % 2][:, n, :], LORT[:, part, P * t:P * t + P],
                                      w[:, 512 * n:512 * n + 512], start=True, stop=True)
                        last.then_inc(sem["acc_ready"], 1)
                        st["b"] += 1

                if l:
                    up(V2, 2)
                up(W2A2, 0)
                up(W2A2, 1)
                for t in range(NT):
                    pe.wait_ge(sem["sig_ready"], c.next("sig_ready"))
                    for tri in (C_TRIX, C_TRI):
                        pe.wait_ge(sem[f"acc_free{st['b'] % 2}"], c.next(f"acc_free{st['b'] % 2}"))
                        for n in range(2):
                            last = mm(ACC[st["b"] % 2][:, n, :], K_[:, tri:tri + P], T1[:, t, 512 * n:512 * n + 512],
                                      start=True, stop=True)
                        last.then_inc(sem["acc_ready"], 1)
                        st["b"] += 1
                    for q in range(KT):
                        last = mm(M[0][:, 4 * q + 2 * t:4 * q + 2 * t + 2], T1[:, t, P * q:P * q + P],
                                  K_[:, C_CHUNK:C_CHUNK + 2], start=True, stop=True)
                last.then_inc(sem["gam_ready"], 1)
                phase()
                for g in range(2):
                    for t in range(NT):
                        wkv_parallel(g, t)
                        wkv_chain(g, t)
                phase()

                for j in range(6):
                    block_wide(HA_hi, HA_lo)
                features(R, "r_done")
                pe.wait_ge(sem["va_ready"], c.next("va_ready"))
                for t in range(NT):
                    pe.wait_ge(sem[f"acc_free{st['b'] % 2}"], c.next(f"acc_free{st['b'] % 2}"))
                    for g in range(8):
                        last = mm(ACC[st["b"] % 2][:, g // 4, P * (g % 4):P * (g % 4) + P], WST[:, g, :],
                                  VA[:, t, P * g:P * g + P], start=True, stop=True)
                    last.then_inc(sem["acc_ready"], 1)
                    st["b"] += 1
                for j in range(2):
                    block_wide(HA_hi, HA_lo)
                need_features()
                block_wide(HB_hi, HB_lo)
                features(VA, "xn_ready")
                block_wide(HB_hi, HB_lo)
                need_features()
                for j in range(2):
                    block_wide(HA_hi, HA_lo)
                for g in range(KT // 2):
                    if g % 2 == 0:
                        pe.wait_ge(sem["merge_done"], c.next("merge_done"))
                    turn(MERG, 2, k0=2 * g)
                block_wide(HB_hi, HB_lo, fresh=True)
                block_wide(HB_hi, HB_lo)

            def wkv_parallel(g, t):
                def turn_pair(p):
                    pe.wait_ge(sem[f"tp_free{st['tp'] % 2}"], c.next(f"tp_free{st['tp'] % 2}"))
                    bank = TP[st["tp"] % 2]
                    for n, src in enumerate((KK, R, AA, K)):
                        last = pe.transpose(bank[:, P * n:P * n + P],
                                            src[:, t, P * (4 * g + p):P * (4 * g + p) + P], ident())
                    last.then_inc(sem["tp_ready"], 1)
                    st["tp"] += 1

                turn_pair(0)
                for p in range(4):
                    if p < 3:
                        turn_pair(p + 1)
                    pe.wait_ge(sem["arbk_ready"], c.next("arbk_ready"))
                    for hb in range(2):
                        n = 8 * (2 * g + t) + 2 * p + hb
                        if n >= 2:
                            pe.wait_ge(sem["lg_ready"], Z["wkv"] + n - 1)
                        ar_ = AR[:, p, :, :].rearrange("p a n -> p (a n)")
                        mm(M[hb][:, 0:256], BK[:, p % 2, hb, 0, :], ar_, start=True, stop=True)
                        mm(M[hb][:, 256:512], BK[:, p % 2, hb, 1, :], ar_, start=True, stop=True) \
                            .then_inc(sem["gram_ready"], 1)
                pe.wait_ge(sem["lg_ready"], Z["wkv"] + 8 * (2 * g + t + 1))
                for p in range(4):
                    for hb in range(2):
                        mm(A4[p][:, P * hb:P * hb + P], LG[:, 2 * p + hb, 0:P], ident(), start=True, stop=False)
                        last = mm(A4[p][:, P * hb:P * hb + P], ident(), ident(), start=False, stop=True)
                    last.then_inc(sem["t_ready"], 1)
                for j in range(1, 6):
                    for p in range(4):
                        pe.wait_ge(sem["x_ready"], c.next("x_ready"))
                        for hb in range(2):
                            last = mm(A4[p][:, P * hb:P * hb + P], LG[:, 2 * p + hb, 0:P], XX[:, p, hb, 0, :],
                                      start=True, stop=True)
                        last.then_inc(sem["t_ready"], 1)
                    for p in range(4):
                        pe.wait_ge(sem["t_masked"], c.next("t_masked"))
                        for hb in range(2):
                            tm = TM[:, p, P * hb:P * hb + P]
                            if j < 5:
                                mm(B4[p][:, 256 * hb:256 * hb + P], XX[:, p, hb, 1, :], tm, start=True, stop=True)
                            last = mm(B4[p][:, 256 * hb + P:256 * hb + 256], tm, XX[:, p, hb, 1, :],
                                      start=True, stop=True)
                        last.then_inc(sem["u_ready"], 1)
                for p in range(4):
                    q = 4 * g + p
                    for n, (col0, lg0) in enumerate(((0, 256), (P, 384))):
                        for hb in range(2):
                            last = mm(A4[p][:, col0 + HD * hb:col0 + HD * hb + HD], LG[:, 2 * p + hb, lg0:lg0 + P],
                                      V[:, t, P * q + HD * hb:P * q + HD * hb + HD], start=True, stop=True)
                    last.then_inc(sem["mv_ready"], 1)
                pe.wait_ge(sem["x_ready"], c.next("x_ready", 4))

            def wkv_chain(g, t):
                call = 2 * g + t
                if t == 0:
                    pe.wait_ge(sem["s_zero"], c.next("s_zero"))
                pe.wait_ge(sem["vz_ready"], c.next("vz_ready"))
                for ch in range(2):
                    rows = slice(CHUNK * ch, CHUNK * ch + CHUNK)
                    for p in range(4):
                        if ch == 0:
                            pe.wait_ge(sem["mv_copied"], c.next("mv_copied"))
                        else:
                            pe.wait_ge(sem["y_done"], Z["wkv"] + 8 * call + p + 1)
                            pe.wait_ge(sem["s_done"], Z["wkv"] + 8 * call + p + 1)
                        mm(A4[p][rows, 0:P], AR[:, p, 0, rows], S[:, p, :], start=True, stop=True) \
                            .then_inc(sem["pp_ready"], 1)
                    for p in range(4):
                        pe.wait_ge(sem["pm_ready"], c.next("pm_ready"))
                        for hb in range(2):
                            last = mm(B4[p][rows, HD * hb:HD * hb + HD], XX[rows, p, hb, 1, rows],
                                      PM[rows, p, HD * hb:HD * hb + HD], start=True, stop=True)
                        last.then_inc(sem["uu_ready"], 1)
                    for p in range(4):
                        q = 4 * g + p
                        pe.wait_ge(sem["u_copied"], c.next("u_copied"))
                        mm(A4[p][rows, P:2 * P], AR[:, p, 1, rows], S[:, p, :], start=True, stop=False)
                        for hb in range(2):
                            mm(A4[p][rows, P + HD * hb:P + HD * hb + HD],
                               LG[rows, 2 * p + hb, P + CHUNK * ch:P + CHUNK * ch + CHUNK],
                               U[rows, p, ch, HD * hb:HD * hb + HD], start=False, stop=hb == 1)
                        cols_ = slice(P * q, P * q + P)
                        mm(B4[p][:, P:2 * P], AA[:, t, cols_], U[:, p, ch, :], start=True, stop=False)
                        mm(B4[p][:, P:2 * P], K[:, t, cols_], VZ[:, p, ch, :], start=False, stop=True) \
                            .then_inc(sem["sy_ready"], 1)
                pe.wait_ge(sem["y_done"], Z["wkv"] + 8 * (call + 1))
                pe.wait_ge(sem["s_done"], Z["wkv"] + 8 * (call + 1))

            def modulation():
                pe.wait_ge(sem["cc_ready"], c.next("cc_ready"))
                for l in range(2):
                    for j in range(12):
                        block_wide(HA_hi, HA_lo, tiles=1)
                        if j in (1, 3, 7, 9):
                            pe.wait_ge(sem["mod_ready"], c.next("mod_ready", 2))
                            for h in range(2):
                                pe.wait_ge(sem[f"tp_free{st['tp'] % 2}"], c.next(f"tp_free{st['tp'] % 2}"))
                                for k in range(4):
                                    m = 4 * h + k
                                    last = pe.transpose(TP[st["tp"] % 2][:, P * k:P * k + P],
                                                        XN[:, j // 2 % 2, P * m:P * m + P], ident())
                                last.then_inc(sem["tp_ready"], 1)
                                st["tp"] += 1

            def project(l):
                normed_features(X, 0)
                for j, (s, _, _, behind) in enumerate(projections(l)):
                    if j == 6:
                        need_features()
                    block_wide(*((HB_hi, HB_lo) if s else (HA_hi, HA_lo)), fresh=j == 0)
                    if j == 0:
                        normed_features(XC, 1)
                    if behind:
                        features(XN, "q_ready")

            def attend(l, s):
                nk = 4 if s == 0 else 2
                keys = slice(0, 512) if s == 0 else slice(T, 2 * T)
                turns = [(q, hp) for q in range(NT) for hp in range(8)]

                def scores(n):
                    q, hp = turns[n]
                    for hb in range(2):
                        if hb == 0:
                            pe.wait_ge(sem["qz_ready"], c.next("qz_ready"))
                        pe.wait_ge(sem["sc_free"], c.next("sc_free"))
                        mm(A4[2 * (n % 2) + hb][:, 0:nk * P], QZ[:, n % 2, hb, :], KTT[:, hp, keys],
                           start=True, stop=True).then_inc(sem["sc_ready"], 1)

                def turn_probs(n):
                    pe.wait_ge(sem["mix_ready"], c.next("mix_ready"))
                    for hb in range(1 if l == 0 else 2):
                        pe.wait_ge(sem[f"tp_free{st['tp'] % 2}"], c.next(f"tp_free{st['tp'] % 2}"))
                        for k in range(nk):
                            last = pe.transpose(TP[st["tp"] % 2][:, P * k:P * k + P],
                                                PR[:, n % 2, hb, P * k:P * k + P], ident())
                        last.then_inc(sem["tp_ready"], 1)
                        st["tp"] += 1

                def values(n):
                    q, hp = turns[n]
                    pe.wait_ge(sem["o_free"], c.next("o_free"))
                    for hb in range(1 if l == 0 else 2):
                        pe.wait_ge(sem["at_ready"], c.next("at_ready"))
                        w = P if l == 0 else HD
                        for k in range(nk):
                            kt = k if s == 0 else 2 + k
                            last = mm(M[n % 2][:, w * hb:w * hb + w],
                                      AT[:, st["at"] % 2, P * k:P * k + P],
                                      VV[:, kt, P * hp + w * hb:P * hp + w * hb + w], start=k == 0, stop=k == nk - 1)
                        st["at"] += 1
                    last.then_inc(sem["o_ready"], 1)

                scores(0)
                scores(1)
                for n in range(17):
                    if n < 14:
                        scores(n + 2)
                    if n:
                        values(n - 1)
                    if n < 16:
                        turn_probs(n)

            def conv_ffn(s):
                normed_features(XC if s else X, s)

                def turn_up(b):
                    pe.wait_ge(sem["u_copy"], c.next("u_copy"))
                    for h in range(2):
                        turn(US[:, b % 2, :, :], 2, k0=2 * h)

                block_wide(HA_hi, HA_lo, fresh=True)
                with c.loop(5, {"lo_ready": 4, "acc_free0": 1, "acc_free1": 1, "u_copy": 2, "tp_free0": 2, "tp_free1": 2}):
                    for b in (1, 2):
                        block_wide(HA_hi, HA_lo)
                        turn_up(b - 1)
                d = down()
                next(d), next(d)
                turn_up(10)
                for _ in d:
                    pass

            pe.wait_ge(sem["const_land"], c.next("const_land", 32))
            for l in range(2):
                Z["wkv"] = 32 * l
                swiglu()
                mixer(l)
                swiglu()
            pe.drain().then_inc(sem["phase_done"], 1)
            c.next("phase_done", 4)
            modulation()
            phase()
            for l in range(2):
                project(l)
                phase()
                for s in range(2 - l):
                    attend(l, s)
                    features(XN, "xn_ready")
                    need_features()
                    for j in range(2):
                        block_wide(HA_hi, HA_lo)
                    phase()
                for s in range(2 - l):
                    conv_ffn(s)
                    phase()

        class Side:

            def __init__(self, eng):
                self.c = Counts(eng, sem)
                self.pos, self.u, self.b, self.tp = 0, 0, 0, 0

            def turn(self):
                return 0 if self.c.i is None else self.c.i * SPLIT

            def skip(self, units, blocks):
                self.pos += units
                self.b += blocks

            def skip_turns(self, n):
                self.tp += n
                self.c.next("tp_ready", n)

            def reached(self, units=2):
                self.pos += units
                return self.turn() + self.pos

            def pair(self):
                self.b += 1
                return ACC[(self.b - 1) % 2]

            def bank(self):
                self.tp += 1
                return TP[(self.tp - 1) % 2]

            def acc_free(self):
                return sem[f"acc_free{(self.b - 1) % 2}"]

            def tp_free(self):
                return sem[f"tp_free{(self.tp - 1) % 2}"]

            @contextmanager
            def loop(self, n, per):
                pos, u, b, tp = self.pos, self.u, self.b, self.tp
                with self.c.loop(n, per) as i:
                    yield i
                    assert self.u - u == SPLIT and self.pos - pos == SPLIT and (self.b - b) % 2 == 0 and (self.tp - tp) % 2 == 0
                self.pos, self.u = self.pos + SPLIT * (n - 1), self.u + SPLIT * (n - 1)

        def tile(b, h, k, dyn):
            at = FT * h + 2 * b + k
            return slice(at, at + 1) if dyn is None else bass.ds(dyn * 4 + at, 1)

        @block.scalar
        def _(act):
            e = Side(act)
            c = e.c

            def phase():
                act.drain().then_inc(sem["phase_done"], 1)
                act.wait_ge(sem["phase_done"], c.next("phase_done", 4))

            def split(n):
                for _ in range(min(n, NUNITS - e.u)):
                    (unit, land), s = arrival(e.u), e.u % SPLIT
                    act.wait_ge(sem[land], c.next(land, 16))
                    if e.u >= SPLIT:
                        act.wait_ge(sem["unit_done"], e.turn() + (e.u + 1 - SPLIT))
                    act.activation(w_hi[:, s, :], unit, ACT.Copy).then_inc(sem["hi_ready"], 1)
                    e.u += 1


            def squares(src, junk, ready="res_ready", k=1):
                act.wait_ge(sem[ready], c.next(ready, k))
                for t in range(NT):
                    last = act.activation(junk[:, t, :], src[:, t, :], ACT.Square, accum_out=SS[:, t:t + 1])
                last.then_inc(sem["ss_ready"], 1)
                root(2)

            def root(n, dst=None, at=0):
                act.wait_ge(sem["rs_pre"], c.next("rs_pre"))
                act.activation(RS[:, at:at + n] if dst is None else dst, RS[:, at:at + n], ACT.Sqrt) \
                    .then_inc(sem["rs_ready"], 1)

            def raw_features():
                e.skip_turns(4)
                for g in range(KT // 2):
                    act.wait_ge(sem["tf_ready"], c.next("tf_ready"))
                    act.activation(HA_hi[:, 2 * g:2 * g + 2, :].rearrange("p k n -> p (k n)"), TF[:, g % 2, :],
                                   ACT.Copy).then_inc(sem["hi_feat"], 1)
                act.wait_ge(sem["x_half"], c.next("x_half", 2))
                for t in range(NT):
                    last = act.activation(XN[:, t, :], X[:, t, :], ACT.Square, accum_out=SS[:, t:t + 1])
                last.then_inc(sem["ss_ready"], 1)
                root(2, dst=RN)
                act.drain()

            def row_squares(s):
                act.wait_ge(sem["res_ready"], c.next("res_ready"))
                for t in range(NT):
                    act.drain()
                    last = act.activation(JUNK[:, :], (XC if s else X)[:, t, :], ACT.Square,
                                          accum_out=SS[:, 2 * s + t:2 * s + t + 1])
                last.then_inc(sem["ss_ready"], 1)
                root(2, at=2 * s)

            def modulated(l, w, s):
                hi = HB_hi if s and w == 0 else HA_hi
                e.skip_turns(4)
                for g in range(KT // 2):
                    act.wait_ge(sem["tf_ready"], c.next("tf_ready"))
                    for k in range(2):
                        last = act.activation(hi[:, 2 * g + k, :], TF[:, g % 2, T * k:T * k + T], ACT.Identity,
                                              bias=MODC[:, l, 2 * w, 2 * g + k, s:s + 1])
                    last.then_inc(sem["hi_feat"], 1)

            def feature_hi(dst):
                act.wait_ge(sem["tp_ready"], c.next("tp_ready"))
                bank = e.bank()
                act.activation(dst, bank[:, :].rearrange("p (k n) -> p k n", n=T), ACT.Copy).then_inc(sem["hi_feat"], 1)

            def features_plain(hi):
                for g in range(KT // 2):
                    feature_hi(hi[:, 2 * g:2 * g + 2, :])

            def swiglu(first=False):
                raw_features()
                if first:
                    split(2)

                def gate(b):
                    act.wait_ge(sem["unit_done"], e.reached())
                    acc = e.pair()
                    for t in range(NT):
                        last = act.activation(HID[:, b % 2, t, :], acc[:, t, 0:256], ACT.Silu, scale=RN[:, t:t + 1])
                    last.then_inc(sem["sil_ready"], 1)

                gate(0)
                split(2)
                with e.loop(5, {"land0": 32, "land1": 32, "tp_ready": 2}) as i:
                    for b in (1, 2):
                        gate(b)
                        feature_hi(FT_hi[:, bass.ds(i * 4 + 2 * (b - 1), 2), :])
                        split(2)
                feature_hi(FT_hi[:, 20:22, :])
                split(11)
                e.skip(11, 2)

            def evacuate(dst, name, func=ACT.Identity, width=512):
                act.wait_ge(sem["unit_done"], e.reached())
                acc = e.pair()
                for t in range(NT):
                    last = act.activation(dst[:, t, :], acc[:, t, 0:width], func, scale=RN[:, t:t + 1])
                last.then_inc(sem[name], 1)
                act.drain().then_inc(e.acc_free(), 1)
                split(2)

            def cols(t, j):
                return t[:, :, 512 * j:512 * j + 512]

            def mixer(l):
                raw_features()
                w = SHIFT[l] - 3 * D
                evacuate(LOR[:, :, 0:w], "p_ready", width=w)
                evacuate(cols(R, 0), "p_ready")
                evacuate(cols(R, 1), "p_ready")
                act.wait_ge(sem["mix_done"], c.next("mix_done"))
                act.activation(LOR[:, :, 0:LORA], LOR[:, :, 0:LORA], ACT.Tanh).then_inc(sem["lora_tanh"], 1)
                c.next("mix_done", 6)
                evacuate(cols(K, 0), "p_ready")
                act.wait_ge(sem["tp_ready"], c.next("tp_ready"))
                bank = e.bank()
                for part in range(2):
                    rows = slice(LORA * part, LORA * part + LORA)
                    last = act.activation(LORT[rows, part, :], bank[rows, 0:T], ACT.Copy)
                if l:
                    last = act.activation(LORT[0:MV, 2, :], bank[0:MV, T:2 * T], ACT.Copy)
                last.then_inc(sem["lora_tr"], 1)
                act.drain().then_inc(e.tp_free(), 1)
                evacuate(cols(K, 1), "p_ready")
                evacuate(cols(V, 0), "p_ready")
                evacuate(cols(V, 1), "p_ready")
                for src, name in ([(KK, "vsig_ready")] if l else []) + [(T1, "sig_ready"), (AA, "asig_ready")]:
                    for t in range(NT):
                        act.wait_ge(sem["pre_ready"], c.next("pre_ready"))
                        act.activation(src[:, t, :], src[:, t, :], ACT.Sigmoid).then_inc(sem[name], 1)
                        c.next("acc_ready")
                        e.b += 1
                root(32)
                n = 0
                for t in range(NT):
                    for signs in ((1.0,), (1.0, -1.0)):
                        act.wait_ge(sem["acc_ready"], c.next("acc_ready"))
                        acc = e.pair()
                        for sign in signs:
                            act.wait_ge(sem["exp_used"], c.next("exp_used"))
                            act.activation(T2[:, n % 2, :], acc[:, :, :].rearrange("p t n -> p (t n)"), ACT.Exp,
                                           scale=sign).then_inc(sem["exp_ready"], 1)
                            n += 1
                        act.drain().then_inc(e.acc_free(), 1)
                act.wait_ge(sem["gam_ready"], c.next("gam_ready"))
                act.activation(GAM[:, :], M[0][:, 0:32], ACT.Exp)
                phase()
                for g in range(2):
                    for t in range(NT):
                        for p in range(4):
                            act.wait_ge(sem["tp_ready"], c.next("tp_ready"))
                            bank = e.bank()
                            act.activation(AR[:, p, :, :].rearrange("p a n -> p (a n)"), bank[:, 0:256], ACT.Copy)
                            for hb in range(2):
                                rows = slice(HD * hb, HD * hb + HD)
                                last = act.activation(BK[rows, p % 2, hb, :, :].rearrange("p a n -> p (a n)"),
                                                      bank[rows, 256:512], ACT.Copy)
                            last.then_inc(sem["arbk_ready"], 1)
                            act.drain().then_inc(e.tp_free(), 1)
                        for p in range(4):
                            act.wait_ge(sem["mv_ready"], c.next("mv_ready"))
                            act.activation(MVY[:, p, :], A4[p][:, 0:256], ACT.Copy).then_inc(sem["mv_copied"], 1)
                        for ch in range(2):
                            rows = slice(CHUNK * ch, CHUNK * ch + CHUNK)
                            for p in range(4):
                                act.wait_ge(sem["uu_ready"], c.next("uu_ready"))
                                act.activation(U[rows, p, ch, :], B4[p][rows, 0:P], ACT.Copy).then_inc(sem["u_copied"], 1)
                phase()
                evacuate(cols(GATE_A, 0), "gate_ready", ACT.Sigmoid)
                root(32)
                evacuate(cols(GATE_A, 1), "gate_ready", ACT.Sigmoid)
                for j in range(2):
                    evacuate(cols(VA, j), "gelu_ready", ACT.Gelu_apprx_tanh)
                squares(VA, SQ)
                act.wait_ge(sem["gn_done"], c.next("gn_done"))
                for j in range(2):
                    evacuate(cols(GATE_B, j), "gate_ready", ACT.Sigmoid)
                features_plain(HB_hi)
                e.b += 2
                c.next("acc_ready", 2)
                for j in range(2):
                    evacuate(cols(UA, j), "gelu_ready", ACT.Gelu_apprx_tanh)
                e.skip(2, 1)
                split(2)
                features_plain(HA_hi)
                for j in range(3):
                    e.skip(2, 1)
                    split(2)
                features_plain(HB_hi)
                for j in range(2):
                    e.skip(2, 1)
                    split(2)

            def modulation():
                for l in range(2):
                    for j in range(12):
                        e.skip(2, 1)
                        split(2)
                e.skip_turns(16)

            def project(l):
                if l:
                    for n in range(3):
                        load_bias(n)
                row_squares(0)
                modulated(l, 0, 0)
                row_squares(1)
                modulated(l, 0, 1)
                for s, part, half, behind in projections(l):
                    turned = False
                    if part == V_PART:
                        act.wait_ge(sem["unit_done"], e.reached())
                        acc = e.pair()
                        act.activation(VV[:, 2 * s:2 * s + 2, 512 * half:512 * half + 512], acc[:, :, :], ACT.Copy)
                        act.drain().then_inc(e.acc_free(), 1)
                        split(2)
                    elif s:
                        if behind == (1, Q_PART):
                            turned = take_turned(*behind)
                        act.wait_ge(sem["unit_done"], e.reached())
                        acc = e.pair()
                        act.activation(cols(XN, half), acc[:, :, :], ACT.Copy)
                        act.drain().then_inc(e.acc_free(), 1)
                        if half:
                            act.drain().then_inc(sem["q_ready"], 1)
                        split(2)
                    else:
                        e.skip(2, 1)
                        split(2)
                    if behind and not turned:
                        take_turned(*behind)

            def take_turned(s, part):
                for g in range(KT // 2):
                    act.wait_ge(sem["tp_ready"], c.next("tp_ready"))
                    bank = e.bank()
                    dst = (QTC if s else QTX)[:, 2 * g:2 * g + 2, :] if part == Q_PART else \
                        KTT[:, 2 * g:2 * g + 2, T * s:T * s + T]
                    act.activation(dst, bank[:, :].rearrange("p (k n) -> p k n", n=T), ACT.Copy)
                    act.drain().then_inc(e.tp_free(), 1)
                return True

            def load_bias(n):
                q, hp = n // 8, n % 8
                for r in range(2):
                    dy = 3 - (2 * q + r)
                    act.dma_start(BIAS[64 * r:64 * r + 64, n % 3, :, :],
                                  toe[hp, :, :, dy:dy + 4, :].rearrange("q h k c -> q h (k c)")) \
                        .then_inc(sem[f"bias{n % 3}"], 16)

            def attend(l, s):
                nk = 4 if s == 0 else 2
                at = 0

                def exps(n):
                    st0 = 8 * (n % 2)
                    for hb in range(2):
                        act.wait_ge(sem["max_ready"], c.next("max_ready"))
                        src = A4[2 * (n % 2) + hb][:, 0:nk * P] if l == 0 else SC[:, n % 2, hb, :]
                        act.activation(PR[:, n % 2, hb, 0:nk * P], src, ACT.Exp,
                                       bias=ST[:, st0 + 2 + hb:st0 + 3 + hb], scale=SCALE if l == 0 else 1.0,
                                       accum_out=ST[:, st0 + 4 + hb:st0 + 5 + hb]).then_inc(sem["prob_ready"], 1)
                        if l == 0:
                            act.drain().then_inc(sem["sc_free"], 1)

                def outputs(n):
                    q, hp = n // 8, n % 8
                    w = P if l == 0 else HD
                    act.wait_ge(sem["o_ready"], c.next("o_ready"))
                    for hb in range(1 if l == 0 else 2):
                        dst = XN[:, q, P * hp + w * hb:P * hp + w * hb + w]
                        src = M[n % 2][:, w * hb:w * hb + w]
                        if l == 0:
                            act.activation(OUTJ[:, :], src, ACT.Square, accum_out=SS[:, n:n + 1])
                            act.activation(dst, src, ACT.Copy).then_inc(sem["o_copied"], 1)
                        else:
                            k = 32 + 2 * (n % 4) + hb
                            act.activation(dst, src, ACT.Identity, scale=ST[:, k:k + 1]).then_inc(sem["o_copied"], 1)
                    act.drain().then_inc(sem["o_free"], 1)

                def queries(n):
                    q, hp = n // 8, n % 8
                    for hb in range(2):
                        rows = slice(HD * hb, HD * hb + HD)
                        last = act.activation(QZ[rows, n % 2, hb, :], (QTC if s else QTX)[rows, hp, P * q:P * q + P],
                                              ACT.Copy)
                    last.then_inc(sem["qz_ready"], 1)

                queries(0)
                queries(1)
                exps(0)
                queries(2)
                for n in range(17):
                    if n < 15:
                        exps(n + 1)
                    if n < 13:
                        queries(n + 3)
                        if l:
                            act.wait_ge(sem["bias_free"], c.next("bias_free"))
                            load_bias(n + 3)
                    if n:
                        outputs(n - 1)
                    for hb in range((1 if l == 0 else 2) if n < 16 else 0):
                        act.wait_ge(sem["tp_ready"], c.next("tp_ready"))
                        bank = e.bank()
                        act.activation(AT[:, at % 2, 0:nk * P], bank[:, 0:nk * P], ACT.Copy) \
                            .then_inc(sem["at_ready"], 1)
                        act.drain().then_inc(e.tp_free(), 1)
                        at += 1
                if l == 0:
                    root(16)
                features_plain(HA_hi)
                for j in range(2):
                    e.skip(2, 1)
                    split(2)

            def conv_ffn(l, s):
                row_squares(s)
                modulated(l, 1, s)
                if s == 0:
                    act.wait_ge(sem["cw_land"], c.next("cw_land", 16))

                def up(b):
                    act.wait_ge(sem["unit_done"], e.reached())
                    acc = e.pair()
                    act.activation(US[:, b % 2, :, :], acc[:, :, :], ACT.Copy).then_inc(sem["u_copy"], 1)
                    act.drain().then_inc(e.acc_free(), 1)

                def conv(b, dyn=None):
                    for h in range(2):
                        act.wait_ge(sem["tp_ready"], c.next("tp_ready"))
                        bank = e.bank()
                        for k in range(2):
                            col = tile(b, h, k, dyn)
                            last = act.activation(CV[:, b % 2, 2 * h + k, :], bank[:, T * k:T * k + T], ACT.Identity,
                                                  scale=CW[:, 1, col], bias=CW[:, 3, col])
                        last.then_inc(sem["cv_ready"], 1)

                def gate(b, dst):
                    act.wait_ge(sem["cv_conv"], c.next("cv_conv"))
                    g = CV[:, b % 2, 2:4, :]
                    act.activation(g, g, ACT.Silu).then_inc(sem["sg_ready"], 1)
                    act.wait_ge(sem["hv_ready"], c.next("hv_ready"))
                    act.activation(dst, HV[:, b % 2, :, :], ACT.Copy).then_inc(sem["hi_feat"], 1)

                up(0)
                split(2)
                with e.loop(5, {"land0": 32, "land1": 32, "tp_ready": 4, "cv_conv": 2, "hv_ready": 2}) as i:
                    for b in (1, 2):
                        up(b)
                        conv(b - 1, i)
                        split(2)
                        gate(b - 1, FT_hi[:, bass.ds(i * 4 + 2 * (b - 1), 2), :])
                split(2)
                conv(10)
                split(1)
                gate(10, FT_hi[:, 20:22, :])
                split(8)
                e.skip(11, 2)

            act.wait_ge(sem["const_land"], c.next("const_land", 32))
            split(2)
            for l in range(2):
                swiglu(first=l == 0)
                mixer(l)
                swiglu()
            act.wait_ge(sem["cc_land"], c.next("cc_land", 16))
            act.activation(CC[:, :], CC_IN[:, :], ACT.Silu)
            act.drain()
            act.activation(HA_hi[:, :, 0:P].rearrange("p k (s n) -> p k s n", s=2),
                           CC[:, :].rearrange("p (k s) -> p k s", s=2).unsqueeze(3).broadcast_to([P, KT, 2, 64]),
                           ACT.Copy).then_inc(sem["cc_hi"], 1)
            squares(X, XN, "x_half", 2)
            phase()
            modulation()
            phase()
            for l in range(2):
                project(l)
                phase()
                if l == 0:
                    act.wait_ge(sem["lam_ready"], c.next("lam_ready"))
                    act.activation(ST[:, 20:22], ST[:, 18:20], ACT.Exp).then_inc(sem["lam_exp"], 1)
                for s in range(2 - l):
                    attend(l, s)
                    phase()
                for s in range(2 - l):
                    conv_ffn(l, s)
                    phase()
            squares(X, XN)

        @block.vector
        def _(dve):
            e = Side(dve)
            c = e.c

            def phase():
                dve.drain().then_inc(sem["phase_done"], 1)
                dve.wait_ge(sem["phase_done"], c.next("phase_done", 4))

            def split(n):
                for _ in range(min(n, NUNITS - e.u)):
                    (unit, _), s = arrival(e.u), e.u % SPLIT
                    dve.wait_ge(sem["hi_ready"], c.next("hi_ready"))
                    dve.tensor_tensor(w_lo[:, s, :], unit, w_hi[:, s, :].bitcast(F32),
                                      ALU.subtract).then_inc(sem["lo_ready"], 1)
                    e.u += 1

            tt, ts, stt = dve.tensor_tensor, dve.tensor_scalar, dve.scalar_tensor_tensor
            vec = {"n": 0}

            def vector():
                s = vec["n"] % 2
                vec["n"] += 1
                dve.wait_ge(sem[f"bc{s}"], c.next(f"bc{s}", 16))
                return BC[:, s, :]

            def cols(t, j):
                return t[:, :, 512 * j:512 * j + 512]

            def both(v):
                return v.unsqueeze(1).broadcast_to([P, NT, D])

            def per_head(v, n, d):
                return v.unsqueeze(2).broadcast_to([P, n, d])

            def rates(n, width=1.0, eps=0.0, floor=None, at=0):
                rs, ss = RS[:, at:at + n], SS[:, at:at + n]
                if floor is None:
                    ts(rs, ss, 1.0 / width, eps, ALU.mult, ALU.add)
                else:
                    ts(rs, ss, floor, None, ALU.max)
                dve.drain()
                dve.reciprocal(rs, rs).then_inc(sem["rs_pre"], 1)

            def feature_lo(dst, dst_hi):
                c.next("tp_ready")
                dve.wait_ge(sem["hi_feat"], c.next("hi_feat"))
                bank = e.bank()
                tt(dst, bank[:, :].rearrange("p (k n) -> p k n", n=T), dst_hi.bitcast(F32), ALU.subtract) \
                    .then_inc(sem["feat_ready"], 1)
                dve.drain().then_inc(e.tp_free(), 1)

            def features_plain(hi, lo):
                for g in range(KT // 2):
                    feature_lo(lo[:, 2 * g:2 * g + 2, :], hi[:, 2 * g:2 * g + 2, :])

            def features_scaled(hi, lo, scaled, rest):
                def low(g):
                    dve.wait_ge(sem["hi_feat"], c.next("hi_feat"))
                    rest(g).then_inc(sem["feat_ready"], 1)

                for g in range(KT // 2):
                    dve.wait_ge(sem["tp_ready"], c.next("tp_ready"))
                    bank = e.bank()
                    for k in range(2):
                        last = scaled(TF[:, g % 2, T * k:T * k + T], bank[:, T * k:T * k + T], 2 * g + k)
                    last.then_inc(sem["tf_ready"], 1)
                    dve.drain().then_inc(e.tp_free(), 1)
                    if g:
                        low(g - 1)
                        dve.drain()
                low(KT // 2 - 1)

            def raw_features(gain):
                features_scaled(
                    HA_hi, HA_lo, lambda dst, src, f: ts(dst, src, COL[:, gain + f:gain + f + 1], None, ALU.mult),
                    lambda g: tt(HA_lo[:, 2 * g:2 * g + 2, :].rearrange("p k n -> p (k n)"), TF[:, g % 2, :],
                                 HA_hi[:, 2 * g:2 * g + 2, :].rearrange("p k n -> p (k n)").bitcast(F32),
                                 ALU.subtract))
                dve.wait_ge(sem["ss_ready"], c.next("ss_ready"))
                rates(2, D, NORM_EPS)
                dve.wait_ge(sem["rs_ready"], c.next("rs_ready"))

            def swiglu(gain, first=False):
                raw_features(gain)
                if first:
                    split(2)

                def hidden(b):
                    dve.wait_ge(sem["unit_done"], e.reached())
                    acc = e.pair()
                    dve.wait_ge(sem["sil_ready"], c.next("sil_ready"))
                    for t in range(NT):
                        h = HID[:, b % 2, t, :]
                        last = stt(h, acc[:, t, 256:512], RN[:, t:t + 1], h, ALU.mult, ALU.mult)
                    last.then_inc(sem["hid_ready"], 1)
                    dve.drain().then_inc(e.acc_free(), 1)

                hidden(0)
                split(2)
                with e.loop(5, {"hi_ready": 4, "sil_ready": 2, "hi_feat": 2, "tp_ready": 2}) as i:
                    for b in (1, 2):
                        hidden(b)
                        f = bass.ds(i * 4 + 2 * (b - 1), 2)
                        feature_lo(FT_lo[:, f, :], FT_hi[:, f, :])
                        split(2)
                feature_lo(FT_lo[:, 20:22, :], FT_hi[:, 20:22, :])
                split(11)
                e.pos += 11
                for n in range(2):
                    x = cols(X, n)
                    dve.wait_ge(sem["unit_done"], e.reached(0))
                    acc = e.pair()
                    stt(x, acc[:, :, :], 0.5, x, ALU.mult, ALU.add).then_inc(e.acc_free(), 1)
                    dve.drain().then_inc(sem["x_half"], 1)

            def to_feat(v):
                return v.rearrange("p t n -> p (t n)")

            def prepare(l):
                for dst, name in ([(KK, 0)] if l else []) + [(T1, 1), (AA, 2)]:
                    v = vector()
                    for t in range(NT):
                        dve.wait_ge(sem["acc_ready"], c.next("acc_ready"))
                        acc = e.pair()
                        tt(dst[:, t, :], to_feat(acc[:, :, :]), v, ALU.add).then_inc(sem["pre_ready"], 1)
                        dve.drain().then_inc(e.acc_free(), 1)
                    dve.drain().then_inc(sem["bc_free"], 1)
                if l:
                    dve.wait_ge(sem["vf_land"], c.next("vf_land", 16))
                    dve.wait_ge(sem["vsig_ready"], c.next("vsig_ready", 2))
                    tt(whole(VF), whole(VF), whole(V), ALU.subtract)
                    dve.drain()
                    tt(whole(VF), whole(VF), whole(KK), ALU.mult)
                    dve.drain()
                    tt(whole(V), whole(V), whole(VF), ALU.add)
                    dve.drain()
                else:
                    dve.drain().then_inc(sem["v_final"], 1)
                v = vector()
                tt(KK[:, :, :], K[:, :, :], both(v), ALU.mult)
                dve.drain().then_inc(sem["bc_free"], 1)
                tt(whole(T2), whole(KK), whole(KK), ALU.mult)
                dve.drain()
                dve.tensor_reduce(SS[:, :], heads(T2), AX.X, ALU.add)
                dve.drain()
                rates(32, floor=1e-24)
                v = vector()
                dve.wait_ge(sem["asig_ready"], c.next("asig_ready", 2))
                stt(T2[:, :, :], AA[:, :, :], -1.0, both(v), ALU.add, ALU.mult)
                dve.drain().then_inc(sem["bc_free"], 1)
                stt(whole(K), whole(T2), 1.0, whole(K), ALU.add, ALU.mult)
                dve.wait_ge(sem["rs_ready"], c.next("rs_ready"))
                tt(heads(KK), heads(KK), per_head(RS[:, :], 32, HD), ALU.mult)
                v = vector()
                dve.drain()
                tt(T2[:, :, :], R[:, :, :], both(v), ALU.mult)
                dve.drain().then_inc(sem["bc_free"], 1)
                tt(whole(AA), whole(AA), whole(KK), ALU.mult)
                tt(whole(T2), whole(T2), whole(K), ALU.mult)
                dve.drain()
                dve.tensor_reduce(BN[:, :, :].rearrange("p t h -> p (t h)"), heads(T2), AX.X, ALU.add)
                dve.drain().then_inc(sem["exp_used"], 2)
                for z in (BK[:, :, :, :, :].rearrange("p s h a n -> p (s h a n)"),
                          VZ[:, :, :, :].rearrange("p q c n -> p (q c n)"),
                          U[:, :, :, :].rearrange("p q c n -> p (q c n)")):
                    dve.memset(z, 0.0)
                n = 0

                def factor():
                    nonlocal n
                    dve.wait_ge(sem["exp_ready"], c.next("exp_ready"))
                    n += 1
                    return T2[:, (n - 1) % 2, :]

                for t in range(NT):
                    w = factor()
                    stt(KK[:, t, :], KK[:, t, :], -1.0, w, ALU.mult, ALU.mult).then_inc(sem["exp_used"], 1)
                    w = factor()
                    last = tt(R[:, t, :], R[:, t, :], w, ALU.mult)
                    if t == 0:
                        last.then_inc(sem["exp_used"], 1)
                    w = factor()
                    tt(AA[:, t, :], AA[:, t, :], w, ALU.mult)
                    last = tt(K[:, t, :], K[:, t, :], w, ALU.mult)
                    if t == 0:
                        last.then_inc(sem["exp_used"], 1)

            def mask(col, n):
                return K_[:, col:col + P].unsqueeze(1).broadcast_to([P, n, P])

            def wkv(g, t):
                if t == 0:
                    dve.drain()
                    dve.memset(S[:, :, :], 0.0)
                    dve.drain().then_inc(sem["s_zero"], 1)
                for n in range(8):
                    dve.wait_ge(sem["gram_ready"], c.next("gram_ready"))
                    tt(LG[:, n, :].rearrange("p (a n) -> p a n", a=2), M[n % 2][:, :].rearrange("p (a n) -> p a n", a=2),
                       K_[:, C_GRAM:C_GRAM + 256].unsqueeze(1).broadcast_to([P, 2, 256]), ALU.mult) \
                        .then_inc(sem["lg_ready"], 1)
                e.tp += 4
                c.next("tp_ready", 4)
                dve.drain()
                for p in range(4):
                    tt(XX[:, p, :, 1, :], LG[:, 2 * p:2 * p + 2, 0:P], mask(C_LEVEL0T, 2), ALU.mult)
                dve.drain()
                for p in range(4):
                    tt(XX[:, p, :, 1, :], XX[:, p, :, 1, :], mask(C_ID, 2), ALU.add)
                for p in range(4):
                    dve.wait_ge(sem["t_ready"], c.next("t_ready"))
                    tt(XX[:, p, :, 0, :], A4[p][:, 0:256].rearrange("p (h n) -> p h n", h=2), mask(C_LEVEL, 2), ALU.mult) \
                        .then_inc(sem["x_ready"], 1)
                for j in range(1, 6):
                    for p in range(4):
                        dve.wait_ge(sem["t_ready"], c.next("t_ready"))
                        tt(TM[:, p, :].rearrange("p (h n) -> p h n", h=2),
                           A4[p][:, 0:256].rearrange("p (h n) -> p h n", h=2), mask(C_LEVEL + P * j, 2), ALU.mult) \
                            .then_inc(sem["t_masked"], 1)
                    for p in range(4):
                        dve.wait_ge(sem["u_ready"], c.next("u_ready"))
                        if j < 5:
                            x = XX[:, p, :, :, :].rearrange("p h a n -> p (h a n)")
                            tt(x, x, B4[p], ALU.add).then_inc(sem["x_ready"], 1)
                        else:
                            x = XX[:, p, :, 1, :]
                            tt(x, x, B4[p].rearrange("p (h a n) -> p h a n", h=2, a=2)[:, :, 1, :], ALU.add) \
                                .then_inc(sem["x_ready"], 1)
                for ch in range(2):
                    rows = slice(CHUNK * ch, CHUNK * ch + CHUNK)
                    for p in range(4):
                        dve.wait_ge(sem["pp_ready"], c.next("pp_ready"))
                        tt(PM[rows, p, :], A4[p][rows, 0:P], MVY[rows, p, 0:P], ALU.add).then_inc(sem["pm_ready"], 1)
                    for p in range(4):
                        q = 4 * g + p
                        dve.wait_ge(sem["sy_ready"], c.next("sy_ready"))
                        gam = GAM[:, 4 * q + 2 * t + ch:4 * q + 2 * t + ch + 1]
                        stt(SU[:, p, :], B4[p][:, P:2 * P], gam, K_[:, C_BD:C_BD + P], ALU.mult, ALU.mult)
                        tt(R[rows, t, P * q:P * q + P], A4[p][rows, P:2 * P], MVY[rows, p, P:2 * P], ALU.add) \
                            .then_inc(sem["y_done"], 1)
                        dve.drain()
                        stt(S[:, p, :], S[:, p, :], gam, SU[:, p, :], ALU.mult, ALU.add).then_inc(sem["s_done"], 1)

            def pass_block():
                e.skip(2, 1)
                split(2)

            def group_norm():
                dve.tensor_reduce(SS[:, :], heads(R), AX.X, ALU.add)
                dve.drain()
                ts(RS[:, :], SS[:, :], -1.0 / HD, None, ALU.mult)
                dve.drain()
                tt(heads(R), heads(R), per_head(RS[:, :], 32, HD), ALU.add)
                dve.drain()
                tt(whole(T1), whole(R), whole(R), ALU.mult)
                dve.drain()
                dve.tensor_reduce(SS[:, :], heads(T1), AX.X, ALU.add)
                dve.drain()
                pass_block()
                rates(32, HD, GN_EPS)
                dve.wait_ge(sem["rs_ready"], c.next("rs_ready"))
                tt(heads(R), heads(R), per_head(RS[:, :], 32, HD), ALU.mult)
                v = vector()
                dve.drain()
                tt(R[:, :, :], R[:, :, :], both(v), ALU.mult)
                dve.drain().then_inc(sem["bc_free"], 1)
                pass_block()
                v = vector()
                tt(R[:, :, :], R[:, :, :], both(v), ALU.add)
                dve.drain().then_inc(sem["bc_free"], 1)
                dve.wait_ge(sem["bonus_ready"], c.next("bonus_ready"))
                tt(whole(R), whole(R), whole(SQ), ALU.add)
                dve.drain().then_inc(sem["gn_done"], 1)
                dve.drain().then_inc(sem["r_done"], 1)

            def mixer(l):
                raw_features(G_MIX + 8 * l)
                dve.memset(LORT[:, :, :], 0.0)
                dve.wait_ge(sem["mu_land"], c.next("mu_land", 16))
                for n in range(7):
                    e.skip(2, 1)
                    split(2)
                    p_, w, mu = shifted(l, n)
                    prev, dif = PREV[:, n % 2, :, 0:w], DIF[:, :, 0:w]
                    dve.wait_ge(sem[f"shift{n % 2}"], c.next(f"shift{n % 2}", 48))
                    tt(dif, prev, p_, ALU.subtract)
                    dve.drain()
                    tt(dif, dif, MU[:, mu:mu + w].unsqueeze(1).broadcast_to([P, NT, w]), ALU.mult)
                    dve.drain()
                    tt(p_, p_, dif, ALU.add)
                    dve.drain().then_inc(sem["mix_done"], 1)
                e.skip_turns(1)
                prepare(l)
                e.b += 4
                c.next("acc_ready", 4)
                phase()
                for g in range(2):
                    for t in range(NT):
                        wkv(g, t)
                phase()
                group_norm()
                dve.wait_ge(sem["wst_land"], c.next("wst_land", 16))
                tt(WST[:, :, :], WST[:, :, :], mask(C_TRIU, 8), ALU.mult)
                pass_block()
                pass_block()
                dve.wait_ge(sem["gelu_ready"], c.next("gelu_ready", 2))
                dve.tensor_reduce(ST[:, 0:2], VA[:, :, :], AX.X, ALU.add)
                dve.drain()
                ts(ST[:, 2:4], ST[:, 0:2], -1.0 / D, None, ALU.mult)
                dve.drain()
                for t in range(NT):
                    ts(VA[:, t, :], VA[:, t, :], ST[:, 2 + t:3 + t], None, ALU.add)
                dve.drain().then_inc(sem["res_ready"], 1)
                dve.wait_ge(sem["ss_ready"], c.next("ss_ready"))
                rates(2, D, LN_EPS)
                pass_block()
                v = vector()
                dve.wait_ge(sem["rs_ready"], c.next("rs_ready"))
                for t in range(NT):
                    stt(VA[:, t, :], VA[:, t, :], RS[:, t:t + 1], v, ALU.mult, ALU.mult)
                dve.drain().then_inc(sem["bc_free"], 1)
                v = vector()
                tt(VA[:, :, :], VA[:, :, :], both(v), ALU.add)
                dve.drain().then_inc(sem["bc_free"], 1)
                dve.drain().then_inc(sem["va_ready"], 1)
                pass_block()
                features_plain(HB_hi, HB_lo)
                bs = COL[:, G_BS + 8 * l:G_BS + 8 * l + 8]
                for t in range(NT):
                    dve.wait_ge(sem["acc_ready"], c.next("acc_ready"))
                    acc = e.pair()
                    tt(SQ[:, t, :].rearrange("p (g d) -> p g d", g=8),
                       to_feat(acc[:, :, :]).rearrange("p (g d) -> p g d", g=8), per_head(bs, 8, P), ALU.add)
                    dve.drain().then_inc(e.acc_free(), 1)
                pass_block()
                pass_block()
                dve.wait_ge(sem["gelu_ready"], c.next("gelu_ready", 2))
                tt(whole(VA), whole(SQ), whole(UA), ALU.mult)
                dve.drain().then_inc(sem["xn_ready"], 1)
                dve.wait_ge(sem["gate_ready"], c.next("gate_ready", 4))
                for j in range(2):
                    dve.wait_ge(sem["unit_done"], e.reached())
                    acc = e.pair()
                    tt(cols(MERG, j), acc[:, :, :], cols(GATE_B, j), ALU.mult).then_inc(e.acc_free(), 1)
                    split(2)
                    if j == 0:
                        features_plain(HA_hi, HA_lo)
                for j in range(2):
                    dve.wait_ge(sem["unit_done"], e.reached())
                    acc = e.pair()
                    tt(cols(SQ, j), acc[:, :, :], cols(GATE_A, j), ALU.mult).then_inc(e.acc_free(), 1)
                    dve.drain()
                    tt(cols(MERG, j), cols(MERG, j), cols(SQ, j), ALU.add)
                    dve.drain().then_inc(sem["merge_done"], 1)
                    split(2)
                features_plain(HB_hi, HB_lo)
                for j in range(2):
                    dve.wait_ge(sem["unit_done"], e.reached())
                    acc = e.pair()
                    x = cols(X, j)
                    tt(x, acc[:, :, :], x, ALU.add).then_inc(e.acc_free(), 1)
                    dve.drain().then_inc(sem["x_half"], 1)
                    split(2)

            def scaled_rows(v, name):
                if name is not None:
                    dve.drain().then_inc(sem["res_ready"], 1)
                dve.wait_ge(sem["ss_ready"], c.next("ss_ready"))
                rates(2, D, NORM_EPS)
                dve.wait_ge(sem["rs_ready"], c.next("rs_ready"))
                for t in range(NT):
                    stt((X if name is None else XN)[:, t, :], X[:, t, :], RS[:, t:t + 1], v, ALU.mult, ALU.mult)

            def modulation():
                for l in range(2):
                    for m in range(6):
                        if (l, m) in ((0, 4), (1, 1), (1, 4)):
                            dve.wait_ge(sem["mod_stored"], c.next("mod_stored", 32))
                        bias = vector()
                        for j in range(2):
                            dve.wait_ge(sem["unit_done"], e.reached())
                            acc = e.pair()
                            tt(XN[:, m % 2, 512 * j:512 * j + 512], acc[:, 0, :], bias[:, 512 * j:512 * j + 512], ALU.add) \
                                .then_inc(sem["modg_ready" if m in (2, 5) else "mod_ready"], 1)
                            dve.drain().then_inc(e.acc_free(), 1)
                            split(2)
                        dve.drain().then_inc(sem["bc_free"], 1)
                        if m in (2, 5):
                            continue
                        for h in range(2):
                            dve.wait_ge(sem["tp_ready"], c.next("tp_ready"))
                            bank = e.bank()
                            dve.tensor_copy(MODC[:, l, (0, 1, None, 2, 3)[m], 4 * h:4 * h + 4, :],
                                            bank[:, :].rearrange("p (k s n) -> p k s n", k=4, s=2)[:, :, :, 0])
                            dve.drain().then_inc(e.tp_free(), 1)
                for l in range(2):
                    for w, gain in enumerate((G_NMIX, G_NFFN)):
                        g = COL[:, gain + 8 * l:gain + 8 * l + 8]
                        stt(MODS[:, l, w, :, :], MODC[:, l, 2 * w + 1, :, :], 1.0, per_head(g, KT, 2), ALU.add, ALU.mult)
                dve.drain()

            def modulated(l, w, s):
                dve.wait_ge(sem["ss_ready"], c.next("ss_ready"))
                rates(2, D, NORM_EPS, at=2 * s)
                dve.wait_ge(sem["rs_ready"], c.next("rs_ready"))
                for t in range(NT):
                    ts(DIAG[:, t, :], ident(), RS[:, 2 * s + t:2 * s + t + 1], None, ALU.mult)
                dve.drain().then_inc(sem["diag_ready"], 1)
                dve.wait_ge(sem["rb_ready"], c.next("rb_ready"))
                dve.tensor_copy(RB[:, s, :], M[s][:, 0:T])
                dve.drain()
                hi, lo = (HB_hi, HB_lo) if s and w == 0 else (HA_hi, HA_lo)

                def rest(g):
                    for k in range(2):
                        f = 2 * g + k
                        last = stt(lo[:, f, :], TF[:, g % 2, T * k:T * k + T], MODC[:, l, 2 * w, f, s:s + 1],
                                   hi[:, f, :].bitcast(F32), ALU.add, ALU.subtract)
                    return last

                features_scaled(hi, lo, lambda dst, src, f: stt(dst, src, MODS[:, l, w, f, s:s + 1], RB[:, s, :],
                                                                ALU.mult, ALU.mult), rest)

            def rotate(acc, j):
                for t in range(NT):
                    src = acc[:, t, :]
                    x = XN[:, t, 512 * j:512 * j + 512]
                    h3 = "p (h x) -> p h x"
                    tt(x.rearrange(h3, x=HD), src.rearrange(h3, x=HD),
                       ROPE[:, 0, t, :].unsqueeze(1).broadcast_to([P, 8, HD]), ALU.mult)
                    for b in range(2):
                        v5 = "p (h a b i) -> p h a b i"
                        tt(QK[:, :].rearrange(v5, a=2, b=2, i=16)[:, :, :, b, :],
                           src.rearrange(v5, a=2, b=2, i=16)[:, :, :, 1 - b, :],
                           ROPE[:, 1, t, :].rearrange("p (a b i) -> p a b i", a=2, b=2)[:, :, b, :].unsqueeze(1)
                           .broadcast_to([P, 8, 2, 16]), ALU.mult)
                    dve.drain()
                    tt(x, x, QK[:, :], ALU.add)
                    dve.drain()

            def project(l):
                dve.drain().then_inc(sem["res_ready"], 2)
                modulated(l, 0, 0)
                modulated(l, 0, 1)
                for j, (s, part, half, behind) in enumerate(projections(l)):
                    if s or part == V_PART:
                        e.skip(2, 1)
                        split(2)
                        continue
                    if (part, half) == (K_PART, 0):
                        dve.wait_ge(sem["tp_ready"], c.next("tp_ready", 4))
                    dve.wait_ge(sem["unit_done"], e.reached())
                    acc = e.pair()
                    if j == 0:
                        split(2)
                    if l == 0:
                        rotate(acc, half)
                    else:
                        dve.tensor_copy(cols(XN, half), acc[:, :, :])
                    dve.drain().then_inc(e.acc_free(), 1)
                    if half:
                        dve.drain().then_inc(sem["q_ready"], 1)
                    if j:
                        split(2)
                e.skip_turns(4 * (3 - l))
                dve.memset(QZ[:, :, :, :], 0.0)

            def attend(l, s):
                nk = 4 if s == 0 else 2
                w = nk * P

                def peak(n):
                    st0 = 8 * (n % 2)
                    for hb in range(2):
                        dve.wait_ge(sem["sc_ready"], c.next("sc_ready"))
                        src = A4[2 * (n % 2) + hb][:, 0:w]
                        if l:
                            if hb == 0:
                                dve.wait_ge(sem["bias_ready"], c.next("bias_ready"))
                            stt(SC[:, n % 2, hb, 0:T], src[:, 0:T], SCALE, BIAS[:, n % 3, hb, :], ALU.mult, ALU.add)
                            ts(SC[:, n % 2, hb, T:2 * T], src[:, T:2 * T], SCALE, None, ALU.mult)
                            dve.drain().then_inc(sem["sc_free"], 1)
                            if hb:
                                dve.drain().then_inc(sem["bias_free"], 1)
                            src = SC[:, n % 2, hb, :]
                        dve.tensor_reduce(ST[:, st0 + hb:st0 + hb + 1], src, AX.X, ALU.max)
                        dve.drain()
                        ts(ST[:, st0 + 2 + hb:st0 + 3 + hb], ST[:, st0 + hb:st0 + hb + 1], -1.0 if l else -SCALE, None,
                           ALU.mult).then_inc(sem["max_ready"], 1)

                def mix(n):
                    st0, at = 8 * (n % 2), 32 + 2 * (n % 4)
                    dve.wait_ge(sem["prob_ready"], c.next("prob_ready", 2))
                    dve.reciprocal(ST[:, at:at + 2], ST[:, st0 + 4:st0 + 6])
                    if l == 0:
                        dve.drain()
                        ts(ST[:, at + 1:at + 2], ST[:, at + 1:at + 2], ST[:, 16:17], None, ALU.mult)
                        dve.drain()
                        p0, p1 = PR[:, n % 2, 0, 0:w], PR[:, n % 2, 1, 0:w]
                        ts(p1, p1, ST[:, at + 1:at + 2], None, ALU.mult)
                        dve.drain()
                        stt(p0, p0, ST[:, at:at + 1], p1, ALU.mult, ALU.subtract)
                    dve.drain().then_inc(sem["mix_ready"], 1)

                peak(0)
                for n in range(16):
                    if n < 15:
                        peak(n + 1)
                    mix(n)
                e.skip_turns(16 if l == 0 else 32)
                dve.wait_ge(sem["o_copied"], c.next("o_copied", 16 if l == 0 else 32))
                if l == 0:
                    rates(16, P, NORM_EPS)
                    dve.wait_ge(sem["rs_ready"], c.next("rs_ready"))
                    y = whole(XN).rearrange("p (h n) -> p h n", n=P)
                    stt(y, y, 1.0 - LAM_INIT, per_head(RS[:, 0:16], 16, P), ALU.mult, ALU.mult)
                    dve.drain()
                    tt(y, y, SUBL[:, :].unsqueeze(1).broadcast_to([P, 16, P]), ALU.mult)
                dve.drain().then_inc(sem["xn_ready"], 1)
                features_plain(HA_hi, HA_lo)
                g = vector()
                dst = XC if s else X
                for j in range(2):
                    dve.wait_ge(sem["unit_done"], e.reached())
                    acc = e.pair()
                    gated(acc, g, j, dst)
                    split(2)
                dve.drain().then_inc(sem["bc_free"], 1)

            def gated(acc, g, j, dst):
                tt(cols(XN, j), acc[:, :, :], g[:, 512 * j:512 * j + 512].unsqueeze(1).broadcast_to([P, NT, 512]),
                   ALU.mult).then_inc(e.acc_free(), 1)
                dve.drain()
                tt(cols(dst, j), cols(dst, j), cols(XN, j), ALU.add)

            def lam_factor():
                dve.wait_ge(sem["lam_land"], c.next("lam_land", 32))
                tt(LAMB[:, 0:2, :], LAMB[:, 0:4:2, :], LAMB[:, 1:4:2, :], ALU.mult)
                dve.drain()
                dve.tensor_reduce(ST[:, 18:20], LAMB[:, 0:2, :], AX.X, ALU.add).then_inc(sem["lam_ready"], 1)
                dve.wait_ge(sem["lam_exp"], c.next("lam_exp"))
                stt(ST[:, 16:17], ST[:, 20:21], LAM_INIT, ST[:, 21:22], ALU.add, ALU.subtract)
                dve.drain()

            def conv_ffn(l, s, src):
                dve.drain().then_inc(sem["res_ready"], 1)
                modulated(l, 1, s)

                def conv(b, dyn=None):
                    for h in range(2):
                        c.next("tp_ready")
                        dve.wait_ge(sem["cv_ready"], c.next("cv_ready"))
                        bank = e.bank()
                        for k in range(2):
                            col = tile(b, h, k, dyn)
                            y, u = CV[:, b % 2, 2 * h + k, :], bank[:, T * k:T * k + T]
                            stt(y[:, 1:T], u[:, 0:T - 1], CW[:, 0, col], y[:, 1:T], ALU.mult, ALU.add)
                        dve.drain()
                        for k in range(2):
                            col = tile(b, h, k, dyn)
                            y, u = CV[:, b % 2, 2 * h + k, :], bank[:, T * k:T * k + T]
                            stt(y[:, 0:T - 1], u[:, 1:T], CW[:, 2, col], y[:, 0:T - 1], ALU.mult, ALU.add)
                        dve.drain().then_inc(e.tp_free(), 1)
                    dve.drain().then_inc(sem["cv_conv"], 1)

                def gate(b, dst_hi, dst_lo):
                    dve.wait_ge(sem["sg_ready"], c.next("sg_ready"))
                    tt(HV[:, b % 2, :, :], CV[:, b % 2, 0:2, :], CV[:, b % 2, 2:4, :], ALU.mult).then_inc(sem["hv_ready"], 1)
                    dve.wait_ge(sem["hi_feat"], c.next("hi_feat"))
                    tt(dst_lo, HV[:, b % 2, :, :], dst_hi.bitcast(F32), ALU.subtract).then_inc(sem["feat_ready"], 1)

                e.skip(2, 1)
                split(2)
                with e.loop(5, {"hi_ready": 4, "tp_ready": 4, "cv_ready": 4, "sg_ready": 2, "hi_feat": 2}) as i:
                    for b in (1, 2):
                        e.skip(2, 1)
                        conv(b - 1, i)
                        split(2)
                        f = bass.ds(i * 4 + 2 * (b - 1), 2)
                        gate(b - 1, FT_hi[:, f, :], FT_lo[:, f, :])
                split(2)
                conv(10)
                split(1)
                gate(10, FT_hi[:, 20:22, :], FT_lo[:, 20:22, :])
                split(8)
                e.pos += 11
                g = vector()
                for n in range(2):
                    dve.wait_ge(sem["unit_done"], e.reached(0))
                    gated(e.pair(), g, n, src)
                dve.drain().then_inc(sem["bc_free"], 1)

            dve.wait_ge(sem["const_land"], c.next("const_land", 32))
            dve.wait_ge(sem["x_land"], c.next("x_land", 16))
            dve.drain().then_inc(sem["x_half"], 2)
            split(2)
            for l in range(2):
                swiglu(G_FFN1 + 8 * l, first=l == 0)
                mixer(l)
                swiglu(G_FFN2 + 8 * l)
            dve.wait_ge(sem["cc_hi"], c.next("cc_hi"))
            tt(HA_lo[:, :, 0:P].rearrange("p k (s n) -> p k s n", s=2),
               CC[:, :].rearrange("p (k s) -> p k s", s=2).unsqueeze(3).broadcast_to([P, KT, 2, 64]),
               HA_hi[:, :, 0:P].rearrange("p k (s n) -> p k s n", s=2).bitcast(F32), ALU.subtract) \
                .then_inc(sem["cc_ready"], 1)
            v = vector()
            scaled_rows(v, None)
            dve.drain().then_inc(sem["bc_free"], 1)
            phase()
            modulation()
            phase()
            dve.wait_ge(sem["ctx_land"], c.next("ctx_land", 16))
            dve.wait_ge(sem["rope_land"], c.next("rope_land", 16))
            for l in range(2):
                project(l)
                phase()
                if l == 0:
                    lam_factor()
                for s in range(2 - l):
                    attend(l, s)
                    phase()
                for s in range(2 - l):
                    if s == 0:
                        dve.wait_ge(sem["cw_land"], c.next("cw_land", 16))
                    conv_ffn(l, s, XC if s else X)
                    phase()
            v = vector()
            scaled_rows(v, "out")
            dve.drain().then_inc(sem["out_ready"], 1)

        @block.gpsimd
        def _(pool):
            c = Counts(pool, sem)

            def phase():
                pool.drain().then_inc(sem["phase_done"], 1)
                pool.wait_ge(sem["phase_done"], c.next("phase_done", 4))

            n_vec = {"n": 0}

            def vector(src):
                s = n_vec["n"] % 2
                n_vec["n"] += 1
                if n_vec["n"] > 2:
                    pool.wait_ge(sem["bc_free"], c.next("bc_free"))
                pool.dma_start(BC[:, s, :], src).then_inc(sem[f"bc{s}"], 16)

            def shifts(l):
                for n in range(7):
                    src, w, _ = shifted(l, n)
                    dst = PREV[:, n % 2, :, 0:w]
                    pool.wait_ge(sem["p_ready"], c.next("p_ready"))
                    if n >= 2:
                        pool.wait_ge(sem["mix_done"], 7 * l + n - 1)
                    pool.dma_start(dst[1:113], src[0:112]).then_inc(sem[f"shift{n % 2}"], 16)
                    pool.dma_start(dst[113:128], src[112:127]).then_inc(sem[f"shift{n % 2}"], 16)
                    pool.dma_start(dst[0:1, 1, :], src[127:128, 0, :]).then_inc(sem[f"shift{n % 2}"], 16)

            def mixer(l):
                pool.wait_ge(sem["feat_ready"], 46 * l + 15 + 4)
                pool.wait_ge(sem["ss_ready"], 4 * l + 2)
                pool.memset(PREV[0:1, :, 0, :], 0.0).then_inc(sem["zero_ready"], 1)
                pool.wait_ge(sem["zero_ready"], c.next("zero_ready"))
                pool.dma_start(MU[:, 0:SHIFT[l]], mus[l:l + 1, 0:SHIFT[l]].broadcast_to([P, SHIFT[l]])) \
                    .then_inc(sem["mu_land"], 16)
                pool.dma_start(W2A2[:, :], lora_wa[l]).then_inc(sem["param_land"], 16)
                if l:
                    pool.dma_start(V2[:, :], lora_v).then_inc(sem["param_land"], 16)
                order = ([V_V0] if l else []) + [V_W0, V_A0, V_KK, V_KA, V_RK]
                rows = [row(v if v == V_V0 else 10 * l + v) for v in order]
                for r in rows[:2]:
                    vector(r)
                shifts(l)
                pool.wait_ge(sem["mix_done"], c.next("mix_done", 7))
                if l:
                    pool.dma_start(VF[:, :, :], vfirst_scr).then_inc(sem["vf_land"], 16)
                for r in rows[2:]:
                    vector(r)
                if not l:
                    pool.wait_ge(sem["v_final"], c.next("v_final"))
                    pool.dma_start(vfirst_scr, V[:, :, :]).then_inc(sem["v_stored"], 16)
                if not l:
                    pool.wait_ge(sem["v_stored"], c.next("v_stored", 16))
                phase()
                for call in range(4):
                    g, t = call // 2, call % 2
                    if call:
                        pool.wait_ge(sem["s_done"], 32 * l + 8 * call)
                    for ch in range(2):
                        rows = slice(CHUNK * ch, CHUNK * ch + CHUNK)
                        pool.drain()
                        last = pool.tensor_copy(VZ[rows, :, ch, :],
                                                V[rows, t, 512 * g:512 * g + 512].rearrange("p (q n) -> p q n", q=4))
                    last.then_inc(sem["vz_ready"], 1)
                phase()
                pool.dma_start(WST[:, :, :], wst[l]).then_inc(sem["wst_land"], 16)
                vector(row(10 * l + V_GNG))
                vector(row(10 * l + V_GNB))
                pool.tensor_tensor(heads(SQ), heads(V), BN[:, :, :].rearrange("p t h -> p (t h)").unsqueeze(2)
                                   .broadcast_to([P, 32, HD]), ALU.mult).then_inc(sem["bonus_ready"], 1)
                vector(row(10 * l + V_LNG))
                vector(row(10 * l + V_LNB))

            def modulation():
                for l in range(2):
                    for m in range(6):
                        vector(row(V_ADA + 6 * l + m))
                        if m in (2, 5):
                            store(l, m)

            def store(l, m):
                pool.wait_ge(sem["modg_ready"], c.next("modg_ready", 2))
                for s in range(2):
                    pool.dma_start(mod_scr[l, m // 3, s:s + 1, :], XN[64 * s:64 * s + 1, m % 2, :]) \
                        .then_inc(sem["mod_stored"], 16)

            def gate_row(l, w, s):
                return mod_scr[l, w, s:s + 1, :].broadcast_to([P, D])

            def windowed(n):
                pool.wait_ge(sem[f"bias{n % 3}"], c.next(f"bias{n % 3}", 32))
                b = BIAS[:, n % 3, :, :]
                pool.drain()
                pool.tensor_tensor(b, b, WIN[:, :].unsqueeze(1).broadcast_to([P, 2, T]), ALU.add) \
                    .then_inc(sem["bias_ready"], 1)

            def attend(l, s):
                for n in range(16 if l else 0):
                    windowed(n)
                vector(gate_row(l, 0, s))

            for name, k in (("acc_free0", 1), ("acc_free1", 1), ("tp_free0", 1), ("tp_free1", 1), ("sc_free", 4), ("o_free", 2)):
                pool.sem_inc(sem[name], k)
            pool.dma_start(X[:, :, :], x_in.rearrange("a (t p) d -> p (a t) d", p=P)).then_inc(sem["x_land"], 16)
            pool.dma_start(K_[:, :], consts).then_inc(sem["const_land"], 16)
            pool.dma_start(COL[:, :], cols).then_inc(sem["const_land"], 16)
            pool.dma_start(CC_IN[:, :], cc).then_inc(sem["cc_land"], 16)
            for l in range(2):
                mixer(l)
            vector(row(V_FINAL))
            phase()
            pool.dma_start(XC[:, :, :], ctx_in.rearrange("a (t p) d -> p (a t) d", p=P)).then_inc(sem["ctx_land"], 16)
            pool.dma_start(ROPE[:, :, :, :], rope).then_inc(sem["rope_land"], 16)
            modulation()
            pool.wait_ge(sem["mod_stored"], c.next("mod_stored", 64 + 64))
            phase()
            for l in range(2):
                if l:
                    pool.dma_start(WIN[:, :], window).then_inc(sem["win_land"], 16)
                    pool.wait_ge(sem["win_land"], c.next("win_land", 16))
                phase()
                if l == 0:
                    pool.dma_start(LAMB[:, :, :], lam).then_inc(sem["lam_land"], 16)
                    pool.dma_start(SUBL[:, :], subln).then_inc(sem["lam_land"], 16)
                for s in range(2 - l):
                    attend(l, s)
                    phase()
                pool.dma_start(CW[:, :, :], convw[l]).then_inc(sem["cw_land"], 16)
                for s in range(2 - l):
                    vector(gate_row(l, 1, s))
                    if l:
                        vector(row(V_OUT))
                    phase()


def _units(w):
    m = w.shape[1] // 512
    return w.reshape(2, 4, P, m, 512).transpose(3, 0, 2, 1, 4).reshape(2 * m, P, UNIT)


def _units_down(w):
    return w.reshape(FT // 2, 2, P, D).transpose(0, 2, 1, 3).reshape(FT // 2, P, UNIT)


def _paired(w):
    return w.reshape(D, 2, FT // 2, 256).transpose(0, 2, 1, 3).reshape(D, 2 * F)


def _by_feature(v):
    return v.reshape(-1, P).T


def _stream(i):
    parts = []
    for l in range(2):
        w = i["w_in_first"] if l == 0 else i["w_in_rest"][0]
        pb = np.zeros((D, 7 * 512), np.float32)
        pb[:, :SHIFT[l] - 3 * D] = w[:, 7 * D:]
        pb[:, 512:] = w[:, 4 * D:7 * D]
        parts += [_units(_paired(i["ffn1_w_gu"][l])), _units_down(i["ffn1_w_down"][l]), _units(pb),
                  _units(w[:, 0:D]), _units(w[:, 3 * D:4 * D]), _units(w[:, D:2 * D]), _units(w[:, 2 * D:3 * D]),
                  _units(i["w_proj_b"][l]), _units(i["w_proj_a"][l]), _units(i["w_out"][l]),
                  _units(_paired(i["ffn2_w_gu"][l])), _units_down(i["ffn2_w_down"][l])]
    parts += [_units(i["ada_w_2"][0]), _units(i["ada_w_2"][1])]
    qkv, up, down = i["a_wqkv_2"][0], _units(_paired(i["ffn_up_2"][0])), _units_down(i["ffn_down_2"][0])
    q, k, v = qkv[:, :D], qkv[:, D:2 * D], qkv[:, 2 * D:]
    parts += [_units(z) for z in (q, v, k, v, q, k)]
    parts += [_units(i["a_wo_2"][0]), _units(i["a_wo_2"][0]), up, down, up, down]
    qkv = i["b_wqkv_2"][0]
    q, k, v = qkv[:, :D], qkv[:, D:2 * D], qkv[:, 2 * D:]
    parts += [_units(z) for z in (q, v, k, v, k)]
    parts += [_units(i["b_wo_2"][0]),
              _units(_paired(i["ffn_up_2"][1])), _units_down(i["ffn_down_2"][1])]
    out = np.concatenate(parts)
    assert out.shape == (NUNITS, P, UNIT)
    return out


def kernel(**inputs):
    import concourse.bacc as bacc
    from concourse.bass_utils import run_bass_kernel_spmd

    i = {k: np.asarray(v) for k, v in inputs.items()}
    vecs = np.zeros((NVEC, D), np.float32)
    cols = np.zeros((P, NCOL), np.float32)
    for l in range(2):
        for n, name in enumerate(("rwkv_w0", "rwkv_a0", "rwkv_k_k", "rwkv_k_a", "rwkv_r_k", "rwkv_gn_g", "rwkv_gn_b",
                                  "sgu_ln_g", "sgu_ln_b")):
            vecs[10 * l + n] = i[name][l].reshape(-1)
        for at, name in ((G_FFN1, "ffn1_norm"), (G_MIX, "mix_norm"), (G_FFN2, "ffn2_norm"), (G_NMIX, "norm_mix_2"),
                         (G_NFFN, "norm_ffn_2")):
            cols[:, at + 8 * l:at + 8 * l + 8] = _by_feature(i[name][l])
        cols[:, G_BS + 8 * l:G_BS + 8 * l + 8] = i["sgu_b_s"][l].T
    vecs[V_V0] = i["rwkv_v0"][0]
    vecs[V_FINAL], vecs[V_OUT] = i["final_norm"], i["norm_out_2"]
    vecs[V_ADA:] = i["ada_b_2"].reshape(12, D)
    mus = np.zeros((2, SHIFT[1]), np.float32)
    mus[0, :SHIFT[0]], mus[1] = i["mu_first"], i["mu_rest"][0]
    col = np.arange(64)
    near = np.clip(col[None, :] - col[:, None], -15, 15) + 15
    arrays = {
        "wstream": _stream(i), "vecs": vecs, "cols": cols, "consts": constants(),
        "x_in": i["x"], "ctx_in": i["ctx_2"], "mus": mus,
        "lora_wa": np.concatenate([i["rwkv_w2"], i["rwkv_a2"]], axis=1), "lora_v": np.pad(i["rwkv_v2"][0], ((0, P - MV), (0, 0))),
        "wst": i["sgu_w_s"].transpose(0, 3, 1, 2),
        "convw": np.stack([np.stack([_by_feature(i["ffn_conv_2"][l, t]) for t in range(3)]
                                    + [_by_feature(i["ffn_conv_b_2"][l])], axis=1) for l in range(2)]),
        "cc": np.stack([i["c_2"][0], i["c_ctx_2"]]).reshape(2, KT, P).transpose(2, 1, 0).reshape(P, 2 * KT),
        "lam": i["a_lambda_2"], "subln": i["a_subln_2"],
        "toe": i["b_rpb_2"][0][:, 4:11][:, :, near].reshape(HEADS // 2, 2, 7, 64, 64).transpose(0, 3, 1, 2, 4), "rope": rope_constants(),
        "window": window_constants(),
    }
    nc = bacc.Bacc("TRN2", target_bir_lowering=False, num_devices=1)
    args = {}
    for name, a in arrays.items():
        arrays[name] = a = np.ascontiguousarray(a)
        args[name] = nc.dram_tensor(name, a.shape, mybir.dt.from_np(a.dtype), kind="ExternalInput").ap()
    args["lam"] = args["lam"].broadcast_to([P, 4, HD])
    args["subln"] = args["subln"].broadcast_to([P, P])
    args["out"] = nc.dram_tensor("out", (1, T, D), F32, kind="ExternalOutput").ap()
    args["mod_scr"] = nc.dram_tensor("mod_scr", (2, 2, 2, D), F32, kind="Internal").ap()
    args["vfirst_scr"] = nc.dram_tensor("vfirst_scr", (P, NT, D), F32, kind="Internal").ap()
    build(nc, **args)
    got = run_bass_kernel_spmd(nc, [arrays], core_ids=[0])
    return got.results[0]["out"]
```
